# Optimizing a Trainium2 kernel written in Bass

```python
import jax, jax.numpy as jnp
from jax import lax
import numpy as np
import math
import jax
import jax.numpy as jnp

D_MODEL = 1024
BATCH = 1
SEQ = 256
DEPTH = 1

CHUNK = 64
Q_BLOCK = 128
HEAD_DIM = 64
N_HEADS_SB = 8
N_HEADS_FOX = 8
D_SB = N_HEADS_SB * HEAD_DIM
D_FOX = N_HEADS_FOX * HEAD_DIM
N_BRANCH = 2
IN_SIZES = (D_SB, D_SB, D_SB, D_SB,
            D_FOX, D_FOX, D_FOX, D_FOX,
            N_HEADS_FOX,
            N_BRANCH * D_MODEL)
D_IN = sum(IN_SIZES)
EPS = 1e-6
NEG_BIG = -1e30


def _rmsnorm(x, g):
    xf = x.astype(jnp.float32)
    inv = lax.rsqrt(jnp.mean(xf * xf, axis=-1, keepdims=True) + EPS)
    return (xf * inv).astype(x.dtype) * g

def _to_heads(t, n_heads):
    b, s, _ = t.shape
    return t.reshape(b, s, n_heads, HEAD_DIM).transpose(0, 2, 1, 3)

def _from_heads(t):
    b, h, s, d = t.shape
    return t.transpose(0, 2, 1, 3).reshape(b, s, h * d)

def _stick_breaking(q, k, v):
    s_len = q.shape[2]
    scale = HEAD_DIM ** -0.5
    outs = []
    for start in range(0, s_len, Q_BLOCK):
        end = start + Q_BLOCK
        qb, kb, vb = q[:, :, start:end], k[:, :, :end], v[:, :, :end]
        z = jnp.einsum('bhtd,bhsd->bhts', qb, kb).astype(jnp.float32) * scale
        t_idx = start + jnp.arange(Q_BLOCK)[:, None]
        s_idx = jnp.arange(end)[None, :]
        mask = s_idx < t_idx
        log_1m = jnp.where(mask, jax.nn.log_sigmoid(-z), 0.0)
        after = lax.cumsum(log_1m, axis=3, reverse=True) - log_1m
        w = jnp.where(mask, jnp.exp(jax.nn.log_sigmoid(z) + after), 0.0)
        outs.append(jnp.einsum('bhts,bhsd->bhtd', w.astype(vb.dtype), vb))
    return jnp.concatenate(outs, axis=2)

def _forgetting_attention(q, k, v, cum_log_f):
    s_len = q.shape[2]
    scale = HEAD_DIM ** -0.5
    outs = []
    for start in range(0, s_len, Q_BLOCK):
        end = start + Q_BLOCK
        qb, kb, vb = q[:, :, start:end], k[:, :, :end], v[:, :, :end]
        z = jnp.einsum('bhtd,bhsd->bhts', qb, kb).astype(jnp.float32) * scale
        z = z + cum_log_f[:, :, start:end, None] - cum_log_f[:, :, None, :end]
        t_idx = start + jnp.arange(Q_BLOCK)[:, None]
        s_idx = jnp.arange(end)[None, :]
        z = jnp.where(s_idx <= t_idx, z, NEG_BIG)
        p = jax.nn.softmax(z, axis=-1)
        outs.append(jnp.einsum('bhts,bhsd->bhtd', p.astype(vb.dtype), vb))
    return jnp.concatenate(outs, axis=2)

def first_inputs(seed: int = 0) -> dict:
    key = jax.random.key(seed)
    ks = jax.random.split(key, 12)
    f32 = jnp.float32
    d = D_MODEL
    x = jax.random.normal(ks[0], (BATCH, SEQ, d), f32)
    c = jax.random.normal(ks[1], (BATCH, d), f32)
    w_ada = jax.random.normal(ks[2], (DEPTH, d, 3 * d), f32) * (0.5 * d ** -0.5)
    b_ada = 0.02 * jax.random.normal(ks[3], (DEPTH, 3 * d), f32)
    norm_g = 1.0 + 0.02 * jax.random.normal(ks[4], (DEPTH, d), f32)
    w_in = jax.random.normal(ks[5], (DEPTH, d, D_IN), f32) * d ** -0.5
    b_forget = jax.random.uniform(ks[6], (DEPTH, N_HEADS_FOX), f32, 1.0, 4.0)
    w_o_sb = jax.random.normal(ks[7], (DEPTH, D_SB, d), f32) * D_SB ** -0.5
    w_o_fox = jax.random.normal(ks[8], (DEPTH, D_FOX, d), f32) * D_FOX ** -0.5
    b_gate = 0.02 * jax.random.normal(ks[9], (DEPTH, N_BRANCH * d), f32)
    w_out = jax.random.normal(ks[10], (DEPTH, d, d), f32) * d ** -0.5
    final_g = 1.0 + 0.02 * jax.random.normal(ks[11], (d,), f32)
    return {"x": x, "c": c, "w_ada": w_ada, "b_ada": b_ada, "norm_g": norm_g,
            "w_in": w_in, "b_forget": b_forget, "w_o_sb": w_o_sb, "w_o_fox": w_o_fox,
            "b_gate": b_gate, "w_out": w_out, "final_g": final_g}

def first_block(x, c, w_ada, b_ada, norm_g, w_in, b_forget, w_o_sb, w_o_fox, b_gate, w_out, final_g):
    b, s, d = x.shape
    split_points = list(np.cumsum(IN_SIZES)[:-1])
    for l in range(DEPTH):
        mod = c @ w_ada[l] + b_ada[l]
        shift, scale, gate = jnp.split(mod, 3, axis=-1)
        h = _rmsnorm(x, norm_g[l]) * (1.0 + scale[:, None, :]) + shift[:, None, :]

        proj = h @ w_in[l]
        (q_a, k_a, v_a, z_a, q_b, k_b, v_b, z_b,
         f_logit, g_logit) = jnp.split(proj, split_points, axis=-1)

        y_a = _from_heads(_stick_breaking(_to_heads(q_a, N_HEADS_SB), _to_heads(k_a, N_HEADS_SB),
                                          _to_heads(v_a, N_HEADS_SB)))
        y_a = (y_a * jax.nn.silu(z_a)) @ w_o_sb[l]

        log_f = jax.nn.log_sigmoid((f_logit + b_forget[l]).astype(jnp.float32))
        cum_log_f = jnp.cumsum(log_f, axis=1).transpose(0, 2, 1)
        y_b = _from_heads(_forgetting_attention(_to_heads(q_b, N_HEADS_FOX), _to_heads(k_b, N_HEADS_FOX),
                                                _to_heads(v_b, N_HEADS_FOX), cum_log_f))
        y_b = (y_b * jax.nn.silu(z_b)) @ w_o_fox[l]

        gates = jax.nn.sigmoid(g_logit + b_gate[l]).reshape(b, s, N_BRANCH, d)
        merged = gates[:, :, 0, :] * y_a + gates[:, :, 1, :] * y_b
        x = x + gate[:, None, :] * (merged @ w_out[l])
    return _rmsnorm(x, final_g)


D_MIX = D_MODEL
D_ATTN = D_MIX // 2
D_CONV = D_MIX - D_ATTN
N_HEADS = D_ATTN // HEAD_DIM
N_KV = 2
HPG = N_HEADS // N_KV
KV_DIM = N_KV * HEAD_DIM
N_MIX_GROUPS = D_MIX // HEAD_DIM
CONV_WIDTH = 3
CMP_LEN = 32
CMP_STRIDE = 16
CMP_HIDDEN = 256
SLC_LEN = 64
N_SELECT = 16
WINDOW = 512
N_BUCKETS = 32
MAX_DISTANCE = 128
N_GROUPS = 8
EXPERTS_PER_GROUP = 8
N_EXPERTS = N_GROUPS * EXPERTS_PER_GROUP
TOP_K = 2
D_EXPERT = D_MODEL // 2
MOE_BLOCK = 128
FORCED_SCORE = 1e4
N_IN = D_ATTN + 6 * KV_DIM + 3 * N_HEADS + 3 * D_CONV


def rms_norm(x, w):
    xf = x.astype(jnp.float32)
    y = xf * lax.rsqrt(jnp.mean(xf * xf, axis=-1, keepdims=True) + EPS)
    return (y * w.astype(jnp.float32)).astype(x.dtype)

def t5_bucket(dist):
    n = jnp.maximum(dist, 0)
    max_exact = N_BUCKETS // 2
    nf = jnp.maximum(n, 1).astype(jnp.float32)
    large = max_exact + (jnp.log(nf / max_exact) / math.log(MAX_DISTANCE / max_exact)
                         * (N_BUCKETS - max_exact)).astype(jnp.int32)
    large = jnp.minimum(large, N_BUCKETS - 1)
    return jnp.where(n < max_exact, n, large)

def masked_softmax(logits, mask):
    lf = jnp.where(mask, logits.astype(jnp.float32), -jnp.inf)
    m = jnp.max(lf, axis=-1, keepdims=True)
    m = jnp.where(jnp.isfinite(m), m, 0.0)
    e = jnp.where(mask, jnp.exp(lf - m), 0.0)
    return e / jnp.maximum(jnp.sum(e, axis=-1, keepdims=True), 1e-30)

def compress(kv, pos_emb, w1, w2):
    b, s, g, dh = kv.shape
    nc = (s - CMP_LEN) // CMP_STRIDE + 1
    idx = jnp.arange(nc)[:, None] * CMP_STRIDE + jnp.arange(CMP_LEN)[None, :]
    blocks = kv[:, idx] + pos_emb[None, None, :, None, :]
    blocks = jnp.moveaxis(blocks, 3, 2).reshape(b, nc, g, CMP_LEN * dh)
    return jax.nn.silu(blocks @ w1) @ w2

def nsa_attention(q, gates, k_cmp, v_cmp, k_slc, v_slc, k_win, v_win, rel_bias):
    b, s = q.shape[0], q.shape[1]
    nc = k_cmp.shape[1]
    ns = s // SLC_LEN
    n_sel = min(N_SELECT, ns)
    nqb = s // Q_BLOCK
    scale = HEAD_DIM ** -0.5
    bias_gh = rel_bias.T.reshape(N_KV, HPG, N_BUCKETS)

    c_start = jnp.arange(nc) * CMP_STRIDE
    c_end = c_start + CMP_LEN - 1
    s_start = jnp.arange(ns) * SLC_LEN
    overlap = ((c_start[:, None] <= s_start[None, :] + SLC_LEN - 1)
               & (c_end[:, None] >= s_start[None, :])).astype(jnp.float32)

    ks_blocks = k_slc.reshape(b, ns, SLC_LEN, N_KV, HEAD_DIM).transpose(0, 3, 1, 2, 4)
    vs_blocks = v_slc.reshape(b, ns, SLC_LEN, N_KV, HEAD_DIM).transpose(0, 3, 1, 2, 4)
    pad = ((0, 0), (WINDOW, 0), (0, 0), (0, 0))
    kw_pad = jnp.pad(k_win, pad)
    vw_pad = jnp.pad(v_win, pad)

    q_all = q.reshape(b, nqb, Q_BLOCK, N_KV, HPG, HEAD_DIM).swapaxes(0, 1)
    g_all = gates.reshape(b, nqb, Q_BLOCK, N_KV, HPG, 3).swapaxes(0, 1)
    b_ix = jnp.arange(b)[:, None, None, None]
    g_ix = jnp.arange(N_KV)[None, :, None, None]
    g_ix5 = jnp.arange(N_KV)[None, :, None, None, None]
    h_ix5 = jnp.arange(HPG)[None, None, :, None, None]
    blk = jnp.arange(ns)

    def block_fn(args):
        j, qb, gb = args
        s0 = j * Q_BLOCK
        pos = s0 + jnp.arange(Q_BLOCK)

        dist_c = pos[:, None] - c_end[None, :]
        lc = jnp.einsum('bqghd,bngd->bghqn', qb, k_cmp) * scale + bias_gh[:, :, t5_bucket(dist_c)]
        p_cmp = masked_softmax(lc, dist_c >= 0)
        o_cmp = jnp.einsum('bghqn,bngd->bqghd', p_cmp.astype(v_cmp.dtype), v_cmp)

        imp = jnp.einsum('bghqn,ns->bgqs', p_cmp, overlap)
        cur = pos // SLC_LEN
        valid = blk[None, :] <= cur[:, None]
        forced = (blk[None, :] == 0) | (blk[None, :] == cur[:, None]) | (blk[None, :] == cur[:, None] - 1)
        score = jnp.where(forced, FORCED_SCORE, jnp.where(valid, imp, -1.0))
        top_val, top_idx = lax.top_k(score, n_sel)
        sel_ok = top_val >= 0.0
        ks = ks_blocks[b_ix, g_ix, top_idx].reshape(b, N_KV, Q_BLOCK, n_sel * SLC_LEN, HEAD_DIM)
        vs = vs_blocks[b_ix, g_ix, top_idx].reshape(b, N_KV, Q_BLOCK, n_sel * SLC_LEN, HEAD_DIM)
        kpos = (top_idx[..., None] * SLC_LEN + jnp.arange(SLC_LEN)).reshape(b, N_KV, Q_BLOCK, -1)
        dist_s = pos[None, None, :, None] - kpos
        mask_s = jnp.repeat(sel_ok, SLC_LEN, axis=-1) & (dist_s >= 0)
        ls = (jnp.einsum('bqghd,bgqkd->bghqk', qb, ks) * scale
              + bias_gh[g_ix5, h_ix5, t5_bucket(dist_s)[:, :, None]])
        p_s = masked_softmax(ls, mask_s[:, :, None])
        o_slc = jnp.einsum('bghqk,bgqkd->bqghd', p_s.astype(vs.dtype), vs)

        kw = lax.dynamic_slice_in_dim(kw_pad, s0, WINDOW + Q_BLOCK, axis=1)
        vw = lax.dynamic_slice_in_dim(vw_pad, s0, WINDOW + Q_BLOCK, axis=1)
        kpos_w = s0 - WINDOW + jnp.arange(WINDOW + Q_BLOCK)
        dist_w = pos[:, None] - kpos_w[None, :]
        mask_w = (dist_w >= 0) & (dist_w < WINDOW) & (kpos_w[None, :] >= 0)
        lw = jnp.einsum('bqghd,bkgd->bghqk', qb, kw) * scale + bias_gh[:, :, t5_bucket(dist_w)]
        p_w = masked_softmax(lw, mask_w)
        o_win = jnp.einsum('bghqk,bkgd->bqghd', p_w.astype(vw.dtype), vw)

        out = gb[..., 0:1] * o_cmp + gb[..., 1:2] * o_slc + gb[..., 2:3] * o_win
        return out.reshape(b, Q_BLOCK, D_ATTN)

    outs = lax.map(block_fn, (jnp.arange(nqb), q_all, g_all))
    return outs.swapaxes(0, 1).reshape(b, s, D_ATTN)

def short_conv(u, w):
    return lax.conv_general_dilated(u, w[:, None, :], window_strides=(1,),
                                    padding=[(CONV_WIDTH - 1, 0)],
                                    dimension_numbers=('NWC', 'WIO', 'NWC'),
                                    feature_group_count=u.shape[-1])

def hier_moe(h, w_group, b_group, w_expert, b_expert, w1, w3, w2):
    b, s, d = h.shape
    t = b * s
    xt = h.reshape(t, d)
    g_prob = jax.nn.softmax((xt @ w_group + b_group).astype(jnp.float32), axis=-1)
    g_top_p, g_top = lax.top_k(g_prob, 1)
    e_logits = (xt @ w_expert + b_expert).astype(jnp.float32).reshape(t, N_GROUPS, EXPERTS_PER_GROUP)
    e_in = jnp.take_along_axis(e_logits, g_top[:, :, None], axis=1)[:, 0]
    e_top_p, e_top = lax.top_k(jax.nn.softmax(e_in, axis=-1), TOP_K)
    e_top_p = e_top_p / jnp.sum(e_top_p, axis=-1, keepdims=True)
    weights = (g_top_p * e_top_p).reshape(-1)
    expert_ids = (g_top * EXPERTS_PER_GROUP + e_top).reshape(-1)
    token_ids = jnp.repeat(jnp.arange(t), TOP_K)

    a = t * TOP_K
    order = jnp.argsort(expert_ids)
    e_sorted = expert_ids[order]
    tok_sorted = token_ids[order]
    w_sorted = weights[order]
    counts = jax.ops.segment_sum(jnp.ones((a,), jnp.int32), expert_ids, num_segments=N_EXPERTS)
    padded = (counts + MOE_BLOCK - 1) // MOE_BLOCK * MOE_BLOCK
    start = jnp.cumsum(counts) - counts
    pad_end = jnp.cumsum(padded)
    pad_start = pad_end - padded
    dest = pad_start[e_sorted] + (jnp.arange(a) - start[e_sorted])
    n_blocks = (a + N_EXPERTS * (MOE_BLOCK - 1)) // MOE_BLOCK + 1
    rows = n_blocks * MOE_BLOCK
    x_disp = jnp.zeros((rows, d), xt.dtype).at[dest].set(xt[tok_sorted])
    blk_expert = jnp.minimum(jnp.searchsorted(pad_end, jnp.arange(n_blocks) * MOE_BLOCK, side='right'),
                             N_EXPERTS - 1)

    def expert_block(args):
        xb, e = args
        return (jax.nn.silu(xb @ w1[e]) * (xb @ w3[e])) @ w2[e]

    y_disp = lax.map(expert_block, (x_disp.reshape(n_blocks, MOE_BLOCK, d), blk_expert)).reshape(rows, d)
    y = jax.ops.segment_sum(y_disp[dest] * w_sorted[:, None].astype(y_disp.dtype), tok_sorted,
                            num_segments=t)
    return y.reshape(b, s, d)

def second_inputs(seed: int = 0) -> dict:
    key = jax.random.key(seed)
    ks = jax.random.split(key, 26)
    f32 = jnp.float32

    def nrm(k, shape, scale):
        return jax.random.normal(k, shape, f32) * scale

    def gain(k, shape):
        return 1.0 + 0.02 * jax.random.normal(k, shape, f32)

    L = DEPTH
    return {
        'x': nrm(ks[0], (BATCH, SEQ, D_MODEL), 1.0),
        'c': nrm(ks[1], (BATCH, D_MODEL), 1.0),
        'w_ada': nrm(ks[2], (L, D_MODEL, 6 * D_MODEL), 0.5 * D_MODEL ** -0.5),
        'b_ada': nrm(ks[3], (L, 6 * D_MODEL), 0.01),
        'norm1_w': gain(ks[4], (L, D_MODEL)),
        'w_in': nrm(ks[5], (L, D_MODEL, N_IN), D_MODEL ** -0.5),
        'q_norm_w': gain(ks[6], (L, HEAD_DIM)),
        'k_norm_w': gain(ks[7], (L, 3, HEAD_DIM)),
        'cmp_pos_k': nrm(ks[8], (L, CMP_LEN, HEAD_DIM), 0.1),
        'cmp_pos_v': nrm(ks[9], (L, CMP_LEN, HEAD_DIM), 0.1),
        'cmp_k_w1': nrm(ks[10], (L, CMP_LEN * HEAD_DIM, CMP_HIDDEN), (CMP_LEN * HEAD_DIM) ** -0.5),
        'cmp_k_w2': nrm(ks[11], (L, CMP_HIDDEN, HEAD_DIM), CMP_HIDDEN ** -0.5),
        'cmp_v_w1': nrm(ks[12], (L, CMP_LEN * HEAD_DIM, CMP_HIDDEN), (CMP_LEN * HEAD_DIM) ** -0.5),
        'cmp_v_w2': nrm(ks[13], (L, CMP_HIDDEN, HEAD_DIM), CMP_HIDDEN ** -0.5),
        'conv_w': nrm(ks[14], (L, CONV_WIDTH, D_CONV), CONV_WIDTH ** -0.5),
        'out_norm_w': gain(ks[15], (L, D_MIX)),
        'w_out': nrm(ks[16], (L, D_MIX, D_MODEL), D_MIX ** -0.5),
        'rel_bias': nrm(ks[17], (N_BUCKETS, N_HEADS), 0.5),
        'norm2_w': gain(ks[18], (L, D_MODEL)),
        'w_group': nrm(ks[19], (L, D_MODEL, N_GROUPS), D_MODEL ** -0.5),
        'b_group': nrm(ks[20], (L, N_GROUPS), 0.01),
        'w_expert': nrm(ks[21], (L, D_MODEL, N_EXPERTS), D_MODEL ** -0.5),
        'b_expert': nrm(ks[22], (L, N_EXPERTS), 0.01),
        'w1': nrm(ks[23], (L, N_EXPERTS, D_MODEL, D_EXPERT), D_MODEL ** -0.5),
        'w3': nrm(ks[24], (L, N_EXPERTS, D_MODEL, D_EXPERT), D_MODEL ** -0.5),
        'w2': nrm(ks[25], (L, N_EXPERTS, D_EXPERT, D_MODEL), D_EXPERT ** -0.5),
    }

def second_block(x, c, w_ada, b_ada, norm1_w, w_in, q_norm_w, k_norm_w, cmp_pos_k, cmp_pos_v,
              cmp_k_w1, cmp_k_w2, cmp_v_w1, cmp_v_w2, conv_w, out_norm_w, w_out, rel_bias,
              norm2_w, w_group, b_group, w_expert, b_expert, w1, w3, w2):
    b, s, _ = x.shape
    cond = jax.nn.silu(c)
    splits = [D_ATTN, D_ATTN + 6 * KV_DIM, D_ATTN + 6 * KV_DIM + 3 * N_HEADS,
              D_ATTN + 6 * KV_DIM + 3 * N_HEADS + D_CONV,
              D_ATTN + 6 * KV_DIM + 3 * N_HEADS + 2 * D_CONV]
    for l in range(DEPTH):
        mod = cond @ w_ada[l] + b_ada[l]
        sh1, sc1, g1, sh2, sc2, g2 = jnp.split(mod[:, None, :], 6, axis=-1)

        h = rms_norm(x, norm1_w[l]) * (1 + sc1) + sh1
        proj = h @ w_in[l]
        q, kvs, gate_logits, b_gate, c_gate, u = jnp.split(proj, splits, axis=-1)
        q = rms_norm(q.reshape(b, s, N_HEADS, HEAD_DIM), q_norm_w[l])
        kv = kvs.reshape(b, s, 6, N_KV, HEAD_DIM)
        k_c = rms_norm(compress(kv[:, :, 0], cmp_pos_k[l], cmp_k_w1[l], cmp_k_w2[l]), k_norm_w[l, 0])
        v_c = compress(kv[:, :, 1], cmp_pos_v[l], cmp_v_w1[l], cmp_v_w2[l])
        k_s = rms_norm(kv[:, :, 2], k_norm_w[l, 1])
        k_w = rms_norm(kv[:, :, 4], k_norm_w[l, 2])
        gates = jax.nn.sigmoid(gate_logits.reshape(b, s, N_HEADS, 3))
        o_attn = nsa_attention(q, gates, k_c, v_c, k_s, kv[:, :, 3], k_w, kv[:, :, 5], rel_bias)
        y_conv = b_gate * short_conv(c_gate * u, conv_w[l])
        mix = jnp.concatenate([o_attn, y_conv], axis=-1).reshape(b, s, N_MIX_GROUPS, HEAD_DIM)
        mix = rms_norm(mix, out_norm_w[l].reshape(N_MIX_GROUPS, HEAD_DIM)).reshape(b, s, D_MIX)
        x = x + g1 * (mix @ w_out[l])

        h2 = rms_norm(x, norm2_w[l]) * (1 + sc2) + sh2
        x = x + g2 * hier_moe(h2, w_group[l], b_group[l], w_expert[l], b_expert[l], w1[l], w3[l], w2[l])
    return x


def setup_inputs(seed=0):
    out = dict(first_inputs(seed))
    for name, value in second_inputs(seed + 1).items():
        if name != "x":
            out[name + "_2"] = value
    return out


def reference(
    x, c, w_ada, b_ada, norm_g, w_in, b_forget, w_o_sb, w_o_fox, b_gate, w_out, final_g, c_2,
    w_ada_2, b_ada_2, norm1_w_2, w_in_2, q_norm_w_2, k_norm_w_2, cmp_pos_k_2, cmp_pos_v_2,
    cmp_k_w1_2, cmp_k_w2_2, cmp_v_w1_2, cmp_v_w2_2, conv_w_2, out_norm_w_2, w_out_2, rel_bias_2,
    norm2_w_2, w_group_2, b_group_2, w_expert_2, b_expert_2, w1_2, w3_2, w2_2,
):
    x = first_block(
        x, c, w_ada, b_ada, norm_g, w_in, b_forget, w_o_sb, w_o_fox, b_gate, w_out, final_g,
    )
    return second_block(
        x, c_2, w_ada_2, b_ada_2, norm1_w_2, w_in_2, q_norm_w_2, k_norm_w_2, cmp_pos_k_2,
        cmp_pos_v_2, cmp_k_w1_2, cmp_k_w2_2, cmp_v_w1_2, cmp_v_w2_2, conv_w_2, out_norm_w_2,
        w_out_2, rel_bias_2, norm2_w_2, w_group_2, b_group_2, w_expert_2, b_expert_2, w1_2,
        w3_2, w2_2,
    )


_drawn_inputs = setup_inputs


def setup_inputs(seed=0):
    import zlib

    import numpy as np

    out = dict(_drawn_inputs(seed))
    spreads = {}
    factors = {'b_ada': 2.997,
     'norm_g': 5.418,
     'b_gate': 8.0,
     'b_ada_2': 3.965,
     'norm1_w_2': 5.784,
     'q_norm_w_2': 8.0,
     'k_norm_w_2': 8.0,
     'cmp_pos_k_2': 8.0,
     'cmp_pos_v_2': 3.098,
     'out_norm_w_2': 7.397,
     'norm2_w_2': 7.453,
     'b_group_2': 8.0,
     'b_expert_2': 8.0}
    for name, (base, spread) in spreads.items():
        noise = np.random.default_rng([zlib.crc32(name.encode()), seed]).standard_normal(out[name].shape)
        drawn = base * np.exp(spread * noise) if base else spread * noise
        out[name] = jnp.asarray(drawn.astype(out[name].dtype))
    for name, factor in factors.items():
        out[name] = (out[name] * factor).astype(out[name].dtype)
    return out
```

```python
from contextlib import ExitStack

import numpy as np

import concourse.bass as bass
from concourse import mybir

ALU = mybir.AluOpType
ACT = mybir.ActivationFunctionType
F32 = mybir.dt.float32
I32 = mybir.dt.int32
AX = mybir.AxisListType.X

P = 128
T = 256
TI = T // P
D = 1024
DC = D // P
HD = 64
H = 8
W5 = 512
EPS = 1e-6
NEG = -1e30
QSCALE = HD ** -0.5
NCMP = (T - 32) // 16 + 1
NE = 64
SLOTS = 32
ITEMS = 4
MAIN = NE // ITEMS
ROUNDS = -(-((2 * T + (SLOTS - 1) * NE) // SLOTS) // ITEMS)
BW = 400
BM = BW + P
RING = 4
MRING = 6
STAGES = 12

C_ID, C_GE, C_LE, C_LT, C_ONE, C_GT, C_IOTA, C_INV, C_S1, C_S1C, C_S2, C_S2C = [k * P for k in range(12)]
C_NM = 12 * P
C_NS = C_NM + 256
C_D64 = C_NS + P
C_D8 = C_D64 + 64
C_THR = C_D8 + 8
C_N = C_THR + 8


def constants():
    p = np.arange(P)[:, None]
    f = np.arange(P)[None, :]
    blocks = [p == f, p >= f, p <= f, p < f, p >= 0 * f, p > f, f + 0 * p, (p + f >= 0) / 32.0,
              f == p + 1, (p == 127) & (f == 0), f == p + 2, f == p - 126]
    f2 = np.arange(256)[None, :]
    blocks.append(np.where(128 + p - f2 >= 0, 0.0, NEG))
    blocks.append(np.where(p >= f, NEG, 0.0))
    blocks.append(np.tile(64.0 - np.arange(64), (P, 1)))
    blocks.append(np.tile(8.0 - np.arange(8), (P, 1)))
    blocks.append(np.tile(32.0 * np.arange(8), (P, 1)))
    return np.concatenate([np.asarray(b, np.float32) for b in blocks], 1)


def bucket_onehot():
    dist = 255 - np.arange(BM)
    n = np.maximum(dist, 0)
    nf = np.maximum(n, 1).astype(np.float32)
    large = 16 + (np.log(nf / np.float32(16)) / np.float32(np.log(8.0)) * np.float32(16)).astype(np.int32)
    b = np.where(n < 16, n, np.minimum(large, 31))
    b = np.where(dist < 0, 32, b)
    return (np.arange(33)[:, None] == b[None, :]).astype(np.float32)


def build(nc, t, out):
    with ExitStack() as ctx:
        def sb(name, cols, dt=F32, parts=P):
            return ctx.enter_context(nc.sbuf_tensor(name, [parts, cols], dt))

        def sem(name):
            return ctx.enter_context(nc.semaphore(name))

        ps = ctx.enter_context(nc.psum_tensor("ps", [P, 8, W5], F32))
        bias_dram = nc.dram_tensor("bias_dram", [P, H, BM], F32).ap()

        ring = sb("ring", RING * 4096)
        arena = sb("arena", 16384)
        cst = sb("cst", C_N)
        x = sb("x_sb", TI * D)
        hT = sb("hT", DC * T)
        hoT = sb("hoT", BM, parts=33)
        xn = sb("xn", TI * D)
        modt = sb("modt", W5)
        grow = sb("grow", 3 * D)
        zS = sb("zS", 2 * 384)
        Pb = sb("Pb", 2 * 384)
        PT = sb("PT", 2 * 384)
        R = sb("R", 384)
        U = sb("U", 2 * 384)
        rowsA = sb("rowsA", P)
        rowsB = sb("rowsB", P)
        colA = sb("colA", 40)
        colB = sb("colB", 128)
        c32 = sb("c32", 2 * DC * 32)
        mod2c = sb("mod2c", 64)
        ab = sb("ab", 6 * DC)
        stat = sb("stat", 256)
        wf = sb("wf", DC * 8)
        fl = sb("fl", 6 * 16)
        bfr = sb("bfr", 8)
        wr = sb("wr", DC * 72)
        br = sb("br", 72)
        w2c = sb("w2c", 2 * 2 * HD)
        rbx = sb("rbx", 8)
        rt = sb("rt", 64)
        ids = sb("ids", 96, I32)

        def cc(o, n=P, parts=P):
            return cst[0:parts, o:o + n]

        IDN = cc(C_ID)

        def ar(o, n):
            return arena[:, o:o + n]
        qT = [ar(0, 1024), ar(2048, 1024)]
        kT = [ar(1024, 1024), ar(3072, 1024)]
        vv = [ar(4096, 1024), ar(5120, 1024)]
        sz = [ar(6144, 1024), ar(7168, 1024)]
        gates = ar(8192, 4096)
        bg = ar(12288, 2048)
        fg = ar(14336, 1024)
        merged = ar(4096, 2048)
        B = ar(0, H * BW).rearrange("p (h f) -> p h f", h=H)
        cw = ar(3200, 1536)
        QK = ar(4736, 1536)
        qkT = ar(6272, 1536)
        kvd = ar(7808, 1024)
        vS = ar(8832, 512)
        X = ar(9344, 1024)
        Hh = ar(10368, 512)
        HE = ar(10880, 512)
        HTk = ar(11392, 64)
        HTv = ar(11456, 512)
        kc = ar(11968, 128)
        kcT = ar(12096, 16)
        Vbd = ar(12112, 512)
        Pc = ar(12624, 512)
        PcT = ar(13136, 512)
        bgt = ar(13648, 1024)
        cu = ar(14672, 1024)
        bR = arena[0:8, 15360:15360 + BM]
        Sc = ar(15696, 256)
        G3 = ar(15952, 48)
        cw0 = ar(4736, 1024)
        cw1 = ar(7808, 1024)
        cw2 = ar(9344, 1024)
        sq = hT
        xe = ar(0, 1024)
        acc = ar(1024, 2048)
        hE = ar(3072, 512)
        hA = ar(3584, 512)
        actT = ar(4096, 512)
        ye = ar(4608, 1024)
        sel = ar(5632, 256)
        wsel = ar(5888, 256)
        wc = ar(6144, 256)
        rL = ar(6400, 144)
        rE = ar(6544, 128)
        rO1 = ar(6672, 128)
        rO2 = ar(6800, 128)
        rA = ar(6928, 128)
        rP = ar(7056, 128)
        rG = ar(7184, 64)
        rQ = ar(7248, 64)
        nb128 = ar(7312, 128)
        cmpi = ar(7440, 80)
        rT = ar(7520, 128)

        def ringv(n):
            s = n % RING
            return ring[:, s * 4096:(s + 1) * 4096]

        def mringv(s):
            return ring[:, s * 4096:(s + 1) * 4096] if s < RING else \
                arena[:, 8192 + (s - RING) * 4096:8192 + (s - RING + 1) * 4096]

        ring_in = [sem(f"ring_in{s}") for s in range(RING)]
        mring_in = [sem(f"mring_in{s}") for s in range(MRING)]
        mring_free = sem("mring_free")
        (ld_cst, ld_x, ld_rowsA, ld_rowsB, ld_rows1, ld_small, ld_grow, ld_bias, st_bias, ld_cw, st_out) = [
            sem(n) for n in ("ld_cst", "ld_x", "ld_rowsA", "ld_rowsB", "ld_rows1", "ld_small", "ld_grow",
                             "ld_bias", "st_bias", "ld_cw", "st_out")]
        (ms_done, v_done, r0_done, xn_done, xt_done, ht_done, ab_done, mod_raw, cols_tr, c1_ok, colB_ok,
         c2_e, c2_ok, ab_ok, ab2_ok) = [
            sem(n) for n in ("ms_done", "v_done", "r0_done", "xn_done", "xt_done", "ht_done", "ab_done",
                             "mod_raw", "cols_tr", "c1_ok", "colB_ok", "c2_e", "c2_ok", "ab_ok", "ab2_ok")]
        unit_done = [sem("unit_done0"), sem("unit_done1")]
        unit_free = [sem("unit_free0"), sem("unit_free1")]
        (misc_done, misc_free, mod_ok, tr_done, tr_free, e_sig) = [
            sem(n) for n in ("misc_done", "misc_free", "mod_ok", "tr_done", "tr_free", "e_sig")]
        (st_z, st_zc, st_ln, st_L, st_Lm, st_c, st_w, st_pv) = [
            sem(n) for n in ("st_z", "st_zc", "st_ln", "st_L", "st_Lm", "st_c", "st_w", "st_pv")]
        (fx_u, fx_z, fx_m, fx_p, fx_sc, fx_pv) = [
            sem(n) for n in ("fx_u", "fx_z", "fx_m", "fx_p", "fx_sc", "fx_pv")]
        names = ("f_e f_l f_lf ya_ok mg_ok x_ok sq_ok qk_ok cp_T cp_X cp_h cp_e cp_H cp_w2 cp_v cp_k cp_z cp_s "
                 "cp_x cp_p cp_n cv_w cv_w2 rb_ok pad_ok att_ok ld_bg").split()
        (f_e, f_l, f_lf, ya_ok, mg_ok, x_ok, sq_ok, qk_ok, cp_T, cp_X, cp_h, cp_e, cp_H, cp_w2, cp_v, cp_k, cp_z,
         cp_s, cp_x, cp_p, cp_n, cv_w, cv_w2, rb_ok, pad_ok, att_ok, ld_bg) = [sem(n) for n in names]
        (r_lg, r_s, r_e, r_A, r_rk, r_nb, r_st, r_ci, r_it, ids_ok) = [
            sem(n) for n in ("r_lg", "r_s", "r_e", "r_A", "r_rk", "r_nb", "r_st", "r_ci", "r_it", "ids_ok")]
        (m_sel, m_d, m_xe, m_e, m_a, m_at, m_atc, m_ye, m_cb, m_cbf, m_wt, m_wc, m_ch) = [
            sem(n) for n in ("m_sel", "m_d", "m_xe", "m_e", "m_a", "m_at", "m_atc", "m_ye", "m_cb", "m_cbf",
                             "m_wt", "m_wc", "m_ch")]
        dve_ch, act_ch = sem("dve_chain"), sem("act_chain")

        def colchunk(w, c0, n=W5):
            return w[:, c0:c0 + n].rearrange("(c p) n -> p c n", p=P), (DC, n)

        w_in, w_in2 = t["w_in"][0], t["w_in_2"][0]
        ada, ada2 = t["w_ada"][0], t["w_ada_2"][0]
        chunks = [colchunk(ada, n * W5) for n in range(4)]
        PROJ0 = len(chunks)
        proj_cols = [512, 0, 1024, 1536, 2560, 2048, 3072, 3584] + [4104 + n * W5 for n in range(4)]
        for q in range(12):
            chunks += [colchunk(w_in, proj_cols[q]), colchunk(ada2, q * W5)]
        ADAG = len(chunks)
        chunks += [colchunk(ada, n * W5) for n in (4, 5)]
        WO = len(chunks)
        for w in (t["w_o_sb"][0], t["w_o_fox"][0]):
            chunks.append((w.rearrange("(c p) n -> p c n", p=P), (4, 1024)))
        WOUT = len(chunks)
        chunks += [colchunk(t["w_out"][0], n * W5) for n in range(2)]
        KV = len(chunks)
        chunks += [colchunk(w_in2, 512), colchunk(w_in2, 1024, 280), colchunk(w_in2, 0)]
        CMP = len(chunks)
        for w in (t["cmp_k_w1_2"][0], t["cmp_v_w1_2"][0]):
            chunks.append((w.rearrange("(j p) n -> p j n", p=P), (16, 256)))
        CONV = len(chunks)
        chunks += [colchunk(w_in2, 1304 + n * W5) for n in range(3)]
        WO2 = len(chunks)
        chunks += [colchunk(t["w_out_2"][0], n * W5) for n in range(2)]
        NCH = len(chunks)

        def cview(n):
            a, b = chunks[n][1]
            return ringv(n)[:, 0:a * b].rearrange("p (a b) -> p a b", a=a)

        def unit_read(u):
            return unit_done[u % 2], u // 2 + 1

        read_by = [(mod_raw, n + 1) for n in range(4)]
        for q in range(12):
            read_by += [unit_read(2 * q + 1), (misc_done, 2 + 2 * q)]
        read_by += [(misc_done, 26), (misc_done, 28), unit_read(27), unit_read(31), unit_read(33), unit_read(35),
                    unit_read(37), unit_read(39), unit_read(41), (cp_h, 1), (cp_h, 2),
                    unit_read(43), unit_read(45), unit_read(47), unit_read(51), unit_read(53)]
        assert len(read_by) == NCH

        def rows(ap, c0, n):
            return bass.AP(tensor=ap.tensor, offset=ap.offset + c0, ap=[[0, P], [1, n]])

        def Z(b):
            return ps[:, 2 + b, 0:384]

        def diag(tile):
            return bass.AP(tensor=tile.tensor, offset=tile.offset, ap=[tile.ap[0], [256, 2], [1, P]])

        v3 = [vv[b].rearrange("p (i n) -> p i n", i=TI) for b in range(2)]
        qT3 = [q.rearrange("p (m t) -> p m t", m=4) for q in qT]
        kT3 = [k.rearrange("p (m t) -> p m t", m=4) for k in kT]
        hT3 = hT[:].rearrange("p (c t) -> p c t", c=DC)
        x3 = x[:].rearrange("p (i d) -> p i d", i=TI)
        xn3 = xn[:].rearrange("p (i d) -> p i d", i=TI)
        g3 = gates.rearrange("p (i n) -> p i n", i=TI)
        mg3 = merged.rearrange("p (i n) -> p i n", i=TI)
        sz3 = [s.rearrange("p (i n) -> p i n", i=TI) for s in sz]
        yT3 = qT3
        QK4 = QK.rearrange("p (i h d) -> p i h d", i=TI, h=12)
        qkT3 = qkT.rearrange("p (m t) -> p m t", m=6)
        kvd6 = kvd.rearrange("p (i kv g a d) -> p i kv g a d", i=2, kv=2, g=2, a=2)
        vS4 = vS.rearrange("p (a i n) -> p a i n", a=2, i=2)
        X5 = X.rearrange("p (kv j g n) -> p kv j g n", kv=2, j=16, g=2)
        HTk3 = HTk.rearrange("p (c n) -> p c n", c=2)
        HTv5 = HTv.rearrange("p (c g r n) -> p c g r n", c=2, g=2, r=4)
        Vbd3 = Vbd.rearrange("p (g n) -> p g n", g=2)
        Pc4 = Pc.rearrange("p (i h n) -> p i h n", i=2, h=8)
        PcT4 = PcT.rearrange("p (i g n) -> p i g n", i=2, g=2)
        Sc4 = Sc.rearrange("p (i h n) -> p i h n", i=2, h=8)
        G34 = G3.rearrange("p (i h n) -> p i h n", i=2, h=8)
        bgt3 = bgt.rearrange("p (i n) -> p i n", i=TI)
        cu3 = cu.rearrange("p (i n) -> p i n", i=TI)
        cwp = [a.rearrange("p (i n) -> p i n", i=TI) for a in (cw0, cw1, cw2)]
        xe3 = xe.rearrange("p (c n) -> p c n", c=DC)
        acc3 = acc.rearrange("p (i n) -> p i n", i=TI)
        actT3 = actT.rearrange("p (j n) -> p j n", j=4)
        sel3 = sel.rearrange("p (i n) -> p i n", i=TI)
        wsel3 = wsel.rearrange("p (i n) -> p i n", i=TI)
        wc3 = wc.rearrange("p (i n) -> p i n", i=TI)

        def zb(buf, b):
            return buf[:, b * 384:(b + 1) * 384]

        MS, VA, LN, RS, TM, SM, MX, CO = (stat[:, k * 32:(k + 1) * 32] for k in range(8))
        NRM = [(2, P), (2, P), (2, P), (24, P), (2, 16), (32, P), (2, P)]

        block = ctx.enter_context(nc.Block())

        @block.sync
        def _(sp):
            for n in range(NCH):
                if n >= RING:
                    sp.wait_ge(*read_by[n - RING])
                sp.dma_start(cview(n), chunks[n][0]).then_inc(ring_in[n % RING], 16)
            sp.wait_ge(ids_ok, 1)

            w1, w3, w2 = t["w1_2"][0], t["w3_2"][0], t["w2_2"][0]

            def round_(it, waits):
                ex = [sp.value_load(ids[0:1, bass.ds(it * ITEMS + e, 1)], min_val=0, max_val=NE - 1)
                      for e in range(ITEMS)]
                for s in range(STAGES):
                    if waits or s >= MRING:
                        sp.wait_ge(mring_free, it * STAGES + (s - MRING + 1))
                    dst = mringv(s % MRING)
                    for e in range(ITEMS):
                        if s < 8:
                            w = (w1, w3)[s % 2]
                            src = w[bass.ds(ex[e], 1), (s // 2) * 256:(s // 2 + 1) * 256, :] \
                                .rearrange("o (r p) n -> p (o r) n", p=P)
                            d = dst[:, e * 1024:(e + 1) * 1024].rearrange("p (r n) -> p r n", r=2)
                        else:
                            src = w2[bass.ds(ex[e], 1), (s - 8) * P:(s - 7) * P, :] \
                                .rearrange("o p n -> p (o n)")
                            d = dst[:, e * 1024:(e + 1) * 1024]
                        sp.dma_start(d, src).then_inc(mring_in[s % MRING], 16)

            round_(0, False)
            with sp.Fori(1, MAIN) as it:
                round_(it, True)
            n_items = sp.value_load(ids[0:1, 80:81], min_val=0, max_val=ROUNDS * ITEMS)
            with sp.If(n_items > MAIN * ITEMS):
                with sp.Fori(MAIN, ROUNDS) as it:
                    round_(it, True)
            sp.wait_ge(x_ok, 4)
            sp.dma_start(out[0].rearrange("(i p) d -> p i d", p=P), x3).then_inc(st_out, 16)
            sp.wait_ge(st_out, 16)

        @block.tensor
        def _(pe):
            used = [0]
            units = [0]
            misc = [0]
            trs = [0]

            def chunk_in(n):
                pe.wait_ge(ring_in[n % RING], 16 * (n // RING + 1))

            def unit_bank():
                u = units[0]
                if u >= 2:
                    pe.wait_ge(unit_free[u % 2], u // 2)
                units[0] += 1
                return u % 2

            def misc_bank():
                if misc[0]:
                    pe.wait_ge(misc_free, misc[0])
                misc[0] += 1

            def tr_bank():
                if trs[0]:
                    pe.wait_ge(tr_free, trs[0])
                trs[0] += 1

            def mod_product(n, which, bank, done):
                chunk_in(n)
                for c in range(DC):
                    j = c % 4
                    cv = c32[:, (which * DC + c) * 32:(which * DC + c + 1) * 32]
                    mm = pe.matmul(ps[32 * j:32 * j + 32, bank, :], cv, cview(n)[:, c, :], start=c < 4,
                                   stop=c >= 4, skip_group_check=True)
                mm.then_inc(done, 1)

            def mod_cols(bank, done):
                for m in range(4):
                    mm = pe.matmul(ps[:, bank, m:m + 1], modt[:, m * P:(m + 1) * P], cst[:, C_INV:C_INV + 1],
                                   start=True, stop=True)
                mm.then_inc(done, 1)

            def mod_row(bank, done):
                pe.matmul(ps[:, bank, :], cc(C_INV), modt[:], start=True, stop=True).then_inc(done, 1)

            def to_features(src3, done):
                for hf in range(2):
                    for i in range(TI):
                        for c in range(4):
                            mm = pe.transpose(ps[:, 2 * hf + i, c * P:(c + 1) * P],
                                              src3[:, i, (4 * hf + c) * P:(4 * hf + c + 1) * P], IDN)
                mm.then_inc(done, 1)

            pe.wait_ge(ld_cst, 16)
            pe.wait_ge(ld_rowsA, 48)
            pe.transpose(ps[:, 7, 0:40], rowsA[0:40, :], cst[0:40, C_ID:C_ID + 40]).then_inc(cols_tr, 1)
            pe.wait_ge(ld_rowsB, 16 * 11)
            pe.transpose(ps[:, 6, 0:116], rowsB[0:116, :], cst[0:116, C_ID:C_ID + 116]).then_inc(cols_tr, 1)
            pe.wait_ge(xn_done, 1)
            to_features(xn3, xt_done)
            pe.wait_ge(c1_ok, 1)
            for n in range(4):
                mod_product(n, 0, 4, mod_raw)
                pe.wait_ge(mod_ok, n + 1)
                for m in range(4):
                    mm = pe.matmul(ps[:, 5, 4 * n + m:4 * n + m + 1], modt[:, m * P:(m + 1) * P],
                                   cst[:, C_INV:C_INV + 1], start=True, stop=True)
                mm.then_inc(ab_done, 1)

            def stationary_unit(n, half, b=None):
                b = unit_bank()
                for m2 in range(2):
                    for c in range(DC):
                        mm = pe.matmul(ps[:, b, m2 * 256:(m2 + 1) * 256],
                                       cview(n)[:, c, (2 * half + m2) * P:(2 * half + m2 + 1) * P],
                                       hT3[:, c, :], start=c == 0, stop=c == DC - 1)
                mm.then_inc(unit_done[b], 1)

            def token_unit(lhs3, i, rhs, kc_, n=W5):
                b = unit_bank()
                for c in range(kc_):
                    mm = pe.matmul(ps[:, b, 0:n], lhs3[:, c, i * P:(i + 1) * P], rhs[:, c, :],
                                   start=c == 0, stop=c == kc_ - 1)
                mm.then_inc(unit_done[b], 1)

            def f_logits():
                misc_bank()
                for i in range(TI):
                    for c in range(DC):
                        mm = pe.matmul(ps[:, 7, i * 8:(i + 1) * 8], hT3[:, c, i * P:(i + 1) * P],
                                       wf[:, c * 8:(c + 1) * 8], start=c == 0, stop=c == DC - 1)
                mm.then_inc(misc_done, 1)

            def mod2_raw(q):
                misc_bank()
                if q == 0:
                    pe.wait_ge(c2_ok, 1)
                mod_product(PROJ0 + 2 * q + 1, 1, 7, misc_done)

            def mod2_out(q):
                misc_bank()
                if q in (4, 5, 10, 11):
                    mod_row(7, misc_done)
                else:
                    mod_cols(7, misc_done)

            def stick_scores(h):
                b, m, lo = h % 2, h // 2, 64 * (h % 2)
                if h == 0:
                    pe.wait_ge(unit_free[0], 2)
                    pe.wait_ge(unit_free[1], 2)
                if h >= 2:
                    pe.wait_ge(st_w, h - 1)
                k, q = kT3[0][lo:lo + 64, m, :], qT3[0][lo:lo + 64, m, :]
                pe.matmul(ps[:, 2 + b, 0:256], k[:, 0:P], q[:, :], start=True, stop=False, skip_group_check=True)
                pe.matmul(ps[:, 2 + b, 256:384], k[:, P:T], q[:, P:T], start=False, stop=False,
                          skip_group_check=True).then_inc(st_z, 1)

            def stick_after(h):
                b = h % 2
                L = zb(PT, b)
                pe.wait_ge(st_Lm, h + 1)
                pe.matmul(ps[:, 2 + b, 0:256], cc(C_GE), L[:, 0:256], start=False, stop=False, skip_group_check=True)
                pe.matmul(ps[:, 2 + b, P:256], cc(C_ONE), L[:, 256:384], start=False, stop=False, skip_group_check=True)
                pe.matmul(ps[:, 2 + b, 256:384], cc(C_GE), L[:, 256:384], start=False, stop=False, skip_group_check=True)
                for o in (0, 256):
                    mm = pe.matmul(ps[:, 2 + b, o:o + P], IDN, cc(C_NS), start=False, stop=True, skip_group_check=True)
                mm.then_inc(st_c, 1)

            def pv(w, v0, v1, h, blocks, start0):
                pe.matmul(ps[:, 5, h * HD:(h + 1) * HD], w[:, blocks[0]:blocks[0] + P], v0, start=start0,
                          stop=False, skip_group_check=True)
                pe.matmul(ps[:, 6, h * HD:(h + 1) * HD], w[:, blocks[1]:blocks[1] + P], v0, start=start0,
                          stop=False, skip_group_check=True)
                return pe.matmul(ps[:, 6, h * HD:(h + 1) * HD], w[:, blocks[2]:blocks[2] + P], v1, start=False,
                                 stop=False, skip_group_check=True)

            def stick_pv(h):
                if h == 0:
                    pe.wait_ge(unit_free[0], 3)
                    pe.wait_ge(unit_free[1], 3)
                pe.wait_ge(st_w, h + 1)
                pv(zb(Pb, h % 2), v3[0][:, 0, h * HD:(h + 1) * HD], v3[0][:, 1, h * HD:(h + 1) * HD], h,
                   (0, 128, 256), True).then_inc(st_pv, 1)

            def y_transposes(b, i):
                tr_bank()
                pe.wait_ge(ya_ok, 2 * b + i + 1)
                for c in range(4):
                    mm = pe.transpose(ps[:, 4, c * P:(c + 1) * P], sz3[b][:, i, c * P:(c + 1) * P], IDN)
                mm.then_inc(tr_done, 1)

            def fox_scores(h):
                b, m, lo = h % 2, h // 2, 64 * (h % 2)
                if h == 0:
                    pe.wait_ge(unit_free[0], 6)
                    pe.wait_ge(unit_free[1], 6)
                    pe.wait_ge(st_w, 8)
                if h >= 2:
                    pe.wait_ge(fx_m, h - 1)
                k, q = kT3[1][lo:lo + 64, m, :], qT3[1][lo:lo + 64, m, :]
                u = zb(U, b)
                pe.wait_ge(fx_u, h + 1)
                kw = dict(skip_group_check=True)
                pe.matmul(ps[:, 2 + b, 0:P], q[:, 0:P], k[:, 0:P], start=True, stop=False, **kw)
                pe.matmul(ps[:, 2 + b, P:384], q[:, P:T], k[:, 0:T], start=False, stop=False, **kw)
                pe.matmul(ps[:, 2 + b, 0:P], u[:, 0:P], cc(C_GT), start=False, stop=False, **kw)
                pe.matmul(ps[:, 2 + b, P:256], u[:, P:256], cc(C_GT), start=False, stop=False, **kw)
                pe.matmul(ps[:, 2 + b, P:384], u[:, 256:384], cst[:, C_ONE:C_ONE + 256], start=False,
                          stop=True, **kw).then_inc(fx_z, 1)

            def p_transposes(k, b, ready):
                tr_bank()
                pe.wait_ge(ready, k + 1)
                for c in range(3):
                    mm = pe.transpose(ps[:, 4, c * P:(c + 1) * P], zb(Pb, b)[:, c * P:(c + 1) * P], IDN)
                mm.then_inc(tr_done, 1)

            def fox_pv(h, tr_index):
                if h == 0:
                    pe.wait_ge(unit_free[0], 7)
                    pe.wait_ge(unit_free[1], 7)
                    pe.wait_ge(ya_ok, 2)
                pe.wait_ge(tr_free, tr_index + 1)
                pv(zb(PT, h % 2), v3[1][:, 0, h * HD:(h + 1) * HD], v3[1][:, 1, h * HD:(h + 1) * HD], h,
                   (0, 128, 256), True).then_inc(fx_pv, 1)

            pe.wait_ge(ht_done, 2)
            fox_tr = {}
            for u in range(26):
                if u < 24:
                    q, half = u // 2, u % 2
                    n = PROJ0 + 2 * q
                    if half == 0:
                        chunk_in(n)
                    if q in (0, 1, 4, 5):
                        stationary_unit(n, half)
                    else:
                        token_unit(hT3, half, cview(n), DC)
                if u == 0:
                    pe.wait_ge(ld_small, 16 * 8)
                    f_logits()
                if u % 2 == 0 and 2 <= u <= 24:
                    mod2_out(u // 2 - 1)
                if 0 <= u - 4 < H:
                    stick_scores(u - 4)
                if 0 <= u - 5 < H:
                    stick_after(u - 5)
                if 0 <= u - 6 < H:
                    stick_pv(u - 6)
                if 0 <= u - 14 < H:
                    fox_scores(u - 14)
                if 0 <= u - 16 < H:
                    fox_pv(u - 16, fox_tr[u - 16])
                if u in (14, 15):
                    y_transposes(0, u - 14)
                if 0 <= u - 15 < H:
                    fox_tr[u - 15] = trs[0]
                    p_transposes(u - 15, (u - 15) % 2, fx_p)
                if u % 2 == 1 and u < 24:
                    mod2_raw(u // 2)

            for k, n in enumerate((ADAG, ADAG + 1)):
                misc_bank()
                mod_product(n, 0, 7, misc_done)
                misc_bank()
                mod_row(7, misc_done)
            for b in range(2):
                if b == 1:
                    y_transposes(1, 0)
                    y_transposes(1, 1)
                pe.wait_ge(tr_free, trs[0] if b else 2)
                chunk_in(WO + b)
                for i in range(TI):
                    for n in range(2):
                        token_unit(yT3[b], i, cview(WO + b)[:, :, n * W5:(n + 1) * W5], 4)
            pe.wait_ge(mg_ok, 1)
            pe.wait_ge(unit_free[0], units[0] // 2)
            pe.wait_ge(unit_free[1], units[0] // 2)
            to_features(mg3, xt_done)
            pe.wait_ge(ht_done, 4)
            for n in range(2):
                chunk_in(WOUT + n)
                for i in range(TI):
                    token_unit(hT3, i, cview(WOUT + n), DC)
            pe.wait_ge(ld_rows1, 32)
            pe.wait_ge(rb_ok, 1)
            misc_bank()
            pe.matmul(ps[0:8, 7, :], rbx[0:33, :], hoT[0:33, 0:W5], start=True, stop=True).then_inc(misc_done, 1)
            misc_bank()
            pe.matmul(ps[0:8, 7, 0:BM - W5], rbx[0:33, :], hoT[0:33, W5:BM], start=True, stop=True).then_inc(misc_done, 1)
            pe.wait_ge(xn_done, 2)
            to_features(xn3, xt_done)
            pe.wait_ge(ht_done, 6)
            for k in range(3):
                chunk_in(KV + k)
                for i in range(TI):
                    token_unit(hT3, i, cview(KV + k), DC, chunks[KV + k][1][1])
                    if k == 1 and i == 0:
                        pe.wait_ge(cp_v, 2)
                        for kv in range(2):
                            for g in range(2):
                                for i2 in range(TI):
                                    mm = pe.transpose(ps[:, 2 + kv, g * 256 + i2 * P:g * 256 + (i2 + 1) * P],
                                                      kvd6[:, i2, kv, g, :, :].rearrange("p a d -> p (a d)"), IDN)
                        mm.then_inc(cp_T, 1)
            pe.wait_ge(qk_ok, 1)
            for i in range(TI):
                tr_bank()
                for c in range(4):
                    mm = pe.transpose(ps[:, 4, c * P:(c + 1) * P],
                                      QK4[:, i, 2 * c:2 * c + 2, :].rearrange("p h d -> p (h d)"), IDN)
                mm.then_inc(tr_done, 1)
            tr_bank()
            for i in range(TI):
                for c in range(2):
                    mm = pe.transpose(ps[:, 4, (2 * i + c) * P:(2 * i + c + 1) * P],
                                      QK4[:, i, 8 + 2 * c:10 + 2 * c, :].rearrange("p h d -> p (h d)"), IDN)
            mm.then_inc(tr_done, 1)

            def attn_scores(t_, a):
                h = t_
                g, m, lo = h // 4, h % 4, 64 * (h // 4)
                v = 2 * t_ + a
                if v >= 2:
                    pe.wait_ge(fx_m, 8 + v - 1)
                q, k = qkT3[lo:lo + 64, m, :], qkT3[lo:lo + 64, 4 + a, :]
                pe.matmul(ps[:, 2 + a, 0:P], q[:, 0:P], k[:, 0:P], start=True, stop=False, skip_group_check=True)
                pe.matmul(ps[:, 2 + a, P:384], q[:, P:T], k[:, 0:T], start=False, stop=True,
                          skip_group_check=True).then_inc(fx_z, 1)

            attn_tr = {}

            def attn_pv(t_, a):
                g = t_ // 4
                pe.wait_ge(tr_free, attn_tr[2 * t_ + a] + 1)
                pv(zb(PT, a), vS4[:, a, 0, g * HD:(g + 1) * HD], vS4[:, a, 1, g * HD:(g + 1) * HD], t_,
                   (0, 128, 256), t_ == 0 and a == 0).then_inc(fx_pv, 1)

            def attn_transposes(t_, a):
                attn_tr[2 * t_ + a] = trs[0]
                p_transposes(2 * t_ + a, a, fx_sc)

            pe.wait_ge(tr_free, trs[0])
            pe.wait_ge(ya_ok, 4)
            pe.wait_ge(cp_X, 4)
            for w in range(10):
                if w < 2:
                    chunk_in(CMP + w)
                    if w == 0:
                        misc_bank()
                    for j in range(16):
                        mm = pe.matmul(ps[0:32, 7, w * 256:(w + 1) * 256],
                                       X5[:, w, j, :, :].rearrange("p g n -> p (g n)"),
                                       cview(CMP + w)[:, j, :], start=j == 0, stop=j == 15)
                    mm.then_inc(cp_h, 1)
                elif w < 8:
                    k, i = (w - 2) // 2, w % 2
                    if i == 0:
                        chunk_in(CONV + k)
                    token_unit(hT3, i, cview(CONV + k), DC)
                if w < 8:
                    attn_scores(w, 0)
                    attn_scores(w, 1)
                if 0 <= w - 2 < 8:
                    attn_pv(w - 2, 0)
                    attn_pv(w - 2, 1)
                if 0 <= w - 1 < 8:
                    attn_transposes(w - 1, 0)
                    attn_transposes(w - 1, 1)
                if w == 2:
                    pe.wait_ge(cp_H, 1)
                    tr_bank()
                    for c in range(4):
                        mm = pe.transpose(ps[:, 4, c * 32:(c + 1) * 32], Hh[0:32, c * P:(c + 1) * P],
                                          cst[0:32, C_ID:C_ID + 32])
                    mm.then_inc(tr_done, 1)
                    h_tr = trs[0]
                if w == 3:
                    pe.wait_ge(tr_free, h_tr)
                    for g in range(2):
                        for c in range(2):
                            pe.matmul(ps[0:16, 7, g * HD:(g + 1) * HD], HTk3[:, c, g * 16:(g + 1) * 16],
                                      w2c[:, c * HD:(c + 1) * HD], start=c == 0, stop=c == 1)
                    for g in range(2):
                        for c in range(2):
                            mm = pe.matmul(ps[:, 7, P + g * HD:P + (g + 1) * HD],
                                           HTv5[:, c, g, :, :].rearrange("p r n -> p (r n)"),
                                           w2c[:, (2 + c) * HD:(3 + c) * HD], start=c == 0, stop=c == 1)
                    mm.then_inc(cp_w2, 1)
                if w == 4:
                    pe.wait_ge(cp_k, 1)
                    tr_bank()
                    pe.transpose(ps[:, 4, 0:16], kc[0:16, :], cst[0:16, C_ID:C_ID + 16]).then_inc(tr_done, 1)
                    k_tr = trs[0]
                if w == 5:
                    pe.wait_ge(tr_free, k_tr)
                    for g in range(2):
                        lo = 64 * g
                        if g:
                            pe.wait_ge(cp_z, 1)
                        for i in range(TI):
                            for m in range(4):
                                o = (i * H + 4 * g + m) * 16
                                mm = pe.matmul(ps[:, 7, o:o + 16], qkT3[lo:lo + 64, m, i * P:(i + 1) * P],
                                               kcT[lo:lo + 64, :], start=True, stop=True)
                        mm.then_inc(cp_z, 1)
                if w == 7:
                    pe.wait_ge(cp_n, 1)
                    tr_bank()
                    for i in range(TI):
                        for g in range(2):
                            mm = pe.transpose(ps[:, 4, (2 * i + g) * P:(2 * i + g + 1) * P],
                                              Pc4[:, i, 4 * g:4 * g + 4, :].rearrange("p h n -> p (h n)"), IDN)
                    mm.then_inc(tr_done, 1)
                    c_tr = trs[0]
                if w == 9:
                    pe.wait_ge(tr_free, c_tr)
                    for i in range(TI):
                        for g in range(2):
                            mm = pe.matmul(ps[:, 5 + i, g * 256:(g + 1) * 256], PcT4[:, i, g, :], Vbd3[:, g, :],
                                           start=False, stop=False, skip_group_check=True)
                    mm.then_inc(cp_p, 1)
                if w == 9:
                    pe.wait_ge(cv_w, 4)
                    for i in range(TI):
                        b = unit_bank()
                        terms = [(C_S1, 1, i), (C_S2, 0, i)] + ([(C_S1C, 1, 0), (C_S2C, 0, 0)] if i else [])
                        for k, (o, wi, i2) in enumerate(terms):
                            mm = pe.matmul(ps[:, b, :], cc(o), cwp[wi][:, i2, :], start=k == 0,
                                           stop=k == len(terms) - 1)
                        mm.then_inc(unit_done[b], 1)
            pe.wait_ge(xn_done, 3)
            to_features(xn3, xt_done)
            pe.wait_ge(ht_done, 8)
            for n in range(2):
                chunk_in(WO2 + n)
                for i in range(TI):
                    token_unit(hT3, i, cview(WO2 + n), DC)
            pe.wait_ge(xn_done, 4)
            to_features(xn3, xt_done)
            pe.wait_ge(ht_done, 10)
            pe.wait_ge(ld_small, 16 * 8)
            for i in range(TI):
                for c in range(DC):
                    mm = pe.matmul(ps[:, 7, i * 72:(i + 1) * 72], hT3[:, c, i * P:(i + 1) * P],
                                   wr[:, c * 72:(c + 1) * 72], start=c == 0, stop=c == DC - 1)
            mm.then_inc(r_lg, 1)
            pe.wait_ge(r_A, 1)
            A3 = rA.rearrange("p (i e) -> p i e", i=TI)
            pe.matmul(ps[:, 7, 0:64], cc(C_LT), A3[:, 0, :], start=True, stop=True)
            pe.matmul(ps[:, 7, 64:128], cc(C_ONE), A3[:, 0, :], start=True, stop=False)
            pe.matmul(ps[:, 7, 64:128], cc(C_LT), A3[:, 1, :], start=False, stop=True)
            pe.matmul(ps[0:64, 7, 128:129], A3[:, 0, :], cst[:, C_ONE:C_ONE + 1], start=True, stop=False)
            pe.matmul(ps[0:64, 7, 128:129], A3[:, 1, :], cst[:, C_ONE:C_ONE + 1], start=False,
                      stop=True).then_inc(r_rk, 1)
            pe.wait_ge(r_nb, 1)
            pe.matmul(ps[:, 4, 192:256], nb128[0:64, :], cst[0:64, C_LT:C_LT + 64], start=True, stop=True)
            pe.matmul(ps[:, 4, 256:257], nb128[0:64, :], cst[0:64, C_ONE:C_ONE + 1], start=True, stop=True)
            pe.matmul(ps[0:64, 4, 257:258], cst[0:64, C_LE:C_LE + 64], nb128[0:64, 0:1], start=True,
                      stop=True).then_inc(r_st, 1)
            pe.wait_ge(r_ci, 1)
            pe.matmul(ps[0:1, 5, 260:340], cst[0:64, C_ONE:C_ONE + 1], cmpi[0:64, :], start=True,
                      stop=True).then_inc(r_it, 1)
            pe.wait_ge(ids_ok, 1)

            def round_(it):
                pe.wait_ge(m_sel, it + 1)
                for c in range(DC):
                    for i in range(TI):
                        mm = pe.matmul(ps[:, 4 + c // 4, (c % 4) * P:(c % 4 + 1) * P],
                                       xn3[:, i, c * P:(c + 1) * P], sel3[:, i, :], start=i == 0, stop=i == 1)
                mm.then_inc(m_d, 1)
                for i in range(TI):
                    mm = pe.transpose(ps[:, 6, i * P:(i + 1) * P], wsel3[:, i, :], IDN)
                mm.then_inc(m_wt, 1)
                pe.wait_ge(m_xe, it * 2 + 2)
                for s in range(8):
                    slot = s % MRING
                    pe.wait_ge(mring_in[slot], it * 128 + 64 * (1 + s // MRING))
                    wv = mringv(slot).rearrange("p (e r n) -> p e r n", e=4, r=2)
                    for r in range(2):
                        c = 2 * (s // 2) + r
                        for e in range(ITEMS):
                            mm = pe.matmul(ps[32 * e:32 * e + 32, s % 2, :], xe3[:, c, 32 * e:32 * e + 32],
                                           wv[:, e, r, :], start=c == 0, stop=c == DC - 1, skip_group_check=True)
                    mm.then_inc(mring_free, 1)
                pe.wait_ge(m_a, it + 1)
                pe.wait_ge(m_wc, it + 1)
                for j in range(4):
                    mm = pe.transpose(ps[:, 6, j * P:(j + 1) * P], hA[:, j * P:(j + 1) * P], IDN)
                mm.then_inc(m_at, 1)
                pe.wait_ge(m_atc, it + 1)
                for s in range(8, STAGES):
                    slot = s % MRING
                    pe.wait_ge(mring_in[slot], it * 128 + 64 * (1 + s // MRING))
                    wv = mringv(slot).rearrange("p (e n) -> p e n", e=4)
                    for n in range(2):
                        for e in range(ITEMS):
                            mm = pe.matmul(ps[32 * e:32 * e + 32, 2 + n, :], actT3[:, s - 8, 32 * e:32 * e + 32],
                                           wv[:, e, n * W5:(n + 1) * W5], start=s == 8, stop=s == STAGES - 1,
                                           skip_group_check=True)
                    mm.then_inc(mring_free, 1)
                pe.wait_ge(m_ye, it + 1)
                for k in range(4):
                    i, n = k // 2, k % 2
                    mm = pe.matmul(ps[:, (7, 6, 4, 5)[k], :], wc3[:, i, :], ye[:, n * W5:(n + 1) * W5],
                                   start=True, stop=True)
                mm.then_inc(m_cb, 1)
                pe.wait_ge(m_cbf, it + 1)

            with pe.Fori(0, MAIN) as it:
                round_(it)
            n_items = pe.value_load(ids[0:1, 80:81], min_val=0, max_val=ROUNDS * ITEMS)
            with pe.If(n_items > MAIN * ITEMS):
                with pe.Fori(MAIN, ROUNDS) as it:
                    round_(it)

        @block.scalar
        def _(act):
            n_ch = [0]

            def link(ins):
                n_ch[0] += 1
                ins.then_inc(act_ch, 1)
                act.wait_ge(act_ch, n_ch[0])

            act.dma_start(x3, t["x"][0].rearrange("(i p) d -> p i d", p=P)).then_inc(ld_x, 16)
            act.dma_start(rowsA[0:8, :], t["c"].rearrange("o (c p) -> (o c) p", p=P)).then_inc(ld_rowsA, 16)
            act.dma_start(rowsA[8:32, :], t["b_ada"].rearrange("o (c p) -> (o c) p", p=P)).then_inc(ld_rowsA, 16)
            act.dma_start(rowsA[32:40, :], t["norm_g"].rearrange("o (c p) -> (o c) p", p=P)).then_inc(ld_rowsA, 16)
            act.dma_start(cst[:], t["constants"]).then_inc(ld_cst, 16)

            norm_k = [0]

            def root():
                k = norm_k[0]
                w, parts = NRM[k]
                act.wait_ge(v_done, k + 1)
                link(act.activation(LN[0:parts, 0:w], VA[0:parts, 0:w], ACT.Ln))
                act.activation(RS[0:parts, 0:w], LN[0:parts, 0:w], ACT.Exp, scale=-0.5).then_inc(r0_done, 1)
                norm_k[0] += 1

            def mean_squares(src3, k, junk3):
                for i in range(TI):
                    act.activation(junk3[:, i, :], src3[:, i, :], ACT.Square, scale=D ** -0.5,
                                   accum_out=MS[:, i:i + 1]).then_inc(ms_done, 1)

            def to_hT(a, k):
                act.wait_ge(xt_done, k + 1)
                for c in range(4):
                    for i in range(TI):
                        if a is None:
                            ins = act.copy(hT3[:, c, i * P:(i + 1) * P], ps[:, i, c * P:(c + 1) * P])
                        elif a[1] is None:
                            ins = act.activation(hT3[:, c, i * P:(i + 1) * P], ps[:, i, c * P:(c + 1) * P], ACT.Copy,
                                                 scale=a[0][:, c:c + 1])
                        else:
                            ins = act.activation(hT3[:, c, i * P:(i + 1) * P], ps[:, i, c * P:(c + 1) * P],
                                                 ACT.Identity, scale=a[0][:, c:c + 1], bias=a[1][:, c:c + 1])
                ins.then_inc(ht_done, 1)

            act.wait_ge(ld_x, 16)
            mean_squares(x3, 0, xn3)
            root()
            act.wait_ge(colB_ok, 1)
            act.activation(colB[:, 120:128], colB[:, 0:8], ACT.Exp, scale=-1.0).then_inc(c2_e, 1)
            act.wait_ge(ab_ok, 1)
            to_hT((ab[:, 0:8], ab[:, 8:16]), 0)

            def unit_wait(u):
                act.wait_ge(unit_done[u % 2], u // 2 + 1)

            def unit_copy(u):
                q, half = u // 2, u % 2
                src = ps[:, u % 2, :]
                unit_wait(u)
                if q in (0, 4):
                    ins = act.copy(kT[q // 4][:, half * W5:(half + 1) * W5], src)
                elif q in (1, 5):
                    ins = act.mul(qT[q // 4][:, half * W5:(half + 1) * W5], src, QSCALE)
                else:
                    ins = act.copy(v3[q // 4][:, half, :], src)
                ins.then_inc(unit_free[u % 2], 1)

            def stick_soft(h):
                z = zb(zS, h % 2)
                act.wait_ge(st_zc, h + 1)
                link(act.activation(z, z, ACT.Exp))
                act.activation(z, z, ACT.Ln, bias=1.0).then_inc(st_ln, 1)

            def stick_weight(h):
                act.wait_ge(st_c, h + 1)
                if h >= 2:
                    act.wait_ge(st_pv, h - 1)
                act.activation(zb(Pb, h % 2), Z(h % 2), ACT.Exp).then_inc(st_w, 1)

            def soft_exp(k, b, pt_done):
                act.wait_ge(fx_m, k + 1)
                if pt_done is not None:
                    act.wait_ge(tr_done, pt_done)
                z, p = zb(zS, b), zb(Pb, b)
                act.activation(p[:, 0:P], z[:, 0:P], ACT.Exp, bias=MX[:, 16 + 2 * b:17 + 2 * b],
                               accum_out=SM[:, sm(k):sm(k) + 1])
                act.activation(p[:, P:384], z[:, P:384], ACT.Exp, bias=MX[:, 17 + 2 * b:18 + 2 * b],
                               accum_out=SM[:, sm(k) + 1:sm(k) + 2]).then_inc(fx_p, 1)

            def sm(k):
                return 2 * k if k < 8 else 16 + 2 * (k % 2)

            trs = [0]

            def p_copy(b, pv_need):
                act.wait_ge(tr_done, trs[0] + 1)
                if pv_need:
                    act.wait_ge(fx_pv, pv_need)
                act.copy(zb(PT, b), ps[:, 4, 0:384]).then_inc(tr_free, 1)
                trs[0] += 1

            fox_trd = {}
            for u in range(26):
                if u < 24:
                    q = u // 2
                    if q in (0, 1, 2, 4, 5, 6):
                        unit_copy(u)
                    elif q in (3, 7):
                        unit_wait(u)
                        act.activation(sz3[q // 4][:, u % 2, :], ps[:, u % 2, :], ACT.Exp, scale=-1.0).then_inc(e_sig, 1)
                    else:
                        act.wait_ge(unit_free[u % 2], u // 2 + 1)
                        gq = g3[:, u % 2, (q - 8) * W5:(q - 7) * W5]
                        act.activation(gq, gq, ACT.Exp, scale=-1.0).then_inc(e_sig, 1)
                if u == 0:
                    act.wait_ge(f_e, 1)
                    link(act.activation(fl[:, 32:48], fl[:, 32:48], ACT.Exp))
                    act.activation(fl[:, 32:48], fl[:, 32:48], ACT.Ln, bias=1.0).then_inc(f_l, 1)
                if 0 <= u - 4 < H:
                    stick_soft(u - 4)
                if 0 <= u - 5 < H:
                    stick_weight(u - 5)
                if u in (14, 15):
                    act.wait_ge(tr_done, trs[0] + 1)
                    act.copy(yT3[0][:, :, (u - 14) * P:(u - 13) * P],
                             ps[:, 4, :].rearrange("p (c t) -> p c t", c=4)).then_inc(tr_free, 1)
                    trs[0] += 1
                if 0 <= u - 14 < H:
                    k = u - 14
                    if k == 0:
                        act.wait_ge(st_pv, 8)
                    soft_exp(k, k % 2, fox_trd[k - 2] if k >= 2 else None)
                if 0 <= u - 15 < H:
                    k = u - 15
                    fox_trd[k] = trs[0] + 1
                    p_copy(k % 2, k - 1 if k >= 2 else 0)
            for i in range(TI):
                act.wait_ge(tr_done, trs[0] + 1)
                act.copy(yT3[1][:, :, i * P:(i + 1) * P],
                         ps[:, 4, :].rearrange("p (c t) -> p c t", c=4)).then_inc(tr_free, 1)
                trs[0] += 1
            to_hT(None, 1)
            act.wait_ge(x_ok, 1)
            mean_squares(x3, 1, xn3)
            root()
            act.wait_ge(x_ok, 2)
            mean_squares(x3, 2, xn3)
            root()
            to_hT((ab[:, 16:24], ab[:, 24:32]), 2)
            u0 = 36
            for k in range(3):
                for i in range(TI):
                    u = u0 + 2 * k + i
                    unit_wait(u)
                    src = ps[:, u % 2, :]
                    if k == 0:
                        s4 = src[:, 0:256].rearrange("p (kv g d) -> p kv g d", kv=2, g=2)
                        for a in range(2):
                            for kv in range(2):
                                act.copy(kvd6[:, i, kv, :, a, :], s4[:, kv, :, :])
                        act.copy(vS4[:, 0, i, :], src[:, 384:512]).then_inc(cp_v, 1)
                        act.copy(QK4[:, i, 8:10, :], src[:, 256:384].rearrange("p (h d) -> p h d", h=2)) \
                            .then_inc(unit_free[u % 2], 1)
                    elif k == 1:
                        act.copy(vS4[:, 1, i, :], src[:, 128:256])
                        act.copy(QK4[:, i, 10:12, :], src[:, 0:128].rearrange("p (h d) -> p h d", h=2))
                        act.activation(G3[:, i * 24:(i + 1) * 24], src[:, 256:280], ACT.Exp, scale=-1.0) \
                            .then_inc(unit_free[u % 2], 1)
                    else:
                        for g in range(2):
                            ins = act.copy(QK4[:, i, g:8:2, :],
                                           src[:, g * 256:(g + 1) * 256].rearrange("p (m d) -> p m d", m=4))
                        ins.then_inc(unit_free[u % 2], 1)
            act.wait_ge(unit_free[1], 21)
            act.wait_ge(unit_free[0], 21)
            for i in range(TI):
                act.activation(xn3[:, i, 0:768], QK[:, i * 768:(i + 1) * 768], ACT.Square,
                               scale=HD ** -0.5).then_inc(sq_ok, 1)
            root()
            for i in range(TI):
                act.wait_ge(tr_done, trs[0] + 1)
                act.activation(qkT3[:, 0:4, i * P:(i + 1) * P], ps[:, 4, :].rearrange("p (c t) -> p c t", c=4),
                               ACT.Copy, scale=colB[:, 117:118]).then_inc(tr_free, 1)
                trs[0] += 1
            act.wait_ge(tr_done, trs[0] + 1)
            p4 = ps[:, 4, :].rearrange("p (i c t) -> p i c t", i=2, c=2)
            for c in range(2):
                ins = act.activation(qkT3[:, 4 + c, :].rearrange("p (i t) -> p i t", i=2), p4[:, :, c, :],
                                     ACT.Copy, scale=colB[:, 114 + c:115 + c])
            ins.then_inc(tr_free, 1)
            trs[0] += 1
            attn_trd = {}
            for w in range(10):
                if 2 <= w < 8:
                    k, i = (w - 2) // 2, w % 2
                    u = u0 + 6 + w - 2
                    if k < 2:
                        unit_wait(u)
                        act.copy((bgt3, cu3)[k][:, i, :], ps[:, u % 2, :]).then_inc(unit_free[u % 2], 1)
                if 0 <= w - 1 < 8:
                    for a in range(2):
                        v = 2 * (w - 1) + a
                        attn_trd[v] = trs[0] + 1
                        p_copy(a, 8 + v - 1)
                if w < 8:
                    for a in range(2):
                        soft_exp(8 + 2 * w + a, a, attn_trd.get(2 * (w - 1) + a))
                if w == 1:
                    act.wait_ge(cp_h, 2)
                    act.activation(HE[0:32, :], ps[0:32, 7, :], ACT.Exp, scale=-1.0).then_inc(cp_e, 1)
                if w == 2:
                    act.wait_ge(tr_done, trs[0] + 1)
                    act.wait_ge(pad_ok, 4)
                    for c in range(2):
                        act.copy(HTk3[:, c, :], ps[:, 4, c * 32:(c + 1) * 32])
                        for r in range(4):
                            ins = act.copy(HTv5[:, c, :, r, 0:16],
                                           ps[:, 4, (2 + c) * 32:(3 + c) * 32].rearrange("p (g n) -> p g n", g=2))
                    ins.then_inc(tr_free, 1)
                    trs[0] += 1
                if w == 3:
                    root()
                if w == 4:
                    act.wait_ge(tr_done, trs[0] + 1)
                    act.activation(kcT, ps[:, 4, 0:16], ACT.Copy, scale=colB[:, 113:114]).then_inc(tr_free, 1)
                    trs[0] += 1
                if w == 5:
                    act.wait_ge(cp_s, 1)
                    act.activation(Pc4[:, :, :, 0:16], Sc4, ACT.Exp).then_inc(cp_x, 1)
                if w == 7:
                    act.wait_ge(tr_done, trs[0] + 1)
                    act.copy(PcT, ps[:, 4, :]).then_inc(tr_free, 1)
                    trs[0] += 1
            act.wait_ge(att_ok, 4)
            for i in range(TI):
                act.activation(hT[:, i * D:(i + 1) * D], xn3[:, i, :], ACT.Square,
                               scale=HD ** -0.5).then_inc(sq_ok, 1)
            root()
            to_hT((colB[:, 72:80], None), 3)
            act.wait_ge(x_ok, 3)
            mean_squares(x3, 3, xn3)
            root()
            to_hT((ab[:, 32:40], ab[:, 40:48]), 4)
            act.wait_ge(r_s, 1)
            act.activation(rG[:, 0:16], rG[:, 0:16], ACT.Exp).then_inc(r_e, 1)
            act.wait_ge(r_s, 2)
            act.activation(rt[:, 8:10], rt[:, 6:8], ACT.Exp).then_inc(r_e, 1)
            act.wait_ge(ids_ok, 1)

            def round_(it):
                act.wait_ge(m_d, it + 1)
                for c in range(4):
                    ins = act.activation(xe3[:, c, :], ps[:, 4, c * P:(c + 1) * P], ACT.Identity,
                                   scale=ab[:, 32 + c:33 + c], bias=ab[:, 40 + c:41 + c])
                ins.then_inc(m_xe, 1)
                act.wait_ge(mring_free, it * STAGES + 8)
                act.activation(hE, ps[:, 0, :], ACT.Exp, scale=-1.0).then_inc(m_e, 1)
                act.wait_ge(m_at, it + 1)
                act.copy(actT, ps[:, 6, :]).then_inc(m_atc, 1)
                act.wait_ge(mring_free, it * STAGES + STAGES)
                act.copy(ye, ps[:, 2:4, :].rearrange("p a b -> p (a b)")).then_inc(m_ye, 1)

            with act.Fori(0, MAIN) as it:
                round_(it)
            n_items = act.value_load(ids[0:1, 80:81], min_val=0, max_val=ROUNDS * ITEMS)
            with act.If(n_items > MAIN * ITEMS):
                with act.Fori(MAIN, ROUNDS) as it:
                    round_(it)

        @block.vector
        def _(dve):
            n_ch = [0]

            def link(ins):
                n_ch[0] += 1
                ins.then_inc(dve_ch, 1)
                dve.wait_ge(dve_ch, n_ch[0])

            def bc(ap, n):
                return bass.AP(tensor=ap.tensor, offset=ap.offset, ap=list(ap.ap) + [[0, n]])

            norm_k = [0]

            def root(scale=1.0):
                k = norm_k[0]
                w, parts = NRM[k]
                v, r, tm = VA[0:parts, 0:w], RS[0:parts, 0:w], TM[0:parts, 0:w]
                dve.tensor_scalar(v, MS[0:parts, 0:w], scale, EPS, ALU.mult, ALU.add).then_inc(v_done, 1)
                dve.wait_ge(r0_done, k + 1)
                link(dve.tensor_tensor(tm, v, r, ALU.mult))
                link(dve.tensor_tensor(tm, tm, r, ALU.mult))
                link(dve.tensor_scalar(tm, tm, -0.5, 1.5, ALU.mult, ALU.add))
                link(dve.tensor_tensor(r, r, tm, ALU.mult))
                norm_k[0] += 1

            def normalise():
                for i in range(TI):
                    ins = dve.tensor_scalar(xn3[:, i, :], x3[:, i, :], RS[:, i:i + 1], None, ALU.mult)
                ins.then_inc(xn_done, 1)

            def to_hT(a, k):
                dve.wait_ge(xt_done, k + 1)
                for c in range(4, DC):
                    src = ps[:, 2:4, (c - 4) * P:(c - 3) * P]
                    dst = hT3[:, c, :].rearrange("p (i t) -> p i t", i=TI)
                    if a is None:
                        ins = dve.tensor_copy(dst, src)
                    elif a[1] is None:
                        ins = dve.tensor_scalar(dst, src, a[0][:, c:c + 1], None, ALU.mult)
                    else:
                        ins = dve.tensor_scalar(dst, src, a[0][:, c:c + 1], a[1][:, c:c + 1], ALU.mult, ALU.add)
                ins.then_inc(ht_done, 1)

            dve.wait_ge(cols_tr, 1)
            link(dve.tensor_copy(colA[:], ps[:, 7, 0:40]))
            dve.tensor_copy(c32[:, 0:256].rearrange("p (c n) -> p c n", c=DC), bc(colA[:, 0:8], 32)).then_inc(c1_ok, 1)
            dve.wait_ge(ms_done, 2)
            root()
            normalise()
            dve.wait_ge(cols_tr, 2)
            dve.tensor_copy(colB[:, 0:116], ps[:, 6, 0:116]).then_inc(colB_ok, 1)
            dve.wait_ge(colB_ok, 1)
            dve.tensor_scalar(colB[:, 117:118], colB[:, 112:113], QSCALE, None, ALU.mult)
            dve.wait_ge(c2_e, 1)
            link(dve.tensor_scalar(colB[:, 120:128], colB[:, 120:128], 1.0, None, ALU.add))
            link(dve.reciprocal(colB[:, 120:128], colB[:, 120:128]))
            link(dve.tensor_tensor(colB[:, 120:128], colB[:, 120:128], colB[:, 0:8], ALU.mult))
            dve.tensor_copy(c32[:, 256:512].rearrange("p (c n) -> p c n", c=DC), bc(colB[:, 120:128], 32)) \
                .then_inc(c2_ok, 1)
            for n in range(4):
                dve.wait_ge(mod_raw, n + 1)
                if n:
                    dve.wait_ge(ab_done, n)
                dve.tensor_copy(modt[:], ps[:, 4, :]).then_inc(mod_ok, 1)
            dve.wait_ge(ab_done, 4)
            dve.tensor_tensor(ab[:, 8:16], ps[:, 5, 0:8], colA[:, 8:16], ALU.add)
            link(dve.tensor_tensor(ab[:, 0:8], ps[:, 5, 8:16], colA[:, 16:24], ALU.add))
            link(dve.scalar_tensor_tensor(ab[:, 0:8], ab[:, 0:8], 1.0, colA[:, 32:40], ALU.add, ALU.mult))
            dve.tensor_copy(TM[:, 0:1], ab[:, 0:1]).then_inc(ab_ok, 1)
            to_hT((ab[:, 0:8], ab[:, 8:16]), 0)

            def unit_wait(u):
                dve.wait_ge(unit_done[u % 2], u // 2 + 1)

            def sigmoid_tail(e):
                link(dve.tensor_scalar(e, e, 1.0, None, ALU.add))
                link(dve.reciprocal(e, e))

            def stick_log(h):
                b = h % 2
                dve.wait_ge(st_z, h + 1)
                if h >= 1:
                    dve.wait_ge(st_L, h)
                dve.tensor_scalar(zb(zS, b), Z(b), 40.0, None, ALU.min).then_inc(st_zc, 1)
                link(dve.tensor_scalar(R[:], Z(b), 40.0, -40.0, ALU.max, ALU.add))
                dve.wait_ge(st_ln, h + 1)
                if h >= 2:
                    dve.wait_ge(st_c, h - 1)
                dve.scalar_tensor_tensor(zb(PT, b), zb(zS, b), -1.0, R[:], ALU.mult, ALU.subtract).then_inc(st_L, 1)

            def row_max(k, b, bias0, bias1):
                dve.wait_ge(fx_z, k + 1)
                if k >= 2:
                    dve.wait_ge(fx_p, k - 1)
                z = zb(zS, b)
                dve.tensor_tensor_reduce(z[:, 0:P], ps[:, 2 + b, 0:P], bias0, 1.0, -3e38, ALU.add, ALU.max,
                                         MX[:, 2 * b:2 * b + 1])
                link(dve.tensor_tensor_reduce(z[:, P:384], ps[:, 2 + b, P:384], bias1, 1.0, -3e38, ALU.add, ALU.max,
                                              MX[:, 2 * b + 1:2 * b + 2]))
                dve.tensor_scalar(MX[:, 16 + 2 * b:18 + 2 * b], MX[:, 2 * b:2 * b + 2], -1.0, None, ALU.mult) \
                    .then_inc(fx_m, 1)

            def mod2_raw():
                dve.wait_ge(misc_done, misc[0] + 1)
                dve.tensor_copy(modt[:], ps[:, 7, :]).then_inc(misc_free, 1)
                misc[0] += 1

            def mod_row(o):
                dve.wait_ge(misc_done, misc[0] + 1)
                dve.tensor_tensor(grow[:, o:o + W5], grow[:, o:o + W5], ps[:, 7, :], ALU.add).then_inc(misc_free, 1)
                misc[0] += 1

            misc = [0]
            dve.wait_ge(ld_grow, 48)
            for u in range(26):
                q = u // 2
                if u == 0:
                    dve.wait_ge(misc_done, 1)
                    dve.wait_ge(ld_small, 16 * 8)
                    f2 = fl[:, 0:16].rearrange("p (i h) -> p i h", i=2)
                    b2 = bass.AP(tensor=bfr[:].tensor, offset=bfr[:].offset, ap=[bfr[:].ap[0], [0, 2], [1, 8]])
                    dve.tensor_tensor(f2, ps[:, 7, 0:16].rearrange("p (i h) -> p i h", i=2), b2,
                                      ALU.add).then_inc(misc_free, 1)
                    misc[0] += 1
                    dve.wait_ge(misc_free, 1)
                    link(dve.tensor_scalar(fl[:, 16:32], fl[:, 0:16], -1.0, None, ALU.mult))
                    dve.tensor_tensor(fl[:, 32:48], fl[:, 0:16], fl[:, 16:32], ALU.min).then_inc(f_e, 1)
                    dve.wait_ge(f_l, 1)
                    dve.scalar_tensor_tensor(fl[:, 48:64], fl[:, 0:16], 0.0, fl[:, 32:48], ALU.min,
                                             ALU.subtract).then_inc(f_lf, 1)
                if 16 <= u < 24:
                    unit_wait(u)
                    if u == 16:
                        dve.wait_ge(ld_bg, 32)
                    gq = g3[:, u % 2, (q - 8) * W5:(q - 7) * W5]
                    dve.tensor_tensor(gq, ps[:, u % 2, :], bg[:, (q - 8) * W5:(q - 7) * W5],
                                      ALU.add).then_inc(unit_free[u % 2], 1)
                if u % 2 == 0 and 2 <= u <= 24:
                    k = u // 2 - 1
                    if k in (4, 5):
                        mod_row(D + (k - 4) * W5)
                    elif k in (10, 11):
                        mod_row(2 * D + (k - 10) * W5)
                    else:
                        dve.wait_ge(misc_done, misc[0] + 1)
                        dve.tensor_tensor(mod2c[:, 4 * k:4 * k + 4], ps[:, 7, 0:4], colB[:, 8 + 4 * k:12 + 4 * k],
                                          ALU.add).then_inc(misc_free, 1)
                        misc[0] += 1
                if 0 <= u - 4 < H:
                    stick_log(u - 4)
                if 0 <= u - 14 < H:
                    row_max(u - 14, u % 2, cst[:, C_NM + P:C_NM + 256], cst[:, C_NM:C_NM + 256])
                if u in (6, 7, 14, 15):
                    s = sz3[q // 4][:, u % 2, :]
                    dve.wait_ge(e_sig, (u - 5) if u < 8 else (u - 11))
                    sigmoid_tail(s)
                    link(dve.tensor_tensor(s, s, ps[:, u % 2, :], ALU.mult))
                    dve.tensor_copy(TM[:, 0:1], s[:, 0:1]).then_inc(unit_free[u % 2], 1)
                if 16 <= u < 24:
                    dve.wait_ge(e_sig, u - 11)
                    sigmoid_tail(g3[:, u % 2, (q - 8) * W5:(q - 7) * W5])
                if u == 13:
                    dve.wait_ge(st_pv, 8)
                    for i in range(TI):
                        dve.tensor_tensor(sz3[0][:, i, :], sz3[0][:, i, :], ps[:, 5 + i, :], ALU.mult).then_inc(ya_ok, 1)
                if u == 23:
                    dve.wait_ge(fx_pv, 8)
                    link(dve.reciprocal(CO[:, 0:16], SM[:, 0:16]))
                    for i in range(TI):
                        s = sz3[1][:, i, :]
                        link(dve.tensor_tensor(s, s, ps[:, 5 + i, :], ALU.mult))
                        s8 = s.rearrange("p (h d) -> p h d", h=H)
                        dve.tensor_tensor(s8, s8, bc(CO[:, i:16:2], HD), ALU.mult).then_inc(ya_ok, 1)
                if u % 2 == 1 and u < 24:
                    mod2_raw()
            for o, sh, sc, g in ((16, 0, 8, 56), (32, 24, 32, 64)):
                dve.tensor_copy(ab[:, o + 8:o + 16], mod2c[:, sh:sh + 8])
                link(dve.scalar_tensor_tensor(ab[:, o:o + 8], mod2c[:, sc:sc + 8], 1.0, colB[:, g:g + 8],
                                              ALU.add, ALU.mult))
            for n in range(2):
                mod2_raw()
                mod_row(n * W5)
            tmp = zS[:, 0:W5]
            for b in range(2):
                for i in range(TI):
                    for n in range(2):
                        u = 24 + 4 * b + 2 * i + n
                        unit_wait(u)
                        g = g3[:, i, b * D + n * W5:b * D + (n + 1) * W5]
                        m = mg3[:, i, n * W5:(n + 1) * W5]
                        if b == 0:
                            dve.tensor_tensor(m, g, ps[:, u % 2, :], ALU.mult).then_inc(unit_free[u % 2], 1)
                        else:
                            dve.tensor_tensor(tmp, g, ps[:, u % 2, :], ALU.mult).then_inc(unit_free[u % 2], 1)
                            dve.wait_ge(unit_free[u % 2], u // 2 + 1)
                            ins = dve.tensor_tensor(m, m, tmp, ALU.add)
                            if i == n == 1:
                                ins.then_inc(mg_ok, 1)
                            else:
                                link(ins)
            to_hT(None, 1)

            def residual(u0, o):
                for n in range(2):
                    for i in range(TI):
                        u = u0 + 2 * n + i
                        unit_wait(u)
                        dve.tensor_tensor(tmp, grow[:, o + n * W5:o + (n + 1) * W5], ps[:, u % 2, :],
                                          ALU.mult).then_inc(unit_free[u % 2], 1)
                        dve.wait_ge(unit_free[u % 2], u // 2 + 1)
                        xs = x3[:, i, n * W5:(n + 1) * W5]
                        ins = dve.tensor_tensor(xs, xs, tmp, ALU.add)
                        if n == i == 1:
                            ins.then_inc(x_ok, 1)
                        else:
                            link(ins)

            residual(32, 0)
            dve.wait_ge(misc_done, 30)
            dve.tensor_copy(bR[:, 0:W5], ps[0:8, 7, :]).then_inc(misc_free, 1)
            dve.wait_ge(misc_done, 31)
            dve.tensor_copy(bR[:, W5:BM], ps[0:8, 7, 0:BM - W5]).then_inc(misc_free, 1)
            dve.wait_ge(ms_done, 4)
            root()
            for i in range(TI):
                ins = dve.scalar_tensor_tensor(x3[:, i, :], x3[:, i, :], RS[:, i:i + 1], fg, ALU.mult, ALU.mult)
            ins.then_inc(x_ok, 1)
            dve.wait_ge(ms_done, 6)
            root()
            normalise()
            to_hT((ab[:, 16:24], ab[:, 24:32]), 2)
            dve.wait_ge(pad_ok, 1)
            dve.wait_ge(cp_T, 1)
            for kv in range(2):
                for a in range(2):
                    lo = 64 * a
                    src = ps[lo:lo + 64, 2 + kv, :]
                    pstep = src.ap[0]
                    t_in = bass.AP(tensor=src.tensor, offset=src.offset + a, ap=[pstep, [2, 16], [256, 2], [16, NCMP]])
                    pos = colB[lo:lo + 64, 80 + 16 * kv:96 + 16 * kv]
                    p_in = bass.AP(tensor=pos.tensor, offset=pos.offset, ap=[pos.ap[0], [1, 16], [0, 2], [0, NCMP]])
                    dve.tensor_tensor(X5[lo:lo + 64, kv, :, :, 0:NCMP], t_in, p_in, ALU.add).then_inc(cp_X, 1)
            dve.wait_ge(unit_free[1], 20)
            sigmoid_tail(G3)
            dve.wait_ge(sq_ok, 2)
            link(dve.tensor_reduce(MS[:, 0:24].rearrange("p (i h) -> p i h", i=2),
                                   xn3[:, :, 0:768].rearrange("p i (h d) -> p i h d", d=HD), AX, ALU.add))
            root()
            QKf = QK.rearrange("p (h d) -> p h d", d=HD)
            dve.tensor_tensor(QKf, QKf, bc(RS[:, 0:24], HD), ALU.mult).then_inc(qk_ok, 1)
            dve.wait_ge(ld_bias, 16)
            for w in range(10):
                if w in (6, 7):
                    u, i = 40 + w, w % 2
                    unit_wait(u)
                    dve.wait_ge(unit_free[u % 2], u // 2)
                    dve.tensor_tensor(cu3[:, i, :], cu3[:, i, :], ps[:, u % 2, :], ALU.mult).then_inc(unit_free[u % 2], 1)
                if w < 8:
                    for a in range(2):
                        row_max(8 + 2 * w + a, a, B[:, w, P:256], B[:, w, 0:256])
                    for a in range(2):
                        k = 8 + 2 * w + a
                        dve.wait_ge(fx_p, k + 1)
                        c2 = CO[:, 2 * a:2 * a + 2]
                        link(dve.reciprocal(c2, SM[:, 16 + 2 * a:18 + 2 * a]))
                        link(dve.tensor_tensor(c2, c2, G34[:, :, w, 1 + a], ALU.mult))
                        p_ = zb(Pb, a)
                        dve.tensor_scalar(p_[:, 0:P], p_[:, 0:P], c2[:, 0:1], None, ALU.mult)
                        dve.tensor_scalar(p_[:, P:384], p_[:, P:384], c2[:, 1:2], None, ALU.mult).then_inc(fx_sc, 1)
                if w == 1:
                    dve.wait_ge(cp_e, 1)
                    he = HE[0:32, :]
                    sigmoid_tail(he)
                    dve.tensor_tensor(Hh[0:32, :], he, ps[0:32, 7, :], ALU.mult).then_inc(cp_H, 1)
                if w == 3:
                    dve.wait_ge(cp_w2, 1)
                    dve.wait_ge(pad_ok, 4)
                    for r in range(4):
                        dve.tensor_copy(Vbd3[32 * r:32 * r + 32, :, r * HD:(r + 1) * HD],
                                        ps[32 * r:32 * r + 32, 7, P:256].rearrange("p (g d) -> p g d", g=2))
                    link(dve.tensor_copy(kc[0:16, :], ps[0:16, 7, 0:P]))
                    link(dve.tensor_tensor(HE[0:16, 0:P], kc[0:16, :], kc[0:16, :], ALU.mult))
                    link(dve.tensor_reduce(MS[0:16, 0:2], HE[0:16, 0:P].rearrange("p (g d) -> p g d", g=2), AX, ALU.add))
                    root(1.0 / HD)
                    k3 = kc[0:16, :].rearrange("p (g d) -> p g d", g=2)
                    dve.tensor_tensor(k3, k3, bc(RS[0:16, 0:2], HD), ALU.mult).then_inc(cp_k, 1)
                if w == 5:
                    dve.wait_ge(cp_z, 2)
                    for i in range(TI):
                        f0 = 31 + P * (1 - i)
                        ins = dve.tensor_tensor(Sc4[:, i, :, :],
                                                ps[:, 7, i * P:(i + 1) * P].rearrange("p (h n) -> p h n", h=H),
                                                B[:, :, f0:f0 + 241:16], ALU.add)
                    link(ins)
                    Sf = Sc.rearrange("p (h n) -> p h n", n=16)
                    link(dve.tensor_reduce(TM[:, 0:16], Sf, AX, ALU.max))
                    link(dve.tensor_scalar(TM[:, 0:16], TM[:, 0:16], -1e20, None, ALU.max))
                    dve.tensor_tensor(Sf, Sf, bc(TM[:, 0:16], 16), ALU.subtract).then_inc(cp_s, 1)
                if w == 6:
                    dve.wait_ge(cp_x, 1)
                    c16 = TM[:, 16:32]
                    Pf = Pc.rearrange("p (h n) -> p h n", n=32)[:, :, 0:16]
                    link(dve.tensor_reduce(c16, Pf, AX, ALU.add))
                    link(dve.tensor_scalar(c16, c16, 1e-30, None, ALU.max))
                    link(dve.reciprocal(c16, c16))
                    link(dve.tensor_tensor(c16, c16, G3[:, 0:48:3], ALU.mult))
                    dve.tensor_tensor(Pf, Pf, bc(c16, 16), ALU.mult).then_inc(cp_n, 1)
            for i in range(TI):
                u = 48 + i
                unit_wait(u)
                dve.wait_ge(cv_w2, i + 1)
                yc = xn3[:, i, W5:D]
                dve.tensor_tensor(yc, ps[:, u % 2, :], cwp[2][:, i, :], ALU.add).then_inc(unit_free[u % 2], 1)
                dve.wait_ge(unit_free[u % 2], u // 2 + 1)
                dve.tensor_tensor(yc, yc, bgt3[:, i, :], ALU.mult).then_inc(att_ok, 1)
            dve.wait_ge(cp_p, 1)
            for i in range(TI):
                dve.tensor_copy(xn3[:, i, 0:W5], ps[:, 5 + i, :]).then_inc(att_ok, 1)
            dve.wait_ge(sq_ok, 4)
            link(dve.tensor_reduce(MS[:, 0:32], hT[:].rearrange("p (h d) -> p h d", d=HD), AX, ALU.add))
            root()
            xf = xn[:].rearrange("p (h d) -> p h d", d=HD)
            dve.tensor_tensor(xf, xf, bc(RS[:, 0:32], HD), ALU.mult).then_inc(xn_done, 1)
            to_hT((colB[:, 72:80], None), 3)
            residual(50, D)
            dve.wait_ge(ms_done, 8)
            root()
            normalise()
            to_hT((ab[:, 32:40], ab[:, 40:48]), 4)
            L3 = rL.rearrange("p (i n) -> p i n", i=2)
            E3 = rE.rearrange("p (i e) -> p i e", i=2)
            E4 = rE.rearrange("p (i g e) -> p i g e", i=2, g=8)
            O1 = rO1.rearrange("p (i e) -> p i e", i=2)
            O2 = rO2.rearrange("p (i e) -> p i e", i=2)
            P3 = rP.rearrange("p (i e) -> p i e", i=2)
            G2 = rG[:, 0:16].rearrange("p (i g) -> p i g", i=2)
            OG = rG[:, 16:32].rearrange("p (i g) -> p i g", i=2)
            PG = rG[:, 32:48].rearrange("p (i g) -> p i g", i=2)
            T3 = rT.rearrange("p (i e) -> p i e", i=2)

            def rb(ap, n):
                return bass.AP(tensor=ap.tensor, offset=ap.offset, ap=[ap.ap[0], [0, 2], [1, n]])

            def first_max(dst3, src3, desc, n, mx, scratch3):
                link(dve.tensor_reduce(mx, src3, AX, ALU.max))
                link(dve.tensor_tensor(scratch3, src3, bc(mx, n), ALU.is_equal))
                link(dve.tensor_tensor(scratch3, scratch3, rb(desc, n), ALU.mult))
                link(dve.tensor_reduce(rt[:, 30:32], scratch3, AX, ALU.max))
                link(dve.tensor_tensor(dst3, scratch3, bc(rt[:, 30:32], n), ALU.is_equal))

            dve.wait_ge(r_lg, 1)
            link(dve.tensor_tensor(L3, ps[:, 7, 0:144].rearrange("p (i n) -> p i n", i=2), rb(br[:, 0:72], 72), ALU.add))
            first_max(OG, L3[:, :, 0:8], cst[:, C_D8:C_D8 + 8], 8, rt[:, 0:2], PG)
            dve.tensor_tensor(G2, L3[:, :, 0:8], bc(rt[:, 0:2], 8), ALU.subtract).then_inc(r_s, 1)
            link(dve.tensor_scalar(PG, OG, -NEG, NEG, ALU.mult, ALU.add))
            for i in range(TI):
                e3 = L3[:, i, 8:72].rearrange("p (g e) -> p g e", g=8)
                link(dve.tensor_tensor(E4[:, i], e3, bc(OG[:, i, :], 8), ALU.mult))
                link(dve.tensor_tensor(E4[:, i], E4[:, i], bc(PG[:, i, :], 8), ALU.add))
            first_max(O1, E3, cst[:, C_D64:C_D64 + 64], 64, rt[:, 2:4], T3)
            link(dve.scalar_tensor_tensor(rE, rO1, -3e30, rE, ALU.mult, ALU.add))
            first_max(O2, E3, cst[:, C_D64:C_D64 + 64], 64, rt[:, 4:6], T3)
            dve.tensor_tensor(rA, rO1, rO2, ALU.add).then_inc(r_A, 1)
            dve.tensor_tensor(rt[:, 6:8], rt[:, 4:6], rt[:, 2:4], ALU.subtract).then_inc(r_s, 1)
            dve.wait_ge(r_e, 2)
            link(dve.tensor_reduce(rt[:, 10:12], G2, AX, ALU.add))
            link(dve.tensor_scalar(rt[:, 12:14], rt[:, 8:10], 1.0, None, ALU.add))
            link(dve.tensor_tensor(rt[:, 10:12], rt[:, 10:12], rt[:, 12:14], ALU.mult))
            link(dve.reciprocal(rt[:, 14:16], rt[:, 10:12]))
            link(dve.tensor_tensor(rt[:, 16:18], rt[:, 14:16], rt[:, 8:10], ALU.mult))
            dve.wait_ge(r_rk, 1)
            link(dve.tensor_copy(rt[0:64, 20:21], ps[0:64, 7, 128:129]))
            link(dve.tensor_scalar(rt[0:64, 22:30], cst[0:64, C_THR:C_THR + 8], rt[0:64, 20:21], None, ALU.is_lt))
            link(dve.tensor_reduce(rt[0:64, 21:22], rt[0:64, 22:30], AX, ALU.add))
            dve.tensor_scalar(nb128[0:64, :], cst[0:64, C_ONE:C_ONE + P], rt[0:64, 21:22], None, ALU.mult).then_inc(r_nb, 1)
            link(dve.tensor_copy(rP, ps[:, 7, 0:128]))
            dve.wait_ge(r_st, 1)
            link(dve.tensor_scalar(T3[:, 0, :], ps[:, 4, 192:256], float(SLOTS), None, ALU.mult))
            link(dve.tensor_copy(rt[0:64, 20:21], ps[0:64, 4, 257:258]))
            dve.tensor_scalar(cmpi[0:64, :], cst[0:64, C_IOTA:C_IOTA + 80], rt[0:64, 20:21], None,
                              ALU.is_ge).then_inc(r_ci, 1)
            for i in range(TI):
                link(dve.tensor_tensor(P3[:, i, :], P3[:, i, :], T3[:, 0, :], ALU.add))
            for o, dst in ((rO1, rQ[:, 0:2]), (rO2, rQ[:, 2:4])):
                link(dve.tensor_tensor(rE, o, rP, ALU.mult))
                link(dve.tensor_reduce(dst, E3, AX, ALU.add))
            link(dve.memset(acc, 0.0))
            dve.wait_ge(r_it, 1)
            link(dve.tensor_scalar(ids[0:1, 0:80], ps[0:1, 5, 260:340], float(NE - 1), None, ALU.min))
            dve.tensor_copy(ids[0:1, 80:81], ps[0:1, 4, 256:257]).then_inc(ids_ok, 1)

            LINKS = 13

            def round_(it):
                j = [0]

                def link_(ins):
                    j[0] += 1
                    ins.then_inc(m_ch, 1)
                    dve.wait_ge(m_ch, it * LINKS + j[0])

                iota = cc(C_IOTA)
                for i in range(TI):
                    p1, p2 = rQ[:, i:i + 1], rQ[:, 2 + i:3 + i]
                    s_, w_ = sel3[:, i, :], wsel3[:, i, :]
                    dve.tensor_scalar(s_, iota, p1, None, ALU.is_equal)
                    dve.tensor_scalar(w_, iota, p1, rt[:, 14 + i:15 + i], ALU.is_equal, ALU.mult)
                    link_(dve.tensor_scalar(rT, iota, p2, rt[:, 16 + i:17 + i], ALU.is_equal, ALU.mult))
                    link_(dve.scalar_tensor_tensor(s_, iota, p2, s_, ALU.is_equal, ALU.add))
                    ins = dve.tensor_tensor(w_, w_, rT, ALU.add)
                    if i == 0:
                        link_(ins)
                    else:
                        ins.then_inc(m_sel, 1)
                dve.wait_ge(m_d, it + 1)
                for c in range(4, DC):
                    ins = dve.tensor_scalar(xe3[:, c, :], ps[:, 5, (c - 4) * P:(c - 3) * P], ab[:, 32 + c:33 + c],
                                            ab[:, 40 + c:41 + c], ALU.mult, ALU.add)
                ins.then_inc(m_xe, 1)
                dve.wait_ge(m_wt, it + 1)
                dve.tensor_copy(wc, ps[:, 6, 0:256]).then_inc(m_wc, 1)
                dve.wait_ge(m_e, it + 1)
                link_(dve.tensor_scalar(hE, hE, 1.0, None, ALU.add))
                link_(dve.reciprocal(hE, hE))
                link_(dve.tensor_tensor(hE, hE, ps[:, 0, :], ALU.mult))
                dve.tensor_tensor(hA, hE, ps[:, 1, :], ALU.mult).then_inc(m_a, 1)
                dve.wait_ge(m_cb, it + 1)
                for k in range(4):
                    a_ = acc3[:, k // 2, (k % 2) * W5:(k % 2 + 1) * W5]
                    ins = dve.tensor_tensor(a_, a_, ps[:, (7, 6, 4, 5)[k], :], ALU.add)
                    if k < 3:
                        link_(ins)
                    else:
                        ins.then_inc(m_cbf, 1)
                link_(dve.tensor_scalar(rQ[:, 0:4], rQ[:, 0:4], float(-P), None, ALU.add))
                dve.wait_ge(m_cbf, it + 1)
                while j[0] < LINKS:
                    link_(dve.tensor_copy(rt[:, 40:41], rt[:, 0:1]))
                assert j[0] == LINKS

            with dve.Fori(0, MAIN) as it:
                round_(it)
            n_items = dve.value_load(ids[0:1, 80:81], min_val=0, max_val=ROUNDS * ITEMS)
            with dve.If(n_items > MAIN * ITEMS):
                with dve.Fori(MAIN, ROUNDS) as it:
                    round_(it)
            for i in range(TI):
                n_ch[0] += 1
                dve.tensor_tensor(acc3[:, i, :], acc3[:, i, :], grow[:, 2 * D:3 * D], ALU.mult).then_inc(dve_ch, 1)
                dve.wait_ge(dve_ch, n_ch[0])
            dve.tensor_tensor(x[:], x[:], acc, ALU.add).then_inc(x_ok, 1)

        @block.gpsimd
        def _(pool):
            rw = [(0, t["c_2"]), (8, t["b_ada_2"]), (56, t["norm1_w_2"]), (64, t["norm2_w_2"]), (72, t["out_norm_w_2"])]
            for r, a in rw:
                n = a.shape[1] // P
                pool.dma_start(rowsB[r:r + n, :], a.rearrange("o (c p) -> (o c) p", p=P)).then_inc(ld_rowsB, 16)
            for r, a in ((80, t["cmp_pos_k_2"]), (96, t["cmp_pos_v_2"])):
                pool.dma_start(rowsB[r:r + 16, :], a[0].rearrange("(j a) d -> j (a d)", a=2)).then_inc(ld_rowsB, 16)
            for a in range(2):
                pool.dma_start(rowsB[112:113, a * HD:(a + 1) * HD], t["q_norm_w_2"]).then_inc(ld_rowsB, 16)
                pool.dma_start(rowsB[113:116, a * HD:(a + 1) * HD], t["k_norm_w_2"][0]).then_inc(ld_rowsB, 16)
            pool.dma_start(bfr[:], rows(t["b_forget"], 0, 8)).then_inc(ld_small, 16)
            pool.dma_start(wf[:].rearrange("p (c n) -> p c n", c=DC),
                           w_in[:, 4096:4104].rearrange("(c p) n -> p c n", p=P)).then_inc(ld_small, 16)
            wr3 = wr[:].rearrange("p (c n) -> p c n", c=DC)
            pool.dma_start(wr3[:, :, 0:8], t["w_group_2"][0].rearrange("(c p) n -> p c n", p=P)).then_inc(ld_small, 16)
            pool.dma_start(wr3[:, :, 8:72], t["w_expert_2"][0].rearrange("(c p) n -> p c n", p=P)).then_inc(ld_small, 16)
            pool.dma_start(br[:, 0:8], rows(t["b_group_2"], 0, 8)).then_inc(ld_small, 16)
            pool.dma_start(br[:, 8:72], rows(t["b_expert_2"], 0, 64)).then_inc(ld_small, 16)
            for k, a in enumerate((t["cmp_k_w2_2"], t["cmp_v_w2_2"])):
                pool.dma_start(w2c[:, k * P:(k + 1) * P].rearrange("p (c n) -> p c n", c=2),
                               a[0].rearrange("(c p) n -> p c n", p=P)).then_inc(ld_small, 16)
            for k, (a, o) in enumerate(((t["b_ada"], 2 * D), (t["b_ada_2"], 2 * D), (t["b_ada_2"], 5 * D))):
                pool.dma_start(grow[:, k * D:(k + 1) * D], rows(a, o, D)).then_inc(ld_grow, 16)
            pool.dma_start(bg, rows(t["b_gate"], 0, 2 * D)).then_inc(ld_bg, 16)
            pool.dma_start(fg, rows(t["final_g"], 0, D)).then_inc(ld_bg, 16)
            pool.memset(rbx[:], NEG).then_inc(rb_ok, 1)
            pool.wait_ge(rb_ok, 1)
            pool.dma_start(rbx[0:32, :], t["rel_bias_2"]).then_inc(ld_rows1, 16)
            pool.dma_start(hoT[:], t["buckets"]).then_inc(ld_rows1, 16)

            def below_diagonal(tile):
                return pool.affine_select(out=diag(tile), in_=diag(tile), compare_op=ALU.is_gt, fill=0.0, base=0,
                                          pattern=[[0, 2], [1, P]], channel_multiplier=-1)

            for h in range(H):
                pool.wait_ge(st_L, h + 1)
                below_diagonal(zb(PT, h % 2)).then_inc(st_Lm, 1)
            pool.wait_ge(f_lf, 1)
            for h in range(H):
                if h >= 2:
                    pool.wait_ge(fx_z, h - 1)
                u = zb(U, h % 2)
                pool.tensor_scalar(u[:, 0:P], cc(C_LE), fl[:, 48 + h:49 + h], None, ALU.mult)
                pool.tensor_scalar(u[:, P:256], cc(C_ONE), fl[:, 48 + h:49 + h], None, ALU.mult)
                pool.tensor_scalar(u[:, 256:384], cc(C_LE), fl[:, 56 + h:57 + h], None, ALU.mult).then_inc(fx_u, 1)
            pool.wait_ge(x_ok, 1)
            for a in (X, HTv, Vbd, Pc):
                pool.memset(a, 0.0).then_inc(pad_ok, 1)
            for k in range(3):
                pool.dma_start(cw[:, k * W5:(k + 1) * W5], rows(t["conv_w_2"], k * W5, W5)).then_inc(ld_cw, 16)
            pool.wait_ge(misc_free, 31)
            pool.dma_start(bias_dram.rearrange("q h m -> h q m"),
                           bass.AP(tensor=bR.tensor, offset=bR.offset, ap=[bR.ap[0], [0, P], [1, BM]])).then_inc(st_bias, 16)
            pool.wait_ge(st_bias, 16)
            pool.dma_start(B, bass.AP(tensor=bias_dram.tensor, offset=P - 1, ap=[[H * BM - 1, P], [BM, H], [1, BW]])) \
                .then_inc(ld_bias, 16)
            pool.wait_ge(ld_cw, 48)
            for i in range(TI):
                pool.wait_ge(unit_free[i], 24)
                for k in range(3):
                    pool.tensor_tensor(cwp[k][:, i, :], cu3[:, i, :], cw[:, k * W5:(k + 1) * W5],
                                       ALU.mult).then_inc((cv_w, cv_w, cv_w2)[k], 1)


_INS = ["x", "c", "w_ada", "b_ada", "norm_g", "w_in", "b_forget", "w_o_sb", "w_o_fox", "b_gate", "w_out", "final_g",
        "c_2", "w_ada_2", "b_ada_2", "norm1_w_2", "w_in_2", "q_norm_w_2", "k_norm_w_2", "cmp_pos_k_2", "cmp_pos_v_2",
        "cmp_k_w1_2", "cmp_k_w2_2", "cmp_v_w1_2", "cmp_v_w2_2", "conv_w_2", "out_norm_w_2", "w_out_2", "rel_bias_2",
        "norm2_w_2", "w_group_2", "b_group_2", "w_expert_2", "b_expert_2", "w1_2", "w3_2", "w2_2"]


def kernel(**inputs):
    import numpy as _np
    import concourse.bacc as _bacc
    from concourse.bass_utils import run_bass_kernel_spmd as _run

    nc = _bacc.Bacc("TRN2", target_bir_lowering=False, num_devices=1)
    arrays = {n: _np.ascontiguousarray(inputs[n]) for n in _INS}
    arrays["constants"] = constants()
    arrays["buckets"] = bucket_onehot()
    t = {n: nc.dram_tensor(f"in_{n}_dram", a.shape, F32, kind="ExternalInput").ap() for n, a in arrays.items()}
    out = nc.dram_tensor("out_0_dram", (1, T, D), F32, kind="ExternalOutput").ap()
    build(nc, t, out)
    r = _run(nc, [{f"in_{n}_dram": a for n, a in arrays.items()}], core_ids=[0])
    return r.results[0]["out_0_dram"]
```

```python
from contextlib import ExitStack

import numpy as np

import concourse.bass as bass
from concourse import mybir

ALU = mybir.AluOpType
ACT = mybir.ActivationFunctionType
F32 = mybir.dt.float32
I32 = mybir.dt.int32
AX = mybir.AxisListType.X

P = 128
T = 256
TI = T // P
D = 1024
DC = D // P
HD = 64
H = 8
W5 = 512
EPS = 1e-6
NEG = -1e30
QSCALE = HD ** -0.5
NCMP = (T - 32) // 16 + 1
NE = 64
SLOTS = 32
ITEMS = 4
MAIN = NE // ITEMS
ROUNDS = MAIN + 2 * T // SLOTS // ITEMS
BW = 400
BM = BW + P
RING = 4
MRING = 6
MSLOT = (0, 1, 4, 5, 2, 3)
STAGES = 12

C_ID, C_INV, C_GE, C_LE, C_LT, C_ONE, C_GT, C_IOTA, C_S1, C_S1C, C_S2, C_S2C = [k * P for k in range(12)]
C_NM = 12 * P
C_NS = C_NM + 256
C_D64 = C_NS + P
C_D8 = C_D64 + 64
C_THR = C_D8 + 8
C_N = C_THR + 8


def constants():
    p = np.arange(P)[:, None]
    f = np.arange(P)[None, :]
    blocks = [p == f, (p + f >= 0) / 32.0, p >= f, p <= f, p < f, p >= 0 * f, p > f, f + 0 * p,
              f == p + 1, (p == 127) & (f == 0), f == p + 2, f == p - 126]
    f2 = np.arange(256)[None, :]
    blocks.append(np.where(128 + p - f2 >= 0, 0.0, NEG))
    blocks.append(np.where(p >= f, NEG, 0.0))
    blocks.append(np.tile(64.0 - np.arange(64), (P, 1)))
    blocks.append(np.tile(8.0 - np.arange(8), (P, 1)))
    blocks.append(np.tile(np.append(32.0 * np.arange(1, 8), 1e9), (P, 1)))
    return np.concatenate([np.asarray(b, np.float32) for b in blocks], 1)


def bucket_onehot():
    dist = 255 - np.arange(BM)
    n = np.maximum(dist, 0)
    nf = np.maximum(n, 1).astype(np.float32)
    large = 16 + (np.log(nf / np.float32(16)) / np.float32(np.log(8.0)) * np.float32(16)).astype(np.int32)
    b = np.where(n < 16, n, np.minimum(large, 31))
    b = np.where(dist < 0, 32, b)
    return (np.arange(33)[:, None] == b[None, :]).astype(np.float32)


def build(nc, t, out):
    with ExitStack() as ctx:
        def sb(name, cols, dt=F32, parts=P):
            return ctx.enter_context(nc.sbuf_tensor(name, [parts, cols], dt))

        def sem(name):
            return ctx.enter_context(nc.semaphore(name))

        ps = ctx.enter_context(nc.psum_tensor("ps", [P, 8, W5], F32))
        bias_dram = nc.dram_tensor("bias_dram", [P, H, BM], F32).ap()

        ring = sb("ring", RING * 4096)
        arena = sb("arena", 16384)
        cst = sb("cst", C_N)
        x = sb("x_sb", TI * D)
        hT = sb("hT", DC * T)
        hoT = sb("hoT", BM, parts=33)
        xn = sb("xn", TI * D)
        modt = sb("modt", W5)
        grow = sb("grow", 3 * D)
        zS = sb("zS", 2 * 384)
        Pb = sb("Pb", 2 * 384)
        PT = sb("PT", 2 * 384)
        R = sb("R", 384)
        U = sb("U", 2 * 384)
        rowsA = sb("rowsA", P)
        rowsB = sb("rowsB", P)
        colA = sb("colA", 40)
        colB = sb("colB", 128)
        c32 = sb("c32", 2 * DC * 32)
        mod2c = sb("mod2c", 64)
        ab = sb("ab", 6 * DC)
        stat = sb("stat", 4 * 72)
        soft = sb("soft", 3 * 32)
        ssum = sb("ssum", 24)
        cm = sb("cm", 32)
        wf = sb("wf", DC * 8)
        fl = sb("fl", 6 * 16)
        bfr = sb("bfr", 8)
        wr = sb("wr", DC * 72)
        br = sb("br", 72)
        w2c = sb("w2c", 2 * 2 * HD)
        rbx = sb("rbx", 8)
        rt = sb("rt", 64)
        ids = sb("ids", 96, I32)

        def cc(o, n=P, parts=P):
            return cst[0:parts, o:o + n]

        IDN = cc(C_ID)

        def ar(o, n):
            return arena[:, o:o + n]
        qT = [ar(0, 1024), ar(2048, 1024)]
        kT = [ar(1024, 1024), ar(3072, 1024)]
        vv = [ar(4096, 1024), ar(5120, 1024)]
        sz = [ar(6144, 1024), ar(7168, 1024)]
        gates = ar(8192, 4096)
        bg = ar(12288, 2048)
        fg = ar(14336, 1024)
        merged = ar(4096, 2048)
        B = ar(0, H * BW).rearrange("p (h f) -> p h f", h=H)
        cw = ar(3200, 1536)
        QK = ar(4736, 1536)
        qkT = ar(6272, 1536)
        kvd = ar(7808, 1024)
        vS = ar(8832, 512)
        X = ar(9344, 1024)
        Hh = ar(10368, 512)
        HE = ar(10880, 512)
        HTk = ar(11392, 64)
        HTv = ar(11456, 512)
        kc = ar(11968, 128)
        kcT = ar(12096, 16)
        Vbd = ar(12112, 512)
        Pc = ar(12624, 512)
        PcT = ar(13136, 512)
        bgt = ar(13648, 1024)
        cu = ar(14672, 1024)
        bR = arena[0:8, 15360:15360 + BM]
        Sc = ar(15696, 256)
        G3 = ar(15952, 48)
        cw0 = ar(4736, 1024)
        cw1 = ar(7808, 1024)
        cw2 = ar(9344, 1024)
        sq = hT
        xe = ar(0, 1024)
        acc = ar(1024, 2048)
        hE = ar(3072, 512)
        hA = ar(3584, 512)
        actT = ar(4096, 512)
        ye = ar(4608, 1024)
        sel = ar(5632, 256)
        wsel = ar(5888, 256)
        wc = ar(6144, 256)
        rL = ar(6400, 144)
        rE = ar(6544, 128)
        rO1 = ar(6672, 128)
        rO2 = ar(6800, 128)
        rA = ar(6928, 128)
        rP = ar(7056, 128)
        rG = ar(7184, 64)
        rQ = ar(7248, 64)
        nb128 = ar(7312, 128)
        cmpi = ar(7440, 80)
        rT = ar(7520, 128)

        def ringv(n):
            s = n % RING
            return ring[:, s * 4096:(s + 1) * 4096]

        def mringv(s):
            return ring[:, s * 4096:(s + 1) * 4096] if s < RING else \
                arena[:, 8192 + (s - RING) * 4096:8192 + (s - RING + 1) * 4096]

        ring_in = [sem(f"ring_in{s}") for s in range(RING)]
        mring_in = [sem(f"mring_in{s}") for s in range(MRING)]
        mring_free = sem("mring_free")
        (ld_id, ld_cst, ld_x, ld_rowsA, ld_rowsB, ld_rows1, ld_small, ld_grow, ld_bias, st_bias, ld_cw, st_out) = [
            sem(n) for n in ("ld_id", "ld_cst", "ld_x", "ld_rowsA", "ld_rowsB", "ld_rows1", "ld_small", "ld_grow",
                             "ld_bias", "st_bias", "ld_cw", "st_out")]
        (ms_done, xn_done, xt_done, hta_done, htv_done, ab_done, mod_raw, cols_tr, c1_ok, colB_ok,
         c2_e, c2_ok, ab_ok, ab2_ok) = [
            sem(n) for n in ("ms_done", "xn_done", "xt_done", "hta_done", "htv_done", "ab_done",
                             "mod_raw", "cols_tr", "c1_ok", "colB_ok", "c2_e", "c2_ok", "ab_ok", "ab2_ok")]
        unit_done = [sem("unit_done0"), sem("unit_done1")]
        unit_free = [sem("unit_free0"), sem("unit_free1")]
        (misc_done, misc_free, mod_ok, tr_done, tr_free, e_sig) = [
            sem(n) for n in ("misc_done", "misc_free", "mod_ok", "tr_done", "tr_free", "e_sig")]
        (st_z, st_zc, st_ln, st_L, st_Lm, st_c, st_w, st_pv) = [
            sem(n) for n in ("st_z", "st_zc", "st_ln", "st_L", "st_Lm", "st_c", "st_w", "st_pv")]
        (fx_u, fx_z, fx_m, fx_p, fx_sc, fx_pv) = [
            sem(n) for n in ("fx_u", "fx_z", "fx_m", "fx_p", "fx_sc", "fx_pv")]
        names = ("f_e f_l f_lf ya_ok mg_ok x_ok sq_ok qk_ok cp_T cp_X cp_h cp_e cp_H cp_w2 cp_v cp_k cp_z cp_s "
                 "cp_x cp_p cp_n cv_w cv_w2 rb_ok pad_ok att_ok ld_bg").split()
        (f_e, f_l, f_lf, ya_ok, mg_ok, x_ok, sq_ok, qk_ok, cp_T, cp_X, cp_h, cp_e, cp_H, cp_w2, cp_v, cp_k, cp_z,
         cp_s, cp_x, cp_p, cp_n, cv_w, cv_w2, rb_ok, pad_ok, att_ok, ld_bg) = [sem(n) for n in names]
        (r_lg, r_s, r_e, r_A, r_rk, r_nb, r_st, r_ci, r_it, ids_ok) = [
            sem(n) for n in ("r_lg", "r_s", "r_e", "r_A", "r_rk", "r_nb", "r_st", "r_ci", "r_it", "ids_ok")]
        (m_sel, m_d, m_xe, m_e, m_a, m_at, m_atc, m_ye, m_cb, m_cbf, m_wt, m_wc, m_ch) = [
            sem(n) for n in ("m_sel", "m_d", "m_xe", "m_e", "m_a", "m_at", "m_atc", "m_ye", "m_cb", "m_cbf",
                             "m_wt", "m_wc", "m_ch")]
        dve_ch, act_ch = sem("dve_chain"), sem("act_chain")

        def colchunk(w, c0, n=W5):
            return w[:, c0:c0 + n].rearrange("(c p) n -> p c n", p=P), (DC, n)

        w_in, w_in2 = t["w_in"][0], t["w_in_2"][0]
        ada, ada2 = t["w_ada"][0], t["w_ada_2"][0]
        chunks = [colchunk(ada, n * W5) for n in range(4)]
        PROJ0 = len(chunks)
        proj_cols = [512, 0, 1024, 1536, 2560, 2048, 3072, 3584] + [4104 + n * W5 for n in range(4)]
        for q in range(12):
            chunks += [colchunk(w_in, proj_cols[q]), colchunk(ada2, q * W5)]
        ADAG = len(chunks)
        chunks += [colchunk(ada, n * W5) for n in (4, 5)]
        WO = len(chunks)
        for w in (t["w_o_sb"][0], t["w_o_fox"][0]):
            chunks.append((w.rearrange("(c p) n -> p c n", p=P), (4, 1024)))
        WOUT = len(chunks)
        chunks += [colchunk(t["w_out"][0], n * W5) for n in range(2)]
        KV = len(chunks)
        chunks += [colchunk(w_in2, 512), colchunk(w_in2, 1024, 280), colchunk(w_in2, 0)]
        CMP = len(chunks)
        for w in (t["cmp_k_w1_2"][0], t["cmp_v_w1_2"][0]):
            chunks.append((w.rearrange("(j p) n -> p j n", p=P), (16, 256)))
        CONV = len(chunks)
        chunks += [colchunk(w_in2, 1304 + n * W5) for n in range(3)]
        WO2 = len(chunks)
        chunks += [colchunk(t["w_out_2"][0], n * W5) for n in range(2)]
        NCH = len(chunks)

        def cview(n):
            a, b = chunks[n][1]
            return ringv(n)[:, 0:a * b].rearrange("p (a b) -> p a b", a=a)

        def unit_read(u):
            return unit_done[u % 2], u // 2 + 1

        read_by = [(mod_raw, n + 1) for n in range(4)]
        for q in range(12):
            read_by += [unit_read(2 * q + 1), (misc_done, 2 + 2 * q)]
        read_by += [(misc_done, 26), (misc_done, 28), unit_read(27), unit_read(31), unit_read(34), unit_read(35),
                    unit_read(39), unit_read(40), unit_read(41), (cp_h, 1), (cp_h, 2),
                    unit_read(43), unit_read(45), unit_read(47), unit_read(52), unit_read(53)]
        assert len(read_by) == NCH

        def rows(ap, c0, n):
            return bass.AP(tensor=ap.tensor, offset=ap.offset + c0, ap=[[0, P], [1, n]])

        def Z(b):
            return ps[:, 2 + b, 0:384]

        def diag(tile):
            return bass.AP(tensor=tile.tensor, offset=tile.offset, ap=[tile.ap[0], [256, 2], [1, P]])

        v3 = [vv[b].rearrange("p (i n) -> p i n", i=TI) for b in range(2)]
        qT3 = [q.rearrange("p (m t) -> p m t", m=4) for q in qT]
        kT3 = [k.rearrange("p (m t) -> p m t", m=4) for k in kT]
        hT3 = hT[:].rearrange("p (c t) -> p c t", c=DC)
        x3 = x[:].rearrange("p (i d) -> p i d", i=TI)
        xn3 = xn[:].rearrange("p (i d) -> p i d", i=TI)
        g3 = gates.rearrange("p (i n) -> p i n", i=TI)
        mg3 = merged.rearrange("p (i n) -> p i n", i=TI)
        sz3 = [s.rearrange("p (i n) -> p i n", i=TI) for s in sz]
        yT3 = qT3
        QK4 = QK.rearrange("p (i h d) -> p i h d", i=TI, h=12)
        qkT3 = qkT.rearrange("p (m t) -> p m t", m=6)
        kvd6 = kvd.rearrange("p (i kv g a d) -> p i kv g a d", i=2, kv=2, g=2, a=2)
        vS4 = vS.rearrange("p (a i n) -> p a i n", a=2, i=2)
        X5 = X.rearrange("p (kv j g n) -> p kv j g n", kv=2, j=16, g=2)
        HTk3 = HTk.rearrange("p (c n) -> p c n", c=2)
        HTv5 = HTv.rearrange("p (c g r n) -> p c g r n", c=2, g=2, r=4)
        Vbd3 = Vbd.rearrange("p (g n) -> p g n", g=2)
        Pc4 = Pc.rearrange("p (i h n) -> p i h n", i=2, h=8)
        PcT4 = PcT.rearrange("p (i g n) -> p i g n", i=2, g=2)
        Sc4 = Sc.rearrange("p (i h n) -> p i h n", i=2, h=8)
        G34 = G3.rearrange("p (i h n) -> p i h n", i=2, h=8)
        bgt3 = bgt.rearrange("p (i n) -> p i n", i=TI)
        cu3 = cu.rearrange("p (i n) -> p i n", i=TI)
        cwp = [a.rearrange("p (i n) -> p i n", i=TI) for a in (cw0, cw1, cw2)]
        xe3 = xe.rearrange("p (c n) -> p c n", c=DC)
        acc3 = acc.rearrange("p (i n) -> p i n", i=TI)
        actT3 = actT.rearrange("p (j n) -> p j n", j=4)
        sel3 = sel.rearrange("p (i n) -> p i n", i=TI)
        wsel3 = wsel.rearrange("p (i n) -> p i n", i=TI)
        wc3 = wc.rearrange("p (i n) -> p i n", i=TI)

        def zb(buf, b):
            return buf[:, b * 384:(b + 1) * 384]

        MS, VA, RS, TM = (stat[:, k * 72:(k + 1) * 72] for k in range(4))
        SM, MX, CO = (soft[:, k * 32:(k + 1) * 32] for k in range(3))
        NRM = [(2, P), (2, P), (2, P), (12, P), (12, P), (2, 16), (16, P), (16, P), (1, P), (1, P)]
        NO = [sum(w for w, _ in NRM[:k]) for k in range(len(NRM) + 1)]
        JA, JB = PT[:, 0:W5], Pb[:, 0:W5]

        block = ctx.enter_context(nc.Block())

        @block.sync
        def _(sp):
            sp.dma_start(cst[:, 0:2 * P], t["constants"][:, 0:2 * P]).then_inc(ld_id, 16)
            for n in range(NCH):
                if n == 1:
                    sp.dma_start(x3, t["x"][0].rearrange("(i p) d -> p i d", p=P)).then_inc(ld_x, 16)
                if n >= RING:
                    sp.wait_ge(*read_by[n - RING])
                sp.dma_start(cview(n), chunks[n][0]).then_inc(ring_in[n % RING], 16)
            w1, w3, w2 = t["w1_2"][0], t["w3_2"][0], t["w2_2"][0]

            def stage(s, ex):
                dst = mringv(MSLOT[s % MRING])
                for e in range(ITEMS):
                    if s < 8:
                        w = (w1, w3)[s % 2]
                        src = w[bass.ds(ex[e], 1), (s // 2) * 256:(s // 2 + 1) * 256, :] \
                            .rearrange("o (r p) n -> p (o r) n", p=P)
                        d = dst[:, e * 1024:(e + 1) * 1024].rearrange("p (r n) -> p r n", r=2)
                    else:
                        src = w2[bass.ds(ex[e], 1), (s - 8) * P:(s - 7) * P, :].rearrange("o p n -> p (o n)")
                        d = dst[:, e * 1024:(e + 1) * 1024]
                    sp.dma_start(d, src).then_inc(mring_in[s % MRING], 16)

            first = [read_by[NCH - 4], read_by[NCH - 3], (att_ok, 4), (att_ok, 4), read_by[NCH - 2], read_by[NCH - 1]]
            for s in range(STAGES):
                if s < MRING:
                    sp.wait_ge(*first[s])
                else:
                    sp.wait_ge(mring_free, s - MRING + 1)
                stage(s, range(ITEMS))
            with sp.Fori(1, MAIN) as it:
                for s in range(STAGES):
                    sp.wait_ge(mring_free, it * STAGES + (s - MRING + 1))
                    stage(s, [it * ITEMS + e for e in range(ITEMS)])
            sp.wait_ge(ids_ok, 1)
            n_over = sp.value_load(ids[0:1, 16:17], min_val=0, max_val=16)
            with sp.If(n_over > 0):
                with sp.Fori(MAIN, ROUNDS) as it:
                    ex = [sp.value_load(ids[0:1, bass.ds((it - MAIN) * ITEMS + e, 1)], min_val=0, max_val=NE - 1)
                          for e in range(ITEMS)]
                    for s in range(STAGES):
                        sp.wait_ge(mring_free, it * STAGES + (s - MRING + 1))
                        stage(s, ex)
            sp.wait_ge(x_ok, 9)
            sp.dma_start(out[0].rearrange("(i p) d -> p i d", p=P), x3).then_inc(st_out, 16)
            sp.wait_ge(st_out, 16)

        @block.tensor
        def _(pe):
            used = [0]
            units = [0]
            misc = [0]
            trs = [0]

            def chunk_in(n):
                pe.wait_ge(ring_in[n % RING], 16 * (n // RING + 1))

            def unit_bank():
                u = units[0]
                if u >= 2:
                    pe.wait_ge(unit_free[u % 2], u // 2)
                units[0] += 1
                return u % 2

            def misc_bank():
                if misc[0]:
                    pe.wait_ge(misc_free, misc[0])
                misc[0] += 1

            def tr_bank():
                if trs[0]:
                    pe.wait_ge(tr_free, trs[0])
                trs[0] += 1

            def mod_product(n, which, bank, done):
                chunk_in(n)
                for c in range(DC):
                    j = c % 4
                    cv = c32[:, (which * DC + c) * 32:(which * DC + c + 1) * 32]
                    mm = pe.matmul(ps[32 * j:32 * j + 32, bank, :], cv, cview(n)[:, c, :], start=c < 4,
                                   stop=c >= 4, skip_group_check=True)
                mm.then_inc(done, 1)

            def mod_cols(bank, done):
                for m in range(4):
                    mm = pe.matmul(ps[:, bank, m:m + 1], modt[:, m * P:(m + 1) * P], cst[:, C_INV:C_INV + 1],
                                   start=True, stop=True)
                mm.then_inc(done, 1)

            def mod_row(bank, done):
                pe.matmul(ps[:, bank, :], cc(C_INV), modt[:], start=True, stop=True).then_inc(done, 1)

            def to_features(src3, i, k):
                pe.wait_ge(xn_done, k)
                for c in range(DC):
                    mm = pe.transpose(ps[:, (2, 5)[i] + c // 4, (c % 4) * P:(c % 4 + 1) * P],
                                      src3[:, i, c * P:(c + 1) * P], IDN)
                mm.then_inc(xt_done, 1)

            pe.wait_ge(ld_id, 16)
            pe.wait_ge(ld_rowsA, 48)
            pe.transpose(ps[:, 7, 0:40], rowsA[0:40, :], cst[0:40, C_ID:C_ID + 40]).then_inc(cols_tr, 1)
            pe.wait_ge(c1_ok, 1)
            for n in range(4):
                mod_product(n, 0, 4, mod_raw)
                pe.wait_ge(mod_ok, n + 1)
                for m in range(4):
                    mm = pe.matmul(ps[:, 0, 4 * n + m:4 * n + m + 1], modt[:, m * P:(m + 1) * P],
                                   cst[:, C_INV:C_INV + 1], start=True, stop=True)
                mm.then_inc(ab_done, 1)
                if n < TI:
                    to_features(xn3, n, n + 1)
                if n == 2:
                    pe.wait_ge(ld_rowsB, 16 * 11)
                    pe.transpose(ps[:, 7, 0:116], rowsB[0:116, :], cst[0:116, C_ID:C_ID + 116]).then_inc(cols_tr, 1)

            def stationary_unit(n, half, b=None):
                b = unit_bank()
                for m2 in range(2):
                    for c in range(DC):
                        mm = pe.matmul(ps[:, b, m2 * 256:(m2 + 1) * 256],
                                       cview(n)[:, c, (2 * half + m2) * P:(2 * half + m2 + 1) * P],
                                       hT3[:, c, :], start=c == 0, stop=c == DC - 1)
                mm.then_inc(unit_done[b], 1)

            def token_unit(lhs3, i, rhs, kc_, n=W5):
                b = unit_bank()
                for c in range(kc_):
                    mm = pe.matmul(ps[:, b, 0:n], lhs3[:, c, i * P:(i + 1) * P], rhs[:, c, :],
                                   start=c == 0, stop=c == kc_ - 1)
                mm.then_inc(unit_done[b], 1)

            def f_logits():
                misc_bank()
                for i in range(TI):
                    for c in range(DC):
                        mm = pe.matmul(ps[:, 7, i * 8:(i + 1) * 8], hT3[:, c, i * P:(i + 1) * P],
                                       wf[:, c * 8:(c + 1) * 8], start=c == 0, stop=c == DC - 1)
                mm.then_inc(misc_done, 1)

            def mod2_raw(q):
                misc_bank()
                if q == 0:
                    pe.wait_ge(c2_ok, 1)
                mod_product(PROJ0 + 2 * q + 1, 1, 7, misc_done)

            def mod2_out(q):
                misc_bank()
                if q in (4, 5, 10, 11):
                    mod_row(7, misc_done)
                else:
                    mod_cols(7, misc_done)

            def stick_scores(h):
                b, m, lo = h % 2, h // 2, 64 * (h % 2)
                if h == 0:
                    pe.wait_ge(ld_cst, 16)
                    pe.wait_ge(unit_free[0], 2)
                    pe.wait_ge(unit_free[1], 2)
                if h >= 2:
                    pe.wait_ge(st_w, h - 1)
                k, q = kT3[0][lo:lo + 64, m, :], qT3[0][lo:lo + 64, m, :]
                pe.matmul(ps[:, 2 + b, 0:256], k[:, 0:P], q[:, :], start=True, stop=False, skip_group_check=True)
                pe.matmul(ps[:, 2 + b, 256:384], k[:, P:T], q[:, P:T], start=False, stop=False,
                          skip_group_check=True).then_inc(st_z, 1)

            def stick_after(h):
                b = h % 2
                L = zb(PT, b)
                pe.wait_ge(st_Lm, h + 1)
                pe.matmul(ps[:, 2 + b, 0:256], cc(C_GE), L[:, 0:256], start=False, stop=False, skip_group_check=True)
                pe.matmul(ps[:, 2 + b, P:256], cc(C_ONE), L[:, 256:384], start=False, stop=False, skip_group_check=True)
                pe.matmul(ps[:, 2 + b, 256:384], cc(C_GE), L[:, 256:384], start=False, stop=False, skip_group_check=True)
                for o in (0, 256):
                    mm = pe.matmul(ps[:, 2 + b, o:o + P], IDN, cc(C_NS), start=False, stop=True, skip_group_check=True)
                mm.then_inc(st_c, 1)

            def pv(w, v0, v1, h, blocks, start0):
                pe.matmul(ps[:, 5, h * HD:(h + 1) * HD], w[:, blocks[0]:blocks[0] + P], v0, start=start0,
                          stop=False, skip_group_check=True)
                pe.matmul(ps[:, 6, h * HD:(h + 1) * HD], w[:, blocks[1]:blocks[1] + P], v0, start=start0,
                          stop=False, skip_group_check=True)
                return pe.matmul(ps[:, 6, h * HD:(h + 1) * HD], w[:, blocks[2]:blocks[2] + P], v1, start=False,
                                 stop=False, skip_group_check=True)

            def stick_pv(h):
                if h == 0:
                    pe.wait_ge(unit_free[0], 3)
                    pe.wait_ge(unit_free[1], 3)
                pe.wait_ge(st_w, h + 1)
                pv(zb(Pb, h % 2), v3[0][:, 0, h * HD:(h + 1) * HD], v3[0][:, 1, h * HD:(h + 1) * HD], h,
                   (0, 128, 256), True).then_inc(st_pv, 1)

            def y_transposes(b, i):
                tr_bank()
                pe.wait_ge(ya_ok, 2 * b + i + 1)
                for c in range(4):
                    mm = pe.transpose(ps[:, 4, c * P:(c + 1) * P], sz3[b][:, i, c * P:(c + 1) * P], IDN)
                mm.then_inc(tr_done, 1)

            def fox_scores(h):
                b, m, lo = h % 2, h // 2, 64 * (h % 2)
                if h == 0:
                    pe.wait_ge(unit_free[0], 6)
                    pe.wait_ge(unit_free[1], 6)
                    pe.wait_ge(st_w, 8)
                if h >= 2:
                    pe.wait_ge(fx_m, h - 1)
                k, q = kT3[1][lo:lo + 64, m, :], qT3[1][lo:lo + 64, m, :]
                u = zb(U, b)
                pe.wait_ge(fx_u, h + 1)
                kw = dict(skip_group_check=True)
                pe.matmul(ps[:, 2 + b, 0:P], q[:, 0:P], k[:, 0:P], start=True, stop=False, **kw)
                pe.matmul(ps[:, 2 + b, P:384], q[:, P:T], k[:, 0:T], start=False, stop=False, **kw)
                pe.matmul(ps[:, 2 + b, 0:P], u[:, 0:P], cc(C_GT), start=False, stop=False, **kw)
                pe.matmul(ps[:, 2 + b, P:256], u[:, P:256], cc(C_GT), start=False, stop=False, **kw)
                pe.matmul(ps[:, 2 + b, P:384], u[:, 256:384], cst[:, C_ONE:C_ONE + 256], start=False,
                          stop=True, **kw).then_inc(fx_z, 1)

            def p_transposes(k, b, ready):
                tr_bank()
                pe.wait_ge(ready, k + 1)
                for c in range(3):
                    mm = pe.transpose(ps[:, 4, c * P:(c + 1) * P], zb(Pb, b)[:, c * P:(c + 1) * P], IDN)
                mm.then_inc(tr_done, 1)

            def fox_pv(h, tr_index):
                if h == 0:
                    pe.wait_ge(unit_free[0], 7)
                    pe.wait_ge(unit_free[1], 7)
                    pe.wait_ge(ya_ok, 2)
                pe.wait_ge(tr_free, tr_index + 1)
                pv(zb(PT, h % 2), v3[1][:, 0, h * HD:(h + 1) * HD], v3[1][:, 1, h * HD:(h + 1) * HD], h,
                   (0, 128, 256), True).then_inc(fx_pv, 1)

            pe.wait_ge(hta_done, 2)
            pe.wait_ge(htv_done, 2)
            fox_tr = {}
            for u in range(26):
                if u < 24:
                    q, half = u // 2, u % 2
                    n = PROJ0 + 2 * q
                    if half == 0:
                        chunk_in(n)
                    if q in (0, 1, 4, 5):
                        stationary_unit(n, half)
                    else:
                        token_unit(hT3, half, cview(n), DC)
                if u == 0:
                    pe.wait_ge(ld_small, 16 * 8)
                    f_logits()
                if u % 2 == 0 and 2 <= u <= 24:
                    mod2_out(u // 2 - 1)
                if 0 <= u - 4 < H:
                    stick_scores(u - 4)
                if 0 <= u - 5 < H:
                    stick_after(u - 5)
                if 0 <= u - 6 < H:
                    stick_pv(u - 6)
                if 0 <= u - 14 < H:
                    fox_scores(u - 14)
                if 0 <= u - 16 < H:
                    fox_pv(u - 16, fox_tr[u - 16])
                if u in (14, 15):
                    y_transposes(0, u - 14)
                if 0 <= u - 15 < H:
                    fox_tr[u - 15] = trs[0]
                    p_transposes(u - 15, (u - 15) % 2, fx_p)
                if u % 2 == 1 and u < 24:
                    mod2_raw(u // 2)

            def gate_row(k):
                misc_bank()
                if k % 2 == 0:
                    mod_product(ADAG + k // 2, 0, 7, misc_done)
                else:
                    mod_row(7, misc_done)

            def rel_bias(n0, n1):
                misc_bank()
                pe.matmul(ps[0:8, 7, 0:n1 - n0], rbx[0:33, :], hoT[0:33, n0:n1], start=True,
                          stop=True).then_inc(misc_done, 1)

            gate_row(0)
            pe.wait_ge(tr_free, 2)
            chunk_in(WO)
            for i in range(TI):
                for n in range(2):
                    token_unit(yT3[0], i, cview(WO)[:, :, n * W5:(n + 1) * W5], 4)
                    if 2 * i + n < 3:
                        gate_row(2 * i + n + 1)
                if i == 0:
                    y_transposes(1, 0)
            pe.wait_ge(ld_rows1, 32)
            pe.wait_ge(rb_ok, 1)
            rel_bias(0, W5)
            y_transposes(1, 1)
            chunk_in(WO + 1)
            for i in range(TI):
                pe.wait_ge(tr_free, trs[0] - 1 + i)
                for n in range(2):
                    token_unit(yT3[1], i, cview(WO + 1)[:, :, n * W5:(n + 1) * W5], 4)
                    if i == n == 0:
                        rel_bias(W5, BM)
                    if i == 1 and n == 0:
                        to_features(mg3, 0, 3)
            for i in range(TI):
                pe.wait_ge(hta_done, 3 + i)
                pe.wait_ge(htv_done, 3 + i)
                for n in range(2):
                    if i == 0:
                        chunk_in(WOUT + n)
                    if i == n == 1:
                        to_features(xn3, 0, 5)
                    token_unit(hT3, i, cview(WOUT + n), DC)
                    if i == n == 0:
                        to_features(mg3, 1, 4)
            for i in range(TI):
                pe.wait_ge(hta_done, 5 + i)
                pe.wait_ge(htv_done, 5 + i)
                for k in range(3):
                    if i == 0:
                        chunk_in(KV + k)
                    token_unit(hT3, i, cview(KV + k), DC, chunks[KV + k][1][1])
                    if i == k == 0:
                        to_features(xn3, 1, 6)

            def qk_transposes(i):
                pe.wait_ge(qk_ok, i + 1)
                for blocks in (range(4), range(4, 6)):
                    tr_bank()
                    for c in blocks:
                        mm = pe.transpose(ps[:, 4, (c % 4) * P:(c % 4 + 1) * P],
                                          QK4[:, i, 2 * c:2 * c + 2, :].rearrange("p h d -> p (h d)"), IDN)
                    mm.then_inc(tr_done, 1)

            def cmp_hidden(kv):
                chunk_in(CMP + kv)
                for j in range(16):
                    mm = pe.matmul(ps[0:32, 7, kv * 256:(kv + 1) * 256],
                                   X5[:, kv, j, :, :].rearrange("p g n -> p (g n)"),
                                   cview(CMP + kv)[:, j, :], start=j == 0, stop=j == 15)
                mm.then_inc(cp_h, 1)

            pe.wait_ge(cp_v, 2)
            for kv in range(2):
                for g in range(2):
                    for i in range(TI):
                        mm = pe.transpose(ps[:, 2 + kv, g * 256 + i * P:g * 256 + (i + 1) * P],
                                          kvd6[:, i, kv, g, :, :].rearrange("p a d -> p (a d)"), IDN)
            mm.then_inc(cp_T, 1)
            qk_transposes(0)
            pe.wait_ge(cp_X, 4)
            misc_bank()
            cmp_hidden(0)
            qk_transposes(1)

            def attn_scores(t_, a):
                h = t_
                g, m, lo = h // 4, h % 4, 64 * (h // 4)
                v = 2 * t_ + a
                if v >= 2:
                    pe.wait_ge(fx_m, 8 + v - 1)
                q, k = qkT3[lo:lo + 64, m, :], qkT3[lo:lo + 64, 4 + a, :]
                pe.matmul(ps[:, 2 + a, 0:P], q[:, 0:P], k[:, 0:P], start=True, stop=False, skip_group_check=True)
                pe.matmul(ps[:, 2 + a, P:384], q[:, P:T], k[:, 0:T], start=False, stop=True,
                          skip_group_check=True).then_inc(fx_z, 1)

            attn_tr = {}

            def attn_pv(t_, a):
                g = t_ // 4
                pe.wait_ge(tr_free, attn_tr[2 * t_ + a] + 1)
                pv(zb(PT, a), vS4[:, a, 0, g * HD:(g + 1) * HD], vS4[:, a, 1, g * HD:(g + 1) * HD], t_,
                   (0, 128, 256), t_ == 0 and a == 0).then_inc(fx_pv, 1)

            def attn_transposes(t_, a):
                attn_tr[2 * t_ + a] = trs[0]
                p_transposes(2 * t_ + a, a, fx_sc)

            pe.wait_ge(tr_free, trs[0])
            pe.wait_ge(ya_ok, 4)
            for w in range(10):
                if w == 1:
                    cmp_hidden(1)
                if 2 <= w < 8:
                    k, i = (w - 2) // 2, w % 2
                    if i == 0:
                        chunk_in(CONV + k)
                    token_unit(hT3, i, cview(CONV + k), DC)
                if w < 8:
                    attn_scores(w, 0)
                    attn_scores(w, 1)
                if 0 <= w - 2 < 8:
                    attn_pv(w - 2, 0)
                    attn_pv(w - 2, 1)
                if 0 <= w - 1 < 8:
                    attn_transposes(w - 1, 0)
                    attn_transposes(w - 1, 1)
                if w == 2:
                    pe.wait_ge(cp_H, 1)
                    tr_bank()
                    for c in range(4):
                        mm = pe.transpose(ps[:, 4, c * 32:(c + 1) * 32], Hh[0:32, c * P:(c + 1) * P],
                                          cst[0:32, C_ID:C_ID + 32])
                    mm.then_inc(tr_done, 1)
                    h_tr = trs[0]
                if w == 3:
                    pe.wait_ge(tr_free, h_tr)
                    for g in range(2):
                        for c in range(2):
                            pe.matmul(ps[0:16, 7, g * HD:(g + 1) * HD], HTk3[:, c, g * 16:(g + 1) * 16],
                                      w2c[:, c * HD:(c + 1) * HD], start=c == 0, stop=c == 1)
                    for g in range(2):
                        for c in range(2):
                            mm = pe.matmul(ps[:, 7, P + g * HD:P + (g + 1) * HD],
                                           HTv5[:, c, g, :, :].rearrange("p r n -> p (r n)"),
                                           w2c[:, (2 + c) * HD:(3 + c) * HD], start=c == 0, stop=c == 1)
                    mm.then_inc(cp_w2, 1)
                if w == 4:
                    pe.wait_ge(cp_k, 1)
                    tr_bank()
                    pe.transpose(ps[:, 4, 0:16], kc[0:16, :], cst[0:16, C_ID:C_ID + 16]).then_inc(tr_done, 1)
                    k_tr = trs[0]
                if w == 5:
                    pe.wait_ge(tr_free, k_tr)
                    for g in range(2):
                        lo = 64 * g
                        if g:
                            pe.wait_ge(cp_z, 1)
                        for i in range(TI):
                            for m in range(4):
                                o = (i * H + 4 * g + m) * 16
                                mm = pe.matmul(ps[:, 7, o:o + 16], qkT3[lo:lo + 64, m, i * P:(i + 1) * P],
                                               kcT[lo:lo + 64, :], start=True, stop=True)
                        mm.then_inc(cp_z, 1)
                if w == 7:
                    pe.wait_ge(cp_n, 1)
                    tr_bank()
                    for i in range(TI):
                        for g in range(2):
                            mm = pe.transpose(ps[:, 4, (2 * i + g) * P:(2 * i + g + 1) * P],
                                              Pc4[:, i, 4 * g:4 * g + 4, :].rearrange("p h n -> p (h n)"), IDN)
                    mm.then_inc(tr_done, 1)
                    c_tr = trs[0]
                if w == 9:
                    pe.wait_ge(tr_free, c_tr)
                    for i in range(TI):
                        for g in range(2):
                            mm = pe.matmul(ps[:, 5 + i, g * 256:(g + 1) * 256], PcT4[:, i, g, :], Vbd3[:, g, :],
                                           start=False, stop=False, skip_group_check=True)
                    mm.then_inc(cp_p, 1)
                if w == 9:
                    pe.wait_ge(cv_w, 4)
                    for i in range(TI):
                        b = unit_bank()
                        terms = [(C_S1, 1, i), (C_S2, 0, i)] + ([(C_S1C, 1, 0), (C_S2C, 0, 0)] if i else [])
                        for k, (o, wi, i2) in enumerate(terms):
                            mm = pe.matmul(ps[:, b, :], cc(o), cwp[wi][:, i2, :], start=k == 0,
                                           stop=k == len(terms) - 1)
                        mm.then_inc(unit_done[b], 1)
            to_features(xn3, 0, 7)
            for i in range(TI):
                pe.wait_ge(hta_done, 7 + i)
                pe.wait_ge(htv_done, 7 + i)
                for n in range(2):
                    if i == 0:
                        chunk_in(WO2 + n)
                    if i == n == 1:
                        to_features(xn3, 0, 9)
                    token_unit(hT3, i, cview(WO2 + n), DC)
                    if i == n == 0:
                        to_features(xn3, 1, 8)
            for i in range(TI):
                if i:
                    to_features(xn3, i, 9 + i)
                pe.wait_ge(hta_done, 9 + i)
                pe.wait_ge(htv_done, 9 + i)
                for c in range(DC):
                    mm = pe.matmul(ps[:, 7, i * 72:(i + 1) * 72], hT3[:, c, i * P:(i + 1) * P],
                                   wr[:, c * 72:(c + 1) * 72], start=c == 0, stop=c == DC - 1)
            mm.then_inc(r_lg, 1)
            pe.wait_ge(r_A, 1)
            A3 = rA.rearrange("p (i e) -> p i e", i=TI)
            pe.matmul(ps[:, 7, 0:64], cc(C_LT), A3[:, 0, :], start=True, stop=True)
            pe.matmul(ps[:, 7, 64:128], cc(C_ONE), A3[:, 0, :], start=True, stop=False)
            pe.matmul(ps[:, 7, 64:128], cc(C_LT), A3[:, 1, :], start=False, stop=True)
            pe.matmul(ps[0:64, 7, 128:129], A3[:, 0, :], cst[:, C_ONE:C_ONE + 1], start=True, stop=False)
            pe.matmul(ps[0:64, 7, 128:129], A3[:, 1, :], cst[:, C_ONE:C_ONE + 1], start=False,
                      stop=True).then_inc(r_rk, 1)
            pe.wait_ge(r_nb, 1)
            pe.matmul(ps[:, 4, 192:256], nb128[0:64, :], cst[0:64, C_LT:C_LT + 64], start=True, stop=True)
            pe.matmul(ps[:, 4, 256:257], nb128[0:64, :], cst[0:64, C_ONE:C_ONE + 1], start=True, stop=True)
            pe.matmul(ps[0:64, 4, 257:258], cst[0:64, C_LE:C_LE + 64], nb128[0:64, 0:1], start=True,
                      stop=True).then_inc(r_st, 1)
            pe.wait_ge(r_ci, 1)
            pe.matmul(ps[0:1, 5, 0:16], cst[0:64, C_ONE:C_ONE + 1], cmpi[0:64, 0:16], start=True,
                      stop=True).then_inc(r_it, 1)
            pe.wait_ge(ids_ok, 1)

            def round_(it):
                pe.wait_ge(m_sel, it + 1)
                for c in range(DC):
                    for i in range(TI):
                        mm = pe.matmul(ps[:, 4 + c // 4, (c % 4) * P:(c % 4 + 1) * P],
                                       xn3[:, i, c * P:(c + 1) * P], sel3[:, i, :], start=i == 0, stop=i == 1)
                mm.then_inc(m_d, 1)
                for i in range(TI):
                    mm = pe.transpose(ps[:, 6, i * P:(i + 1) * P], wsel3[:, i, :], IDN)
                mm.then_inc(m_wt, 1)
                pe.wait_ge(m_xe, it * 2 + 2)
                for s in range(8):
                    slot = s % MRING
                    pe.wait_ge(mring_in[slot], it * 128 + 64 * (1 + s // MRING))
                    wv = mringv(MSLOT[slot]).rearrange("p (e r n) -> p e r n", e=4, r=2)
                    for r in range(2):
                        c = 2 * (s // 2) + r
                        for e in range(ITEMS):
                            mm = pe.matmul(ps[32 * e:32 * e + 32, s % 2, :], xe3[:, c, 32 * e:32 * e + 32],
                                           wv[:, e, r, :], start=c == 0, stop=c == DC - 1, skip_group_check=True)
                    mm.then_inc(mring_free, 1)
                pe.wait_ge(m_a, it + 1)
                pe.wait_ge(m_wc, it + 1)
                for j in range(4):
                    mm = pe.transpose(ps[:, 6, j * P:(j + 1) * P], hA[:, j * P:(j + 1) * P], IDN)
                mm.then_inc(m_at, 1)
                pe.wait_ge(m_atc, it + 1)
                for s in range(8, STAGES):
                    slot = s % MRING
                    pe.wait_ge(mring_in[slot], it * 128 + 64 * (1 + s // MRING))
                    wv = mringv(MSLOT[slot]).rearrange("p (e n) -> p e n", e=4)
                    for n in range(2):
                        for e in range(ITEMS):
                            mm = pe.matmul(ps[32 * e:32 * e + 32, 2 + n, :], actT3[:, s - 8, 32 * e:32 * e + 32],
                                           wv[:, e, n * W5:(n + 1) * W5], start=s == 8, stop=s == STAGES - 1,
                                           skip_group_check=True)
                    mm.then_inc(mring_free, 1)
                pe.wait_ge(m_ye, it + 1)
                for k in range(4):
                    i, n = k // 2, k % 2
                    mm = pe.matmul(ps[:, (7, 6, 4, 5)[k], :], wc3[:, i, :], ye[:, n * W5:(n + 1) * W5],
                                   start=True, stop=True)
                mm.then_inc(m_cb, 1)
                pe.wait_ge(m_cbf, it + 1)

            with pe.Fori(0, MAIN) as it:
                round_(it)
            n_over = pe.value_load(ids[0:1, 16:17], min_val=0, max_val=16)
            with pe.If(n_over > 0):
                with pe.Fori(MAIN, ROUNDS) as it:
                    round_(it)

        @block.scalar
        def _(act):
            n_ch = [0]

            def link(ins):
                n_ch[0] += 1
                ins.then_inc(act_ch, 1)
                act.wait_ge(act_ch, n_ch[0])

            act.dma_start(rowsA[0:8, :], t["c"].rearrange("o (c p) -> (o c) p", p=P)).then_inc(ld_rowsA, 16)
            act.dma_start(rowsA[8:32, :], t["b_ada"].rearrange("o (c p) -> (o c) p", p=P)).then_inc(ld_rowsA, 16)
            act.dma_start(rowsA[32:40, :], t["norm_g"].rearrange("o (c p) -> (o c) p", p=P)).then_inc(ld_rowsA, 16)

            n_ms = [0]

            def squares(out_, src, width, acc_):
                act.activation(out_, src, ACT.Square, scale=width ** -0.5, accum_out=acc_).then_inc(ms_done, 1)
                n_ms[0] += 1

            def to_hT(a, i, k):
                act.wait_ge(xt_done, k)
                for c in range(4):
                    dst, src = hT3[:, c, i * P:(i + 1) * P], ps[:, (2, 5)[i], c * P:(c + 1) * P]
                    if a is None:
                        ins = act.copy(dst, src)
                    elif a[1] is None:
                        ins = act.activation(dst, src, ACT.Copy, scale=a[0][:, c:c + 1])
                    else:
                        ins = act.activation(dst, src, ACT.Identity, scale=a[0][:, c:c + 1], bias=a[1][:, c:c + 1])
                ins.then_inc(hta_done, 1)

            act.wait_ge(ld_x, 16)
            for i in range(TI):
                squares(xn3[:, i, :], x3[:, i, :], D, ssum[:, i:i + 1])
            act.wait_ge(ab_ok, 1)
            for i in range(TI):
                to_hT((ab[:, 0:8], ab[:, 8:16]), i, i + 1)
            act.wait_ge(colB_ok, 1)
            act.activation(colB[:, 120:128], colB[:, 0:8], ACT.Exp, scale=-1.0).then_inc(c2_e, 1)

            def unit_wait(u):
                act.wait_ge(unit_done[u % 2], u // 2 + 1)

            def unit_copy(u):
                q, half = u // 2, u % 2
                src = ps[:, u % 2, :]
                unit_wait(u)
                if q in (0, 4):
                    ins = act.copy(kT[q // 4][:, half * W5:(half + 1) * W5], src)
                elif q in (1, 5):
                    ins = act.mul(qT[q // 4][:, half * W5:(half + 1) * W5], src, QSCALE)
                else:
                    ins = act.copy(v3[q // 4][:, half, :], src)
                ins.then_inc(unit_free[u % 2], 1)

            def block_squares(i, n):
                act.wait_ge(x_ok, 2 * i + n + 1)
                if n_ms[0] > 2:
                    act.wait_ge(ms_done, n_ms[0])
                o = 4 + 4 * i + 2 * n
                squares(JA, x3[:, i, n * W5:(n + 1) * W5], D, ssum[:, o:o + 1])
                squares(JB, xn3[:, i, n * W5:(n + 1) * W5], D, ssum[:, o + 1:o + 2])

            def stick_soft(h):
                z = zb(zS, h % 2)
                act.wait_ge(st_zc, h + 1)
                link(act.activation(z, z, ACT.Exp))
                act.activation(z, z, ACT.Ln, bias=1.0).then_inc(st_ln, 1)

            def stick_weight(h):
                act.wait_ge(st_c, h + 1)
                if h >= 2:
                    act.wait_ge(st_pv, h - 1)
                act.activation(zb(Pb, h % 2), Z(h % 2), ACT.Exp).then_inc(st_w, 1)

            def soft_exp(k, b, pt_done):
                act.wait_ge(fx_m, k + 1)
                if pt_done is not None:
                    act.wait_ge(tr_done, pt_done)
                z, p = zb(zS, b), zb(Pb, b)
                act.activation(p[:, 0:P], z[:, 0:P], ACT.Exp, bias=MX[:, 16 + 2 * b:17 + 2 * b],
                               accum_out=SM[:, sm(k):sm(k) + 1])
                act.activation(p[:, P:384], z[:, P:384], ACT.Exp, bias=MX[:, 17 + 2 * b:18 + 2 * b],
                               accum_out=SM[:, sm(k) + 1:sm(k) + 2]).then_inc(fx_p, 1)

            def sm(k):
                return 2 * k if k < 8 else 16 + 2 * (k % 2)

            trs = [0]

            def p_copy(b, pv_need):
                act.wait_ge(tr_done, trs[0] + 1)
                if pv_need:
                    act.wait_ge(fx_pv, pv_need)
                act.copy(zb(PT, b), ps[:, 4, 0:384]).then_inc(tr_free, 1)
                trs[0] += 1

            fox_trd = {}
            for u in range(26):
                if u < 24:
                    q = u // 2
                    if q in (0, 1, 2, 4, 5, 6):
                        unit_copy(u)
                    elif q in (3, 7):
                        unit_wait(u)
                        act.activation(sz3[q // 4][:, u % 2, :], ps[:, u % 2, :], ACT.Exp, scale=-1.0).then_inc(e_sig, 1)
                    else:
                        act.wait_ge(unit_free[u % 2], u // 2 + 1)
                        gq = g3[:, u % 2, (q - 8) * W5:(q - 7) * W5]
                        act.activation(gq, gq, ACT.Exp, scale=-1.0).then_inc(e_sig, 1)
                if u == 0:
                    act.wait_ge(f_e, 1)
                    link(act.activation(fl[:, 32:48], fl[:, 32:48], ACT.Exp))
                    act.activation(fl[:, 32:48], fl[:, 32:48], ACT.Ln, bias=1.0).then_inc(f_l, 1)
                if 0 <= u - 4 < H:
                    stick_soft(u - 4)
                if 0 <= u - 5 < H:
                    stick_weight(u - 5)
                if u in (14, 15):
                    act.wait_ge(tr_done, trs[0] + 1)
                    act.copy(yT3[0][:, :, (u - 14) * P:(u - 13) * P],
                             ps[:, 4, :].rearrange("p (c t) -> p c t", c=4)).then_inc(tr_free, 1)
                    trs[0] += 1
                if 0 <= u - 14 < H:
                    k = u - 14
                    if k == 0:
                        act.wait_ge(st_pv, 8)
                    soft_exp(k, k % 2, fox_trd[k - 2] if k >= 2 else None)
                if 0 <= u - 15 < H:
                    k = u - 15
                    fox_trd[k] = trs[0] + 1
                    p_copy(k % 2, k - 1 if k >= 2 else 0)
            for i in range(TI):
                act.wait_ge(tr_done, trs[0] + 1)
                act.copy(yT3[1][:, :, i * P:(i + 1) * P],
                         ps[:, 4, :].rearrange("p (c t) -> p c t", c=4)).then_inc(tr_free, 1)
                trs[0] += 1
            for i in range(TI):
                to_hT(None, i, 3 + i)
            for n in range(2):
                block_squares(0, n)
            block_squares(1, 0)
            to_hT((ab[:, 16:24], ab[:, 24:32]), 0, 5)
            block_squares(1, 1)
            u0 = 36
            for i in range(TI):
                for k in range(3):
                    u = u0 + 3 * i + k
                    unit_wait(u)
                    src = ps[:, u % 2, :]
                    if k == 0:
                        s4 = src[:, 0:256].rearrange("p (kv g d) -> p kv g d", kv=2, g=2)
                        for a in range(2):
                            for kv in range(2):
                                act.copy(kvd6[:, i, kv, :, a, :], s4[:, kv, :, :])
                        act.copy(vS4[:, 0, i, :], src[:, 384:512]).then_inc(cp_v, 1)
                        act.copy(QK4[:, i, 8:10, :], src[:, 256:384].rearrange("p (h d) -> p h d", h=2)) \
                            .then_inc(unit_free[u % 2], 1)
                        if i == 0:
                            to_hT((ab[:, 16:24], ab[:, 24:32]), 1, 6)
                    elif k == 1:
                        act.copy(vS4[:, 1, i, :], src[:, 128:256])
                        act.copy(QK4[:, i, 10:12, :], src[:, 0:128].rearrange("p (h d) -> p h d", h=2))
                        act.activation(G3[:, i * 24:(i + 1) * 24], src[:, 256:280], ACT.Exp, scale=-1.0) \
                            .then_inc(unit_free[u % 2], 1)
                    else:
                        for g in range(2):
                            ins = act.copy(QK4[:, i, g:8:2, :],
                                           src[:, g * 256:(g + 1) * 256].rearrange("p (m d) -> p m d", m=4))
                        ins.then_inc(unit_free[u % 2], 1)
                        act.wait_ge(unit_free[u % 2], u // 2 + 1)
                        act.wait_ge(unit_free[(u - 1) % 2], (u - 1) // 2 + 1)
                        act.activation(xn3[:, i, 0:768], QK[:, i * 768:(i + 1) * 768], ACT.Square,
                                       scale=HD ** -0.5).then_inc(sq_ok, 1)

            def qk_copy(i):
                act.wait_ge(tr_done, trs[0] + 1)
                act.activation(qkT3[:, 0:4, i * P:(i + 1) * P], ps[:, 4, :].rearrange("p (c t) -> p c t", c=4),
                               ACT.Copy, scale=colB[:, 117:118]).then_inc(tr_free, 1)
                act.wait_ge(tr_done, trs[0] + 2)
                for c in range(2):
                    ins = act.activation(qkT3[:, 4 + c, i * P:(i + 1) * P], ps[:, 4, c * P:(c + 1) * P],
                                         ACT.Copy, scale=colB[:, 114 + c:115 + c])
                ins.then_inc(tr_free, 1)
                trs[0] += 2

            qk_copy(0)
            qk_copy(1)
            attn_trd = {}
            for w in range(10):
                if 2 <= w < 8:
                    k, i = (w - 2) // 2, w % 2
                    u = 42 + w - 2
                    if k < 2:
                        unit_wait(u)
                        act.copy((bgt3, cu3)[k][:, i, :], ps[:, u % 2, :]).then_inc(unit_free[u % 2], 1)
                if 0 <= w - 1 < 8:
                    for a in range(2):
                        v = 2 * (w - 1) + a
                        attn_trd[v] = trs[0] + 1
                        p_copy(a, 8 + v - 1)
                if w < 8:
                    for a in range(2):
                        soft_exp(8 + 2 * w + a, a, attn_trd.get(2 * (w - 1) + a))
                if w == 1:
                    act.wait_ge(cp_h, 2)
                    act.activation(HE[0:32, :], ps[0:32, 7, :], ACT.Exp, scale=-1.0).then_inc(cp_e, 1)
                if w == 2:
                    act.wait_ge(tr_done, trs[0] + 1)
                    act.wait_ge(pad_ok, 4)
                    for c in range(2):
                        act.copy(HTk3[:, c, :], ps[:, 4, c * 32:(c + 1) * 32])
                        for r in range(4):
                            ins = act.copy(HTv5[:, c, :, r, 0:16],
                                           ps[:, 4, (2 + c) * 32:(3 + c) * 32].rearrange("p (g n) -> p g n", g=2))
                    ins.then_inc(tr_free, 1)
                    trs[0] += 1
                if w == 4:
                    act.wait_ge(tr_done, trs[0] + 1)
                    act.activation(kcT, ps[:, 4, 0:16], ACT.Copy, scale=colB[:, 113:114]).then_inc(tr_free, 1)
                    trs[0] += 1
                if w == 5:
                    act.wait_ge(cp_s, 1)
                    act.activation(Pc4[:, :, :, 0:16], Sc4, ACT.Exp).then_inc(cp_x, 1)
                if w == 7:
                    act.wait_ge(tr_done, trs[0] + 1)
                    act.copy(PcT, ps[:, 4, :]).then_inc(tr_free, 1)
                    trs[0] += 1
            for i in range(TI):
                act.wait_ge(att_ok, 2 + i + 1)
                act.activation(hT[:, i * D:(i + 1) * D], xn3[:, i, :], ACT.Square,
                               scale=HD ** -0.5).then_inc(sq_ok, 1)
            for i in range(TI):
                to_hT((colB[:, 72:80], None), i, 7 + i)
            for i in range(TI):
                for n in range(2):
                    act.wait_ge(x_ok, 4 + 2 * i + n + 1)
                    act.wait_ge(ms_done, n_ms[0])
                    squares(JA, x3[:, i, n * W5:(n + 1) * W5], D, ssum[:, 12 + 2 * i + n:13 + 2 * i + n])
                    if i == 1 and n == 0:
                        to_hT((ab[:, 32:40], ab[:, 40:48]), 0, 9)
            to_hT((ab[:, 32:40], ab[:, 40:48]), 1, 10)
            act.wait_ge(r_s, 1)
            act.activation(rG[:, 0:16], rG[:, 0:16], ACT.Exp).then_inc(r_e, 1)
            act.wait_ge(r_s, 2)
            act.activation(rt[:, 8:10], rt[:, 6:8], ACT.Exp).then_inc(r_e, 1)
            act.wait_ge(ids_ok, 1)

            def round_(it):
                act.wait_ge(m_d, it + 1)
                for c in range(4):
                    ins = act.activation(xe3[:, c, :], ps[:, 4, c * P:(c + 1) * P], ACT.Identity,
                                   scale=ab[:, 32 + c:33 + c], bias=ab[:, 40 + c:41 + c])
                ins.then_inc(m_xe, 1)
                act.wait_ge(mring_free, it * STAGES + 8)
                act.activation(hE, ps[:, 0, :], ACT.Exp, scale=-1.0).then_inc(m_e, 1)
                act.wait_ge(m_at, it + 1)
                act.copy(actT, ps[:, 6, :]).then_inc(m_atc, 1)
                act.wait_ge(mring_free, it * STAGES + STAGES)
                act.copy(ye, ps[:, 2:4, :].rearrange("p a b -> p (a b)")).then_inc(m_ye, 1)

            with act.Fori(0, MAIN) as it:
                round_(it)
            n_over = act.value_load(ids[0:1, 16:17], min_val=0, max_val=16)
            with act.If(n_over > 0):
                with act.Fori(MAIN, ROUNDS) as it:
                    round_(it)

        @block.vector
        def _(dve):
            n_ch = [0]

            def link(ins):
                n_ch[0] += 1
                ins.then_inc(dve_ch, 1)
                dve.wait_ge(dve_ch, n_ch[0])

            def bc(ap, n):
                return bass.AP(tensor=ap.tensor, offset=ap.offset, ap=list(ap.ap) + [[0, n]])

            norm_k = [0]

            def root(mean, scale=1.0):
                (w, parts), o = NRM[norm_k[0]], NO[norm_k[0]]
                norm_k[0] += 1
                v, r, tm = (a[0:parts, o:o + w] for a in (VA, RS, TM))
                if mean is not None:
                    link(dve.tensor_scalar(v, mean, scale, EPS, ALU.mult, ALU.add))
                link(dve.tensor_scalar(tm.bitcast(I32), v.bitcast(I32), 1, None, ALU.logical_shift_right))
                link(dve.tensor_scalar(r.bitcast(I32), tm.bitcast(I32), -1.0, float(0x5f3759df), ALU.mult, ALU.add))
                for _ in range(3):
                    link(dve.scalar_tensor_tensor(tm, r, -0.5, r, ALU.mult, ALU.mult))
                    link(dve.tensor_tensor(tm, tm, v, ALU.mult))
                    link(dve.scalar_tensor_tensor(r, tm, 1.5, r, ALU.add, ALU.mult))
                return r

            def to_hT(a, i, k):
                dve.wait_ge(xt_done, k)
                for c in range(4, DC):
                    dst, src = hT3[:, c, i * P:(i + 1) * P], ps[:, (3, 6)[i], (c - 4) * P:(c - 3) * P]
                    if a is None:
                        ins = dve.tensor_copy(dst, src)
                    elif a[1] is None:
                        ins = dve.tensor_scalar(dst, src, a[0][:, c:c + 1], None, ALU.mult)
                    else:
                        ins = dve.tensor_scalar(dst, src, a[0][:, c:c + 1], a[1][:, c:c + 1], ALU.mult, ALU.add)
                ins.then_inc(htv_done, 1)

            dve.wait_ge(cols_tr, 1)
            link(dve.tensor_copy(colA[:], ps[:, 7, 0:40]))
            dve.tensor_copy(c32[:, 0:256].rearrange("p (c n) -> p c n", c=DC), bc(colA[:, 0:8], 32)).then_inc(c1_ok, 1)
            dve.wait_ge(ms_done, 2)
            r = root(ssum[:, 0:2])
            for i in range(TI):
                dve.tensor_scalar(xn3[:, i, :], x3[:, i, :], r[:, i:i + 1], None, ALU.mult).then_inc(xn_done, 1)
            for n in range(4):
                if n == 3:
                    dve.wait_ge(cols_tr, 2)
                    dve.tensor_copy(colB[:, 0:116], ps[:, 7, 0:116]).then_inc(colB_ok, 1)
                dve.wait_ge(mod_raw, n + 1)
                if n:
                    dve.wait_ge(ab_done, n)
                dve.tensor_copy(modt[:], ps[:, 4, :]).then_inc(mod_ok, 1)
            dve.wait_ge(ab_done, 4)
            dve.tensor_tensor(ab[:, 8:16], ps[:, 0, 0:8], colA[:, 8:16], ALU.add)
            link(dve.tensor_tensor(ab[:, 0:8], ps[:, 0, 8:16], colA[:, 16:24], ALU.add))
            dve.scalar_tensor_tensor(ab[:, 0:8], ab[:, 0:8], 1.0, colA[:, 32:40], ALU.add, ALU.mult).then_inc(ab_ok, 1)
            dve.wait_ge(ab_ok, 1)
            for i in range(TI):
                to_hT((ab[:, 0:8], ab[:, 8:16]), i, i + 1)
            dve.wait_ge(colB_ok, 1)
            dve.tensor_scalar(colB[:, 117:118], colB[:, 112:113], QSCALE, None, ALU.mult)
            dve.wait_ge(c2_e, 1)
            link(dve.tensor_scalar(colB[:, 120:128], colB[:, 120:128], 1.0, None, ALU.add))
            link(dve.reciprocal(colB[:, 120:128], colB[:, 120:128]))
            link(dve.tensor_tensor(colB[:, 120:128], colB[:, 120:128], colB[:, 0:8], ALU.mult))
            dve.tensor_copy(c32[:, 256:512].rearrange("p (c n) -> p c n", c=DC), bc(colB[:, 120:128], 32)) \
                .then_inc(c2_ok, 1)

            def unit_wait(u):
                dve.wait_ge(unit_done[u % 2], u // 2 + 1)

            def sigmoid_tail(e):
                link(dve.tensor_scalar(e, e, 1.0, None, ALU.add))
                link(dve.reciprocal(e, e))

            def stick_log(h):
                b = h % 2
                dve.wait_ge(st_z, h + 1)
                if h >= 1:
                    dve.wait_ge(st_L, h)
                dve.tensor_scalar(zb(zS, b), Z(b), 40.0, None, ALU.min).then_inc(st_zc, 1)
                link(dve.tensor_scalar(R[:], Z(b), 40.0, -40.0, ALU.max, ALU.add))
                dve.wait_ge(st_ln, h + 1)
                if h >= 2:
                    dve.wait_ge(st_c, h - 1)
                dve.scalar_tensor_tensor(zb(PT, b), zb(zS, b), -1.0, R[:], ALU.mult, ALU.subtract).then_inc(st_L, 1)

            def row_max(k, b, bias0, bias1):
                dve.wait_ge(fx_z, k + 1)
                if k >= 2:
                    dve.wait_ge(fx_p, k - 1)
                z = zb(zS, b)
                dve.tensor_tensor_reduce(z[:, 0:P], ps[:, 2 + b, 0:P], bias0, 1.0, -3e38, ALU.add, ALU.max,
                                         MX[:, 2 * b:2 * b + 1])
                link(dve.tensor_tensor_reduce(z[:, P:384], ps[:, 2 + b, P:384], bias1, 1.0, -3e38, ALU.add, ALU.max,
                                              MX[:, 2 * b + 1:2 * b + 2]))
                dve.tensor_scalar(MX[:, 16 + 2 * b:18 + 2 * b], MX[:, 2 * b:2 * b + 2], -1.0, None, ALU.mult) \
                    .then_inc(fx_m, 1)

            def mod2_raw():
                dve.wait_ge(misc_done, misc[0] + 1)
                dve.tensor_copy(modt[:], ps[:, 7, :]).then_inc(misc_free, 1)
                misc[0] += 1

            def mod_row(o):
                dve.wait_ge(misc_done, misc[0] + 1)
                dve.tensor_tensor(grow[:, o:o + W5], grow[:, o:o + W5], ps[:, 7, :], ALU.add).then_inc(misc_free, 1)
                misc[0] += 1

            misc = [0]
            for u in range(26):
                q = u // 2
                if u == 0:
                    dve.wait_ge(misc_done, 1)
                    dve.wait_ge(ld_small, 16 * 8)
                    f2 = fl[:, 0:16].rearrange("p (i h) -> p i h", i=2)
                    b2 = bass.AP(tensor=bfr[:].tensor, offset=bfr[:].offset, ap=[bfr[:].ap[0], [0, 2], [1, 8]])
                    dve.tensor_tensor(f2, ps[:, 7, 0:16].rearrange("p (i h) -> p i h", i=2), b2,
                                      ALU.add).then_inc(misc_free, 1)
                    misc[0] += 1
                    dve.wait_ge(misc_free, 1)
                    link(dve.tensor_scalar(fl[:, 16:32], fl[:, 0:16], -1.0, None, ALU.mult))
                    dve.tensor_tensor(fl[:, 32:48], fl[:, 0:16], fl[:, 16:32], ALU.min).then_inc(f_e, 1)
                    dve.wait_ge(f_l, 1)
                    dve.scalar_tensor_tensor(fl[:, 48:64], fl[:, 0:16], 0.0, fl[:, 32:48], ALU.min,
                                             ALU.subtract).then_inc(f_lf, 1)
                if 16 <= u < 24:
                    unit_wait(u)
                    if u == 16:
                        dve.wait_ge(ld_bg, 32)
                    gq = g3[:, u % 2, (q - 8) * W5:(q - 7) * W5]
                    dve.tensor_tensor(gq, ps[:, u % 2, :], bg[:, (q - 8) * W5:(q - 7) * W5],
                                      ALU.add).then_inc(unit_free[u % 2], 1)
                if u % 2 == 0 and 2 <= u <= 24:
                    k = u // 2 - 1
                    if k == 4:
                        dve.wait_ge(ld_grow, 48)
                    if k in (4, 5):
                        mod_row(D + (k - 4) * W5)
                    elif k in (10, 11):
                        mod_row(2 * D + (k - 10) * W5)
                    else:
                        dve.wait_ge(misc_done, misc[0] + 1)
                        dve.tensor_tensor(mod2c[:, 4 * k:4 * k + 4], ps[:, 7, 0:4], colB[:, 8 + 4 * k:12 + 4 * k],
                                          ALU.add).then_inc(misc_free, 1)
                        misc[0] += 1
                if 0 <= u - 4 < H:
                    stick_log(u - 4)
                if 0 <= u - 14 < H:
                    row_max(u - 14, u % 2, cst[:, C_NM + P:C_NM + 256], cst[:, C_NM:C_NM + 256])
                if u in (6, 7, 14, 15):
                    s = sz3[q // 4][:, u % 2, :]
                    dve.wait_ge(e_sig, (u - 5) if u < 8 else (u - 11))
                    sigmoid_tail(s)
                    dve.tensor_tensor(s, s, ps[:, u % 2, :], ALU.mult).then_inc(unit_free[u % 2], 1)
                if 16 <= u < 24:
                    dve.wait_ge(e_sig, u - 11)
                    sigmoid_tail(g3[:, u % 2, (q - 8) * W5:(q - 7) * W5])
                if u == 13:
                    dve.wait_ge(st_pv, 8)
                    dve.wait_ge(unit_free[0], 4)
                    dve.wait_ge(unit_free[1], 4)
                    for i in range(TI):
                        dve.tensor_tensor(sz3[0][:, i, :], sz3[0][:, i, :], ps[:, 5 + i, :], ALU.mult).then_inc(ya_ok, 1)
                if u == 23:
                    dve.wait_ge(fx_pv, 8)
                    dve.wait_ge(unit_free[0], 8)
                    dve.wait_ge(unit_free[1], 8)
                    link(dve.reciprocal(CO[:, 0:16], SM[:, 0:16]))
                    for i in range(TI):
                        s = sz3[1][:, i, :]
                        link(dve.tensor_tensor(s, s, ps[:, 5 + i, :], ALU.mult))
                        s8 = s.rearrange("p (h d) -> p h d", h=H)
                        dve.tensor_tensor(s8, s8, bc(CO[:, i:16:2], HD), ALU.mult).then_inc(ya_ok, 1)
                if u % 2 == 1 and u < 24:
                    mod2_raw()
            for o, sh, sc, g in ((16, 0, 8, 56), (32, 24, 32, 64)):
                dve.tensor_copy(ab[:, o + 8:o + 16], mod2c[:, sh:sh + 8])
                link(dve.scalar_tensor_tensor(ab[:, o:o + 8], mod2c[:, sc:sc + 8], 1.0, colB[:, g:g + 8],
                                              ALU.add, ALU.mult))
            tmp = zS[:, 0:W5]
            for b in range(2):
                for i in range(TI):
                    for n in range(2):
                        u = 24 + 4 * b + 2 * i + n
                        if b == 0:
                            if n == 0:
                                mod2_raw()
                            else:
                                mod_row(i * W5)
                        unit_wait(u)
                        if u == 28:
                            dve.wait_ge(misc_done, 30)
                            dve.tensor_copy(bR[:, 0:W5], ps[0:8, 7, :]).then_inc(misc_free, 1)
                        if u == 29:
                            dve.wait_ge(misc_done, 31)
                            dve.tensor_copy(bR[:, W5:BM], ps[0:8, 7, 0:BM - W5]).then_inc(misc_free, 1)
                        g = g3[:, i, b * D + n * W5:b * D + (n + 1) * W5]
                        m = mg3[:, i, n * W5:(n + 1) * W5]
                        if b == 0:
                            dve.tensor_tensor(m, g, ps[:, u % 2, :], ALU.mult).then_inc(unit_free[u % 2], 1)
                        else:
                            dve.tensor_tensor(tmp, g, ps[:, u % 2, :], ALU.mult).then_inc(unit_free[u % 2], 1)
                            dve.wait_ge(unit_free[u % 2], u // 2 + 1)
                            ins = dve.tensor_tensor(m, m, tmp, ALU.add)
                            if n == 1:
                                ins.then_inc(xn_done, 1)
                                dve.wait_ge(xn_done, 3 + i)
                            else:
                                link(ins)
                            if i == 1 and n == 0:
                                to_hT(None, 0, 3)

            def residual(u, o, i, n, done):
                unit_wait(u)
                dve.tensor_tensor(tmp, grow[:, o + n * W5:o + (n + 1) * W5], ps[:, u % 2, :],
                                  ALU.mult).then_inc(unit_free[u % 2], 1)
                dve.wait_ge(unit_free[u % 2], u // 2 + 1)
                xs = x3[:, i, n * W5:(n + 1) * W5]
                ins = dve.tensor_tensor(xs, xs, tmp, ALU.add)
                if done:
                    ins.then_inc(x_ok, 1)
                else:
                    link(ins)

            for i in range(TI):
                for n in range(2):
                    residual(32 + 2 * i + n, 0, i, n, False)
                    xs = x3[:, i, n * W5:(n + 1) * W5]
                    dve.tensor_tensor(xn3[:, i, n * W5:(n + 1) * W5], xs, fg[:, n * W5:(n + 1) * W5],
                                      ALU.mult).then_inc(x_ok, 1)
                    if i == n == 0:
                        to_hT(None, 1, 4)
                    if i == 1 and n == 0:
                        to_hT((ab[:, 16:24], ab[:, 24:32]), 0, 5)
                k, o = norm_k[0], NO[norm_k[0]]
                dve.wait_ge(ms_done, 2 + 4 * i + 4)
                q = 4 + 4 * i
                link(dve.tensor_tensor(MS[:, o:o + 2], ssum[:, q:q + 2], ssum[:, q + 2:q + 4], ALU.add))
                link(dve.tensor_scalar(VA[:, o:o + 1], MS[:, o:o + 1], EPS, None, ALU.add))
                link(dve.reciprocal(TM[:, o:o + 1], VA[:, o:o + 1]))
                link(dve.tensor_tensor(TM[:, o + 1:o + 2], MS[:, o + 1:o + 2], TM[:, o:o + 1], ALU.mult))
                link(dve.tensor_scalar(VA[:, o + 1:o + 2], TM[:, o + 1:o + 2], EPS, None, ALU.add))
                r = root(None)
                link(dve.tensor_scalar(x3[:, i, :], xn3[:, i, :], r[:, 0:1], None, ALU.mult))
                dve.tensor_scalar(xn3[:, i, :], x3[:, i, :], r[:, 1:2], None, ALU.mult).then_inc(xn_done, 1)
            to_hT((ab[:, 16:24], ab[:, 24:32]), 1, 6)

            def qk_norm(i):
                dve.wait_ge(sq_ok, i + 1)
                o = NO[norm_k[0]]
                link(dve.tensor_reduce(MS[:, o:o + 12], xn3[:, i, 0:768].rearrange("p (h d) -> p h d", d=HD), AX, ALU.add))
                r = root(MS[:, o:o + 12])
                dve.tensor_tensor(QK4[:, i], QK4[:, i], bc(r, HD), ALU.mult).then_inc(qk_ok, 1)

            qk_norm(0)
            dve.wait_ge(pad_ok, 1)
            dve.wait_ge(cp_T, 1)
            for kv in range(2):
                for a in range(2):
                    lo = 64 * a
                    src = ps[lo:lo + 64, 2 + kv, :]
                    pstep = src.ap[0]
                    t_in = bass.AP(tensor=src.tensor, offset=src.offset + a, ap=[pstep, [2, 16], [256, 2], [16, NCMP]])
                    pos = colB[lo:lo + 64, 80 + 16 * kv:96 + 16 * kv]
                    p_in = bass.AP(tensor=pos.tensor, offset=pos.offset, ap=[pos.ap[0], [1, 16], [0, 2], [0, NCMP]])
                    dve.tensor_tensor(X5[lo:lo + 64, kv, :, :, 0:NCMP], t_in, p_in, ALU.add).then_inc(cp_X, 1)
            qk_norm(1)
            dve.wait_ge(unit_free[0], 21)
            sigmoid_tail(G3)
            dve.wait_ge(ld_bias, 16)
            for w in range(10):
                if w in (6, 7):
                    u, i = 40 + w, w % 2
                    unit_wait(u)
                    dve.wait_ge(unit_free[u % 2], u // 2)
                    dve.tensor_tensor(cu3[:, i, :], cu3[:, i, :], ps[:, u % 2, :], ALU.mult).then_inc(unit_free[u % 2], 1)
                if w < 8:
                    for a in range(2):
                        row_max(8 + 2 * w + a, a, B[:, w, P:256], B[:, w, 0:256])
                    for a in range(2):
                        k = 8 + 2 * w + a
                        dve.wait_ge(fx_p, k + 1)
                        c2 = CO[:, 2 * a:2 * a + 2]
                        link(dve.reciprocal(c2, SM[:, 16 + 2 * a:18 + 2 * a]))
                        link(dve.tensor_tensor(c2, c2, G34[:, :, w, 1 + a], ALU.mult))
                        p_ = zb(Pb, a)
                        dve.tensor_scalar(p_[:, 0:P], p_[:, 0:P], c2[:, 0:1], None, ALU.mult)
                        dve.tensor_scalar(p_[:, P:384], p_[:, P:384], c2[:, 1:2], None, ALU.mult).then_inc(fx_sc, 1)
                if w == 1:
                    dve.wait_ge(cp_e, 1)
                    he = HE[0:32, :]
                    sigmoid_tail(he)
                    dve.tensor_tensor(Hh[0:32, :], he, ps[0:32, 7, :], ALU.mult).then_inc(cp_H, 1)
                if w == 3:
                    dve.wait_ge(cp_w2, 1)
                    dve.wait_ge(pad_ok, 4)
                    for r in range(4):
                        dve.tensor_copy(Vbd3[32 * r:32 * r + 32, :, r * HD:(r + 1) * HD],
                                        ps[32 * r:32 * r + 32, 7, P:256].rearrange("p (g d) -> p g d", g=2))
                    link(dve.tensor_copy(kc[0:16, :], ps[0:16, 7, 0:P]))
                    link(dve.tensor_tensor(HE[0:16, 0:P], kc[0:16, :], kc[0:16, :], ALU.mult))
                    o = NO[norm_k[0]]
                    link(dve.tensor_reduce(MS[0:16, o:o + 2], HE[0:16, 0:P].rearrange("p (g d) -> p g d", g=2), AX, ALU.add))
                    r = root(MS[0:16, o:o + 2], 1.0 / HD)
                    k3 = kc[0:16, :].rearrange("p (g d) -> p g d", g=2)
                    dve.tensor_tensor(k3, k3, bc(r, HD), ALU.mult).then_inc(cp_k, 1)
                if w == 5:
                    dve.wait_ge(cp_z, 2)
                    for i in range(TI):
                        f0 = 31 + P * (1 - i)
                        ins = dve.tensor_tensor(Sc4[:, i, :, :],
                                                ps[:, 7, i * P:(i + 1) * P].rearrange("p (h n) -> p h n", h=H),
                                                B[:, :, f0:f0 + 241:16], ALU.add)
                    link(ins)
                    Sf = Sc.rearrange("p (h n) -> p h n", n=16)
                    link(dve.tensor_reduce(cm[:, 0:16], Sf, AX, ALU.max))
                    link(dve.tensor_scalar(cm[:, 0:16], cm[:, 0:16], -1e20, None, ALU.max))
                    dve.tensor_tensor(Sf, Sf, bc(cm[:, 0:16], 16), ALU.subtract).then_inc(cp_s, 1)
                if w == 6:
                    dve.wait_ge(cp_x, 1)
                    c16 = cm[:, 16:32]
                    Pf = Pc.rearrange("p (h n) -> p h n", n=32)[:, :, 0:16]
                    link(dve.tensor_reduce(c16, Pf, AX, ALU.add))
                    link(dve.tensor_scalar(c16, c16, 1e-30, None, ALU.max))
                    link(dve.reciprocal(c16, c16))
                    link(dve.tensor_tensor(c16, c16, G3[:, 0:48:3], ALU.mult))
                    dve.tensor_tensor(Pf, Pf, bc(c16, 16), ALU.mult).then_inc(cp_n, 1)
            for i in range(TI):
                u = 48 + i
                unit_wait(u)
                dve.wait_ge(cv_w2, i + 1)
                yc = xn3[:, i, W5:D]
                dve.tensor_tensor(yc, ps[:, u % 2, :], cwp[2][:, i, :], ALU.add).then_inc(unit_free[u % 2], 1)
                dve.wait_ge(unit_free[u % 2], u // 2 + 1)
                dve.tensor_tensor(yc, yc, bgt3[:, i, :], ALU.mult).then_inc(att_ok, 1)
            dve.wait_ge(cp_p, 1)
            for i in range(TI):
                dve.tensor_copy(xn3[:, i, 0:W5], ps[:, 5 + i, :]).then_inc(att_ok, 1)
            for i in range(TI):
                dve.wait_ge(sq_ok, 3 + i)
                o = NO[norm_k[0]]
                link(dve.tensor_reduce(MS[:, o:o + 16], hT[:, i * D:(i + 1) * D].rearrange("p (h d) -> p h d", d=HD),
                                       AX, ALU.add))
                r = root(MS[:, o:o + 16])
                xf = xn3[:, i, :].rearrange("p (h d) -> p h d", d=HD)
                dve.tensor_tensor(xf, xf, bc(r, HD), ALU.mult).then_inc(xn_done, 1)
            for i in range(TI):
                to_hT((colB[:, 72:80], None), i, 7 + i)
            for i in range(TI):
                for n in range(2):
                    residual(50 + 2 * i + n, D, i, n, True)
                    dve.wait_ge(x_ok, 4 + 2 * i + n + 1)
                    if i == 1 and n == 0:
                        to_hT((ab[:, 32:40], ab[:, 40:48]), 0, 9)
                dve.wait_ge(ms_done, 10 + 2 * i + 2)
                o = NO[norm_k[0]]
                q = 12 + 2 * i
                link(dve.tensor_tensor(MS[:, o:o + 1], ssum[:, q:q + 1], ssum[:, q + 1:q + 2], ALU.add))
                r = root(MS[:, o:o + 1])
                dve.tensor_scalar(xn3[:, i, :], x3[:, i, :], r, None, ALU.mult).then_inc(xn_done, 1)
            to_hT((ab[:, 32:40], ab[:, 40:48]), 1, 10)
            L3 = rL.rearrange("p (i n) -> p i n", i=2)
            E3 = rE.rearrange("p (i e) -> p i e", i=2)
            E4 = rE.rearrange("p (i g e) -> p i g e", i=2, g=8)
            O1 = rO1.rearrange("p (i e) -> p i e", i=2)
            O2 = rO2.rearrange("p (i e) -> p i e", i=2)
            P3 = rP.rearrange("p (i e) -> p i e", i=2)
            G2 = rG[:, 0:16].rearrange("p (i g) -> p i g", i=2)
            OG = rG[:, 16:32].rearrange("p (i g) -> p i g", i=2)
            PG = rG[:, 32:48].rearrange("p (i g) -> p i g", i=2)
            T3 = rT.rearrange("p (i e) -> p i e", i=2)

            def rb(ap, n):
                return bass.AP(tensor=ap.tensor, offset=ap.offset, ap=[ap.ap[0], [0, 2], [1, n]])

            def first_max(dst3, src3, desc, n, mx, scratch3):
                link(dve.tensor_reduce(mx, src3, AX, ALU.max))
                link(dve.tensor_tensor(scratch3, src3, bc(mx, n), ALU.is_equal))
                link(dve.tensor_tensor(scratch3, scratch3, rb(desc, n), ALU.mult))
                link(dve.tensor_reduce(rt[:, 30:32], scratch3, AX, ALU.max))
                link(dve.tensor_tensor(dst3, scratch3, bc(rt[:, 30:32], n), ALU.is_equal))

            dve.wait_ge(r_lg, 1)
            link(dve.tensor_tensor(L3, ps[:, 7, 0:144].rearrange("p (i n) -> p i n", i=2), rb(br[:, 0:72], 72), ALU.add))
            first_max(OG, L3[:, :, 0:8], cst[:, C_D8:C_D8 + 8], 8, rt[:, 0:2], PG)
            dve.tensor_tensor(G2, L3[:, :, 0:8], bc(rt[:, 0:2], 8), ALU.subtract).then_inc(r_s, 1)
            link(dve.tensor_scalar(PG, OG, -NEG, NEG, ALU.mult, ALU.add))
            for i in range(TI):
                e3 = L3[:, i, 8:72].rearrange("p (g e) -> p g e", g=8)
                link(dve.tensor_tensor(E4[:, i], e3, bc(OG[:, i, :], 8), ALU.mult))
                link(dve.tensor_tensor(E4[:, i], E4[:, i], bc(PG[:, i, :], 8), ALU.add))
            first_max(O1, E3, cst[:, C_D64:C_D64 + 64], 64, rt[:, 2:4], T3)
            link(dve.scalar_tensor_tensor(rE, rO1, -3e30, rE, ALU.mult, ALU.add))
            first_max(O2, E3, cst[:, C_D64:C_D64 + 64], 64, rt[:, 4:6], T3)
            dve.tensor_tensor(rA, rO1, rO2, ALU.add).then_inc(r_A, 1)
            dve.tensor_tensor(rt[:, 6:8], rt[:, 4:6], rt[:, 2:4], ALU.subtract).then_inc(r_s, 1)
            dve.wait_ge(r_e, 2)
            link(dve.tensor_reduce(rt[:, 10:12], G2, AX, ALU.add))
            link(dve.tensor_scalar(rt[:, 12:14], rt[:, 8:10], 1.0, None, ALU.add))
            link(dve.tensor_tensor(rt[:, 10:12], rt[:, 10:12], rt[:, 12:14], ALU.mult))
            link(dve.reciprocal(rt[:, 14:16], rt[:, 10:12]))
            link(dve.tensor_tensor(rt[:, 16:18], rt[:, 14:16], rt[:, 8:10], ALU.mult))
            dve.wait_ge(r_rk, 1)
            link(dve.tensor_copy(rt[0:64, 20:21], ps[0:64, 7, 128:129]))
            link(dve.tensor_scalar(rt[0:64, 22:30], cst[0:64, C_THR:C_THR + 8], rt[0:64, 20:21], None, ALU.is_lt))
            link(dve.tensor_reduce(rt[0:64, 21:22], rt[0:64, 22:30], AX, ALU.add))
            dve.tensor_scalar(nb128[0:64, :], cst[0:64, C_ONE:C_ONE + P], rt[0:64, 21:22], None, ALU.mult).then_inc(r_nb, 1)
            link(dve.tensor_copy(rP, ps[:, 7, 0:128]))
            dve.wait_ge(r_st, 1)
            e32 = T3[:, 0, :]
            link(dve.tensor_scalar(e32, cst[:, C_D64:C_D64 + 64], -float(SLOTS), float(SLOTS * NE), ALU.mult, ALU.add))
            link(dve.scalar_tensor_tensor(T3[:, 1, :], ps[:, 4, 192:256], float(SLOTS), e32, ALU.mult, ALU.subtract))
            link(dve.tensor_scalar(T3[:, 1, :], T3[:, 1, :], float(SLOTS * (NE - 1)), None, ALU.add))
            link(dve.tensor_copy(rt[0:64, 20:21], ps[0:64, 4, 257:258]))
            dve.tensor_scalar(cmpi[0:64, 0:16], cst[0:64, C_IOTA:C_IOTA + 16], rt[0:64, 20:21], None,
                              ALU.is_ge).then_inc(r_ci, 1)
            link(dve.tensor_scalar(rE, rP, float(SLOTS), None, ALU.is_ge))
            link(dve.tensor_tensor(E3, E3, rb(T3[:, 1, :], 64), ALU.mult))
            link(dve.tensor_tensor(rP, rP, rE, ALU.add))
            link(dve.tensor_tensor(P3, P3, rb(e32, 64), ALU.add))
            for o, dst in ((rO1, rQ[:, 0:2]), (rO2, rQ[:, 2:4])):
                link(dve.tensor_tensor(rE, o, rP, ALU.mult))
                link(dve.tensor_reduce(dst, E3, AX, ALU.add))
            link(dve.memset(acc, 0.0))
            dve.wait_ge(r_it, 1)
            link(dve.tensor_scalar(ids[0:1, 0:16], ps[0:1, 5, 0:16], float(NE - 1), None, ALU.min))
            dve.tensor_copy(ids[0:1, 16:17], ps[0:1, 4, 256:257]).then_inc(ids_ok, 1)

            LINKS = 13

            def round_(it):
                j = [0]

                def link_(ins):
                    j[0] += 1
                    ins.then_inc(m_ch, 1)
                    dve.wait_ge(m_ch, it * LINKS + j[0])

                iota = cc(C_IOTA)
                for i in range(TI):
                    p1, p2 = rQ[:, i:i + 1], rQ[:, 2 + i:3 + i]
                    s_, w_ = sel3[:, i, :], wsel3[:, i, :]
                    dve.tensor_scalar(s_, iota, p1, None, ALU.is_equal)
                    dve.tensor_scalar(w_, iota, p1, rt[:, 14 + i:15 + i], ALU.is_equal, ALU.mult)
                    link_(dve.tensor_scalar(rT, iota, p2, rt[:, 16 + i:17 + i], ALU.is_equal, ALU.mult))
                    link_(dve.scalar_tensor_tensor(s_, iota, p2, s_, ALU.is_equal, ALU.add))
                    ins = dve.tensor_tensor(w_, w_, rT, ALU.add)
                    if i == 0:
                        link_(ins)
                    else:
                        ins.then_inc(m_sel, 1)
                dve.wait_ge(m_d, it + 1)
                for c in range(4, DC):
                    ins = dve.tensor_scalar(xe3[:, c, :], ps[:, 5, (c - 4) * P:(c - 3) * P], ab[:, 32 + c:33 + c],
                                            ab[:, 40 + c:41 + c], ALU.mult, ALU.add)
                ins.then_inc(m_xe, 1)
                dve.wait_ge(m_wt, it + 1)
                dve.tensor_copy(wc, ps[:, 6, 0:256]).then_inc(m_wc, 1)
                dve.wait_ge(m_e, it + 1)
                link_(dve.tensor_scalar(hE, hE, 1.0, None, ALU.add))
                link_(dve.reciprocal(hE, hE))
                link_(dve.tensor_tensor(hE, hE, ps[:, 0, :], ALU.mult))
                dve.tensor_tensor(hA, hE, ps[:, 1, :], ALU.mult).then_inc(m_a, 1)
                dve.wait_ge(m_cb, it + 1)
                for k in range(4):
                    a_ = acc3[:, k // 2, (k % 2) * W5:(k % 2 + 1) * W5]
                    ins = dve.tensor_tensor(a_, a_, ps[:, (7, 6, 4, 5)[k], :], ALU.add)
                    if k < 3:
                        link_(ins)
                    else:
                        ins.then_inc(m_cbf, 1)
                link_(dve.tensor_scalar(rQ[:, 0:4], rQ[:, 0:4], float(-P), None, ALU.add))
                dve.wait_ge(m_cbf, it + 1)
                while j[0] < LINKS:
                    link_(dve.tensor_copy(rt[:, 40:41], rt[:, 0:1]))
                assert j[0] == LINKS

            with dve.Fori(0, MAIN) as it:
                round_(it)
            n_over = dve.value_load(ids[0:1, 16:17], min_val=0, max_val=16)
            with dve.If(n_over > 0):
                with dve.Fori(MAIN, ROUNDS) as it:
                    round_(it)
            for i in range(TI):
                n_ch[0] += 1
                dve.tensor_tensor(acc3[:, i, :], acc3[:, i, :], grow[:, 2 * D:3 * D], ALU.mult).then_inc(dve_ch, 1)
                dve.wait_ge(dve_ch, n_ch[0])
            dve.tensor_tensor(x[:], x[:], acc, ALU.add).then_inc(x_ok, 1)

        @block.gpsimd
        def _(pool):
            rw = [(0, t["c_2"]), (8, t["b_ada_2"]), (56, t["norm1_w_2"]), (64, t["norm2_w_2"]), (72, t["out_norm_w_2"])]
            for r, a in rw:
                n = a.shape[1] // P
                pool.dma_start(rowsB[r:r + n, :], a.rearrange("o (c p) -> (o c) p", p=P)).then_inc(ld_rowsB, 16)
            for r, a in ((80, t["cmp_pos_k_2"]), (96, t["cmp_pos_v_2"])):
                pool.dma_start(rowsB[r:r + 16, :], a[0].rearrange("(j a) d -> j (a d)", a=2)).then_inc(ld_rowsB, 16)
            for a in range(2):
                pool.dma_start(rowsB[112:113, a * HD:(a + 1) * HD], t["q_norm_w_2"]).then_inc(ld_rowsB, 16)
                pool.dma_start(rowsB[113:116, a * HD:(a + 1) * HD], t["k_norm_w_2"][0]).then_inc(ld_rowsB, 16)
            pool.dma_start(bfr[:], rows(t["b_forget"], 0, 8)).then_inc(ld_small, 16)
            pool.dma_start(wf[:].rearrange("p (c n) -> p c n", c=DC),
                           w_in[:, 4096:4104].rearrange("(c p) n -> p c n", p=P)).then_inc(ld_small, 16)
            wr3 = wr[:].rearrange("p (c n) -> p c n", c=DC)
            pool.dma_start(wr3[:, :, 0:8], t["w_group_2"][0].rearrange("(c p) n -> p c n", p=P)).then_inc(ld_small, 16)
            pool.dma_start(wr3[:, :, 8:72], t["w_expert_2"][0].rearrange("(c p) n -> p c n", p=P)).then_inc(ld_small, 16)
            pool.dma_start(br[:, 0:8], rows(t["b_group_2"], 0, 8)).then_inc(ld_small, 16)
            pool.dma_start(br[:, 8:72], rows(t["b_expert_2"], 0, 64)).then_inc(ld_small, 16)
            for k, a in enumerate((t["cmp_k_w2_2"], t["cmp_v_w2_2"])):
                pool.dma_start(w2c[:, k * P:(k + 1) * P].rearrange("p (c n) -> p c n", c=2),
                               a[0].rearrange("(c p) n -> p c n", p=P)).then_inc(ld_small, 16)
            pool.wait_ge(mod_raw, 4)
            pool.dma_start(cst[:, 2 * P:], t["constants"][:, 2 * P:]).then_inc(ld_cst, 16)
            pool.dma_start(bg, rows(t["b_gate"], 0, 2 * D)).then_inc(ld_bg, 16)
            pool.dma_start(fg, rows(t["final_g"], 0, D)).then_inc(ld_bg, 16)
            for k, (a, o) in enumerate(((t["b_ada"], 2 * D), (t["b_ada_2"], 2 * D), (t["b_ada_2"], 5 * D))):
                pool.dma_start(grow[:, k * D:(k + 1) * D], rows(a, o, D)).then_inc(ld_grow, 16)
            pool.memset(rbx[:], NEG).then_inc(rb_ok, 1)
            pool.wait_ge(rb_ok, 1)
            pool.dma_start(rbx[0:32, :], t["rel_bias_2"]).then_inc(ld_rows1, 16)
            pool.dma_start(hoT[:], t["buckets"]).then_inc(ld_rows1, 16)

            def below_diagonal(tile):
                return pool.affine_select(out=diag(tile), in_=diag(tile), compare_op=ALU.is_gt, fill=0.0, base=0,
                                          pattern=[[0, 2], [1, P]], channel_multiplier=-1)

            for h in range(H):
                pool.wait_ge(st_L, h + 1)
                below_diagonal(zb(PT, h % 2)).then_inc(st_Lm, 1)
            pool.wait_ge(f_lf, 1)
            pool.wait_ge(ld_cst, 16)
            for h in range(H):
                if h >= 2:
                    pool.wait_ge(fx_z, h - 1)
                u = zb(U, h % 2)
                pool.tensor_scalar(u[:, 0:P], cc(C_LE), fl[:, 48 + h:49 + h], None, ALU.mult)
                pool.tensor_scalar(u[:, P:256], cc(C_ONE), fl[:, 48 + h:49 + h], None, ALU.mult)
                pool.tensor_scalar(u[:, 256:384], cc(C_LE), fl[:, 56 + h:57 + h], None, ALU.mult).then_inc(fx_u, 1)
            pool.wait_ge(misc_free, 31)
            pool.dma_start(bias_dram.rearrange("q h m -> h q m"),
                           bass.AP(tensor=bR.tensor, offset=bR.offset, ap=[bR.ap[0], [0, P], [1, BM]])).then_inc(st_bias, 16)
            pool.wait_ge(st_bias, 16)
            pool.wait_ge(x_ok, 1)
            pool.dma_start(B, bass.AP(tensor=bias_dram.tensor, offset=P - 1, ap=[[H * BM - 1, P], [BM, H], [1, BW]])) \
                .then_inc(ld_bias, 16)
            for a in (X, HTv, Vbd, Pc):
                pool.memset(a, 0.0).then_inc(pad_ok, 1)
            for k in range(3):
                pool.dma_start(cw[:, k * W5:(k + 1) * W5], rows(t["conv_w_2"], k * W5, W5)).then_inc(ld_cw, 16)
            pool.wait_ge(ld_cw, 48)
            for i in range(TI):
                pool.wait_ge(unit_free[i], 24)
                for k in range(3):
                    pool.tensor_tensor(cwp[k][:, i, :], cu3[:, i, :], cw[:, k * W5:(k + 1) * W5],
                                       ALU.mult).then_inc((cv_w, cv_w, cv_w2)[k], 1)


_INS = ["x", "c", "w_ada", "b_ada", "norm_g", "w_in", "b_forget", "w_o_sb", "w_o_fox", "b_gate", "w_out", "final_g",
        "c_2", "w_ada_2", "b_ada_2", "norm1_w_2", "w_in_2", "q_norm_w_2", "k_norm_w_2", "cmp_pos_k_2", "cmp_pos_v_2",
        "cmp_k_w1_2", "cmp_k_w2_2", "cmp_v_w1_2", "cmp_v_w2_2", "conv_w_2", "out_norm_w_2", "w_out_2", "rel_bias_2",
        "norm2_w_2", "w_group_2", "b_group_2", "w_expert_2", "b_expert_2", "w1_2", "w3_2", "w2_2"]


def kernel(**inputs):
    import numpy as _np
    import concourse.bacc as _bacc
    from concourse.bass_utils import run_bass_kernel_spmd as _run

    nc = _bacc.Bacc("TRN2", target_bir_lowering=False, num_devices=1)
    arrays = {n: _np.ascontiguousarray(inputs[n]) for n in _INS}
    arrays["constants"] = constants()
    arrays["buckets"] = bucket_onehot()
    t = {n: nc.dram_tensor(f"in_{n}_dram", a.shape, F32, kind="ExternalInput").ap() for n, a in arrays.items()}
    out = nc.dram_tensor("out_0_dram", (1, T, D), F32, kind="ExternalOutput").ap()
    build(nc, t, out)
    r = _run(nc, [{f"in_{n}_dram": a for n, a in arrays.items()}], core_ids=[0])
    return r.results[0]["out_0_dram"]
```

```python
from contextlib import ExitStack

import numpy as np

import concourse.bass as bass
from concourse import mybir

ALU = mybir.AluOpType
ACT = mybir.ActivationFunctionType
F32 = mybir.dt.float32
I32 = mybir.dt.int32
AX = mybir.AxisListType.X

P = 128
T = 256
TI = T // P
D = 1024
DC = D // P
HD = 64
H = 8
W5 = 512
EPS = 1e-6
NEG = -1e30
QSCALE = HD ** -0.5
NCMP = (T - 32) // 16 + 1
NE = 64
SLOTS = 32
ITEMS = 4
MAIN = NE // ITEMS
ROUNDS = MAIN + 2 * T // SLOTS // ITEMS
BW = 400
BM = BW + P
RING = 4
MRING = 6
MSLOT = (0, 1, 4, 5, 2, 3)
FIRST = (0, 1, 2, 3, 6, 4, 5, 7)
STAGES = 12

C_ID, C_INV, C_GE, C_LE, C_LT, C_ONE, C_GT, C_IOTA, C_S1, C_S1C, C_S2, C_S2C = [k * P for k in range(12)]
C_NM = 12 * P
C_NS = C_NM + 256
C_D64 = C_NS + P
C_D8 = C_D64 + 64
C_THR = C_D8 + 8
C_N = C_THR + 8


def constants():
    p = np.arange(P)[:, None]
    f = np.arange(P)[None, :]
    blocks = [p == f, (p + f >= 0) / 32.0, p >= f, p <= f, p < f, p >= 0 * f, p > f, f + 0 * p,
              f == p + 1, (p == 127) & (f == 0), f == p + 2, f == p - 126]
    f2 = np.arange(256)[None, :]
    blocks.append(np.where(128 + p - f2 >= 0, 0.0, NEG))
    blocks.append(np.where(p >= f, NEG, 0.0))
    blocks.append(np.tile(64.0 - np.arange(64), (P, 1)))
    blocks.append(np.tile(8.0 - np.arange(8), (P, 1)))
    blocks.append(np.tile(np.append(32.0 * np.arange(1, 8), 1e9), (P, 1)))
    return np.concatenate([np.asarray(b, np.float32) for b in blocks], 1)


def bucket_onehot():
    dist = 255 - np.arange(BM)
    n = np.maximum(dist, 0)
    nf = np.maximum(n, 1).astype(np.float32)
    large = 16 + (np.log(nf / np.float32(16)) / np.float32(np.log(8.0)) * np.float32(16)).astype(np.int32)
    b = np.where(n < 16, n, np.minimum(large, 31))
    b = np.where(dist < 0, 32, b)
    return (np.arange(33)[:, None] == b[None, :]).astype(np.float32)


def build(nc, t, out):
    with ExitStack() as ctx:
        def sb(name, cols, dt=F32, parts=P):
            return ctx.enter_context(nc.sbuf_tensor(name, [parts, cols], dt))

        def sem(name):
            return ctx.enter_context(nc.semaphore(name))

        ps = ctx.enter_context(nc.psum_tensor("ps", [P, 8, W5], F32))
        bias_dram = nc.dram_tensor("bias_dram", [P, H, BM], F32).ap()

        ring = sb("ring", RING * 4096)
        arena = sb("arena", 16384)
        cst = sb("cst", C_N)
        x = sb("x_sb", TI * D)
        flex = sb("flex", 4096)
        hT, zS, PT = flex[:, 0:DC * T], flex[:, 2048:2816], flex[:, 2816:3584]
        hoT = sb("hoT", BM, parts=33)
        xn = sb("xn", TI * D)
        modt = sb("modt", W5)
        mod2p = sb("mod2p", W5)
        grow = sb("grow", 3 * D)
        Pb = sb("Pb", 2 * 384)
        R = sb("R", 384)
        U = sb("U", 2 * 384)
        rowsA = sb("rowsA", P)
        rowsB = sb("rowsB", P)
        colA = sb("colA", 40)
        colB = sb("colB", 128)
        c32 = sb("c32", DC * 32)
        mod2c = sb("mod2c", 64)
        ab = sb("ab", 6 * DC)
        stat = sb("stat", 4 * 72)
        soft = sb("soft", 3 * 32)
        ssum = sb("ssum", 24)
        cm = sb("cm", 32)
        wf = sb("wf", DC * 8)
        fl = sb("fl", 6 * 16)
        bfr = sb("bfr", 8)
        wr = sb("wr", DC * 72)
        br = sb("br", 72)
        w2c = sb("w2c", 2 * 2 * HD)
        rbx = sb("rbx", 8)
        rt = sb("rt", 64)
        rGQ = sb("rGQ", 128)
        ids = sb("ids", 96, I32)

        def cc(o, n=P, parts=P):
            return cst[0:parts, o:o + n]

        IDN = cc(C_ID)

        def ar(o, n):
            return arena[:, o:o + n]
        qT = [ar(0, 1024), ar(2048, 1024)]
        kT = [ar(1024, 1024), ar(3072, 1024)]
        vv = [ar(4096, 1024), ar(5120, 1024)]
        sz = [ar(6144, 1024), ar(7168, 1024)]
        gates = ar(8192, 4096)
        bg = ar(12288, 2048)
        fg = ar(14336, 1024)
        merged = ar(4096, 2048)
        B = ar(0, H * BW).rearrange("p (h f) -> p h f", h=H)
        cw = ar(3200, 1536)
        QK = ar(4736, 1536)
        qkT = ar(6272, 1536)
        kvd = ar(7808, 1024)
        vS = ar(8832, 512)
        X = ar(9344, 1024)
        Hh = ar(10368, 512)
        HE = ar(10880, 512)
        HTk = ar(11392, 64)
        HTv = ar(11456, 512)
        kc = ar(11968, 128)
        kcT = ar(12096, 16)
        Vbd = ar(12112, 512)
        Pc = ar(12624, 512)
        PcT = ar(13136, 512)
        bgt = ar(13648, 1024)
        cu = ar(14672, 1024)
        bR = arena[0:8, 15360:15360 + BM]
        Sc = ar(15696, 256)
        G3 = ar(15952, 48)
        cw0 = ar(4736, 1024)
        cw1 = ar(7808, 1024)
        cw2 = ar(9344, 1024)
        sq = hT
        xe = ar(0, 1024)
        hE = ar(1024, 512)
        hA = ar(1536, 512)
        actT = ar(2048, 512)
        ye = ar(2560, 1024)
        sel, wsel, wc = (U[:, k * 256:(k + 1) * 256] for k in range(3))
        rL = Pb[:, 0:144]
        rE, rO1, rO2, rA = (Pb[:, 144 + k * P:144 + (k + 1) * P] for k in range(4))
        cmpi = Pb[:, 656:736]
        rP, nb128, rT = (R[:, k * P:(k + 1) * P] for k in range(3))
        rG, rQ = rGQ[:, 0:64], rGQ[:, 64:128]

        def ringv(n):
            s = n % RING
            return ring[:, s * 4096:(s + 1) * 4096]

        def mringv(q):
            if q >= MRING:
                return arena[:, 4096:8192] if q == MRING else flex[:]
            s = MSLOT[q]
            return ring[:, s * 4096:(s + 1) * 4096] if s < RING else \
                arena[:, 8192 + (s - RING) * 4096:8192 + (s - RING + 1) * 4096]

        def place(it, s):
            if isinstance(it, int) and it * STAGES + s < len(FIRST):
                return FIRST[s], 16 * ITEMS
            return (s - 2) % MRING, it * (32 * ITEMS) + 16 * ITEMS * ((s - 2) // MRING + 1)

        ring_in = [sem(f"ring_in{s}") for s in range(RING)]
        mring_in = [sem(f"mring_in{s}") for s in range(MRING + 2)]
        mring_free = sem("mring_free")
        (ld_id, ld_cst, ld_x, ld_rowsA, ld_rowsB, ld_rows1, ld_small, ld_grow, ld_bias, st_bias, ld_cw, st_out) = [
            sem(n) for n in ("ld_id", "ld_cst", "ld_x", "ld_rowsA", "ld_rowsB", "ld_rows1", "ld_small", "ld_grow",
                             "ld_bias", "st_bias", "ld_cw", "st_out")]
        (ms_done, xn_done, xt_done, hta_done, htv_done, ab_done, mod_raw, cols_tr, c1_ok, colB_ok,
         c2_e, c2_ok, ab_ok, ab2_ok) = [
            sem(n) for n in ("ms_done", "xn_done", "xt_done", "hta_done", "htv_done", "ab_done",
                             "mod_raw", "cols_tr", "c1_ok", "colB_ok", "c2_e", "c2_ok", "ab_ok", "ab2_ok")]
        unit_done = [sem("unit_done0"), sem("unit_done1")]
        unit_free = [sem("unit_free0"), sem("unit_free1")]
        (misc_done, misc_free, mod_ok, mod2_sum, tr_done, tr_free, e_sig) = [
            sem(n) for n in ("misc_done", "misc_free", "mod_ok", "mod2_sum", "tr_done", "tr_free", "e_sig")]
        (st_z, st_zc, st_ln, st_L, st_Lm, st_c, st_w, st_pv) = [
            sem(n) for n in ("st_z", "st_zc", "st_ln", "st_L", "st_Lm", "st_c", "st_w", "st_pv")]
        (fx_u, fx_z, fx_m, fx_p, fx_sc, fx_pv) = [
            sem(n) for n in ("fx_u", "fx_z", "fx_m", "fx_p", "fx_sc", "fx_pv")]
        names = ("f_e f_l f_lf ya_ok mg_ok x_ok sq_ok qk_ok cp_T cp_X cp_h cp_e cp_H cp_w2 cp_v cp_k cp_z cp_s "
                 "cp_x cp_p cp_n cv_w cv_w2 rb_ok pad_ok att_ok ld_bg").split()
        (f_e, f_l, f_lf, ya_ok, mg_ok, x_ok, sq_ok, qk_ok, cp_T, cp_X, cp_h, cp_e, cp_H, cp_w2, cp_v, cp_k, cp_z,
         cp_s, cp_x, cp_p, cp_n, cv_w, cv_w2, rb_ok, pad_ok, att_ok, ld_bg) = [sem(n) for n in names]
        (r_lg, r_s, r_e, r_A, r_rk, r_nb, r_st, r_ci, r_it, ids_ok) = [
            sem(n) for n in ("r_lg", "r_s", "r_e", "r_A", "r_rk", "r_nb", "r_st", "r_ci", "r_it", "ids_ok")]
        (m_sel, m_wsel, m_d, m_xe, m_e, m_a, m_at, m_atc, m_ye, m_cb, m_cbf, m_wt, m_wc, m_ch) = [
            sem(n) for n in ("m_sel", "m_wsel", "m_d", "m_xe", "m_e", "m_a", "m_at", "m_atc", "m_ye", "m_cb", "m_cbf",
                             "m_wt", "m_wc", "m_ch")]
        dve_ch, act_ch = sem("dve_chain"), sem("act_chain")

        def colchunk(w, c0, n=W5):
            return w[:, c0:c0 + n].rearrange("(c p) n -> p c n", p=P), (DC, n)

        w_in, w_in2 = t["w_in"][0], t["w_in_2"][0]
        ada, ada2 = t["w_ada"][0], t["w_ada_2"][0]
        chunks = [colchunk(ada, n * W5) for n in range(4)]
        PROJ0, MODQ = len(chunks), 10
        proj_cols = [512, 0, 1024, 1536, 2560, 2048, 3072, 3584] + [4104 + n * W5 for n in range(4)]
        for q in range(12):
            chunks += [colchunk(w_in, proj_cols[q])] + ([colchunk(ada2, q * W5)] if q < MODQ else [])
        ADAG = len(chunks)
        chunks += [colchunk(ada, n * W5) for n in (4, 5)]
        WO = len(chunks)
        for w in (t["w_o_sb"][0], t["w_o_fox"][0]):
            chunks.append((w.rearrange("(c p) n -> p c n", p=P), (4, 1024)))
        WOUT = len(chunks)
        chunks += [colchunk(t["w_out"][0], n * W5) for n in range(2)]
        KV = len(chunks)
        chunks += [colchunk(w_in2, 512), colchunk(w_in2, 1024, 280), colchunk(w_in2, 0)]
        CMP = len(chunks)
        for w in (t["cmp_k_w1_2"][0], t["cmp_v_w1_2"][0]):
            chunks.append((w.rearrange("(j p) n -> p j n", p=P), (16, 256)))
        CONV = len(chunks)
        chunks += [colchunk(w_in2, 1304 + W5), colchunk(ada2, 10 * W5), colchunk(w_in2, 1304 + 2 * W5),
                   colchunk(ada2, 11 * W5), colchunk(w_in2, 1304)]
        WO2 = len(chunks)
        chunks += [colchunk(t["w_out_2"][0], n * W5) for n in range(2)]
        NCH = len(chunks)

        def proj(q):
            return PROJ0 + 2 * q if q < MODQ else PROJ0 + MODQ + q

        def mod2(q):
            return PROJ0 + 2 * q + 1 if q < MODQ else CONV + 1 + 2 * (q - MODQ)

        def cview(n):
            a, b = chunks[n][1]
            return ringv(n)[:, 0:a * b].rearrange("p (a b) -> p a b", a=a)

        def unit_read(u):
            return unit_done[u % 2], u // 2 + 1

        read_by = [(mod_raw, n + 1) for n in range(4)]
        for q in range(12):
            read_by += [unit_read(2 * q + 1)] + ([(mod2_sum, q + 1)] if q < MODQ else [])
        read_by += [(misc_done, 12), (misc_done, 14), unit_read(27), unit_read(31), unit_read(34), unit_read(35),
                    unit_read(39), unit_read(40), unit_read(41), (cp_h, 1), (cp_h, 2),
                    unit_read(43), (mod2_sum, 11), unit_read(45), (mod2_sum, 12), unit_read(47), unit_read(52), unit_read(53)]
        assert len(read_by) == NCH

        def rows(ap, c0, n):
            return bass.AP(tensor=ap.tensor, offset=ap.offset + c0, ap=[[0, P], [1, n]])

        def Z(b):
            return ps[:, 2 + b, 0:384]

        def diag(tile):
            return bass.AP(tensor=tile.tensor, offset=tile.offset, ap=[tile.ap[0], [256, 2], [1, P]])

        v3 = [vv[b].rearrange("p (i n) -> p i n", i=TI) for b in range(2)]
        qT3 = [q.rearrange("p (m t) -> p m t", m=4) for q in qT]
        kT3 = [k.rearrange("p (m t) -> p m t", m=4) for k in kT]
        hT3 = hT[:].rearrange("p (c t) -> p c t", c=DC)
        x3 = x[:].rearrange("p (i d) -> p i d", i=TI)
        xn3 = xn[:].rearrange("p (i d) -> p i d", i=TI)
        g3 = gates.rearrange("p (i n) -> p i n", i=TI)
        mg3 = merged.rearrange("p (i n) -> p i n", i=TI)
        sz3 = [s.rearrange("p (i n) -> p i n", i=TI) for s in sz]
        yT3 = qT3
        QK4 = QK.rearrange("p (i h d) -> p i h d", i=TI, h=12)
        qkT3 = qkT.rearrange("p (m t) -> p m t", m=6)
        kvd6 = kvd.rearrange("p (i kv g a d) -> p i kv g a d", i=2, kv=2, g=2, a=2)
        vS4 = vS.rearrange("p (a i n) -> p a i n", a=2, i=2)
        X5 = X.rearrange("p (kv j g n) -> p kv j g n", kv=2, j=16, g=2)
        HTk3 = HTk.rearrange("p (c n) -> p c n", c=2)
        HTv5 = HTv.rearrange("p (c g r n) -> p c g r n", c=2, g=2, r=4)
        Vbd3 = Vbd.rearrange("p (g n) -> p g n", g=2)
        Pc4 = Pc.rearrange("p (i h n) -> p i h n", i=2, h=8)
        PcT4 = PcT.rearrange("p (i g n) -> p i g n", i=2, g=2)
        Sc4 = Sc.rearrange("p (i h n) -> p i h n", i=2, h=8)
        G34 = G3.rearrange("p (i h n) -> p i h n", i=2, h=8)
        bgt3 = bgt.rearrange("p (i n) -> p i n", i=TI)
        cu3 = cu.rearrange("p (i n) -> p i n", i=TI)
        cwp = [a.rearrange("p (i n) -> p i n", i=TI) for a in (cw0, cw1, cw2)]
        xe3 = xe.rearrange("p (c n) -> p c n", c=DC)
        actT3 = actT.rearrange("p (j n) -> p j n", j=4)
        sel3 = sel.rearrange("p (i n) -> p i n", i=TI)
        wsel3 = wsel.rearrange("p (i n) -> p i n", i=TI)
        wc3 = wc.rearrange("p (i n) -> p i n", i=TI)

        def zb(buf, b):
            return buf[:, b * 384:(b + 1) * 384]

        MS, VA, RS, TM = (stat[:, k * 72:(k + 1) * 72] for k in range(4))
        SM, MX, CO = (soft[:, k * 32:(k + 1) * 32] for k in range(3))
        NRM = [(2, P), (2, P), (2, P), (12, P), (12, P), (2, 16), (16, P), (16, P), (1, P), (1, P)]
        NO = [sum(w for w, _ in NRM[:k]) for k in range(len(NRM) + 1)]
        JA, JB = PT[:, 0:W5], Pb[:, 0:W5]

        block = ctx.enter_context(nc.Block())

        @block.sync
        def _(sp):
            sp.dma_start(cst[:, 0:2 * P], t["constants"][:, 0:2 * P]).then_inc(ld_id, 16)
            for n in range(NCH):
                if n == 1:
                    sp.dma_start(x3, t["x"][0].rearrange("(i p) d -> p i d", p=P)).then_inc(ld_x, 16)
                if n >= RING:
                    sp.wait_ge(*read_by[n - RING])
                sp.dma_start(cview(n), chunks[n][0]).then_inc(ring_in[n % RING], 16)
            w1, w3, w2 = t["w1_2"][0], t["w3_2"][0], t["w2_2"][0]

            def stage(it, s, ex):
                q = place(it, s)[0]
                dst = mringv(q)
                for e in range(ITEMS):
                    if s < 8:
                        w = (w1, w3)[s % 2]
                        src = w[bass.ds(ex[e], 1), (s // 2) * 256:(s // 2 + 1) * 256, :] \
                            .rearrange("o (r p) n -> p (o r) n", p=P)
                        d = dst[:, e * 1024:(e + 1) * 1024].rearrange("p (r n) -> p r n", r=2)
                    else:
                        src = w2[bass.ds(ex[e], 1), (s - 8) * P:(s - 7) * P, :].rearrange("o p n -> p (o n)")
                        d = dst[:, e * 1024:(e + 1) * 1024]
                    sp.dma_start(d, src).then_inc(mring_in[q], 16)

            out_of_arena = [(att_ok, 2), (cp_p, 1)]
            first = [[read_by[NCH - 4]], [read_by[NCH - 3]], out_of_arena, [], [],
                     [read_by[NCH - 2]], [read_by[NCH - 1]], [(r_lg, 1)]]
            for s in range(STAGES):
                if s < len(FIRST):
                    for sem_, value in first[s]:
                        sp.wait_ge(sem_, value)
                else:
                    sp.wait_ge(mring_free, s - len(FIRST) + 1)
                stage(0, s, range(ITEMS))
            with sp.Fori(1, MAIN) as it:
                for s in range(STAGES):
                    sp.wait_ge(mring_free, it * STAGES + (s - MRING + 1))
                    stage(it, s, [it * ITEMS + e for e in range(ITEMS)])
            sp.wait_ge(ids_ok, 1)
            n_over = sp.value_load(ids[0:1, 16:17], min_val=0, max_val=16)
            with sp.If(n_over > 0):
                with sp.Fori(MAIN, ROUNDS) as it:
                    ex = [sp.value_load(ids[0:1, bass.ds((it - MAIN) * ITEMS + e, 1)], min_val=0, max_val=NE - 1)
                          for e in range(ITEMS)]
                    for s in range(STAGES):
                        sp.wait_ge(mring_free, it * STAGES + (s - MRING + 1))
                        stage(it, s, ex)
                sp.wait_ge(m_cbf, ROUNDS)
            sp.wait_ge(m_cbf, MAIN)
            sp.dma_start(out[0].rearrange("(i p) d -> p i d", p=P), x3).then_inc(st_out, 16)
            sp.wait_ge(st_out, 16)

        @block.tensor
        def _(pe):
            used = [0]
            units = [0]
            misc = [0]
            trs = [0]

            def chunk_in(n):
                pe.wait_ge(ring_in[n % RING], 16 * (n // RING + 1))

            def unit_bank():
                u = units[0]
                if u >= 2:
                    pe.wait_ge(unit_free[u % 2], u // 2)
                units[0] += 1
                return u % 2

            def misc_bank():
                if misc[0]:
                    pe.wait_ge(misc_free, misc[0])
                misc[0] += 1

            def tr_bank():
                if trs[0]:
                    pe.wait_ge(tr_free, trs[0])
                trs[0] += 1

            def mod_product(n, bank, done):
                chunk_in(n)
                for c in range(DC):
                    j = c % 4
                    mm = pe.matmul(ps[32 * j:32 * j + 32, bank, :], c32[:, c * 32:(c + 1) * 32], cview(n)[:, c, :],
                                   start=c < 4, stop=c >= 4, skip_group_check=True)
                mm.then_inc(done, 1)

            def to_features(src3, i, k):
                pe.wait_ge(xn_done, k)
                for c in range(DC):
                    mm = pe.transpose(ps[:, (2, 5)[i] + c // 4, (c % 4) * P:(c % 4 + 1) * P],
                                      src3[:, i, c * P:(c + 1) * P], IDN)
                mm.then_inc(xt_done, 1)

            pe.wait_ge(ld_id, 16)
            pe.wait_ge(ld_rowsA, 48)
            pe.transpose(ps[:, 7, 0:40], rowsA[0:40, :], cst[0:40, C_ID:C_ID + 40]).then_inc(cols_tr, 1)
            pe.wait_ge(c1_ok, 1)
            for n in range(4):
                mod_product(n, 4, mod_raw)
                pe.wait_ge(mod_ok, n + 1)
                for m in range(4):
                    mm = pe.matmul(ps[:, 0, 4 * n + m:4 * n + m + 1], modt[:, m * P:(m + 1) * P],
                                   cst[:, C_INV:C_INV + 1], start=True, stop=True)
                mm.then_inc(ab_done, 1)
                if n < TI:
                    to_features(xn3, n, n + 1)
                if n == 2:
                    pe.wait_ge(ld_rowsB, 16 * 11)
                    pe.transpose(ps[:, 7, 0:116], rowsB[0:116, :], cst[0:116, C_ID:C_ID + 116]).then_inc(cols_tr, 1)

            def stationary_unit(n, half, b=None):
                b = unit_bank()
                for m2 in range(2):
                    for c in range(DC):
                        mm = pe.matmul(ps[:, b, m2 * 256:(m2 + 1) * 256],
                                       cview(n)[:, c, (2 * half + m2) * P:(2 * half + m2 + 1) * P],
                                       hT3[:, c, :], start=c == 0, stop=c == DC - 1)
                mm.then_inc(unit_done[b], 1)

            def token_unit(lhs3, i, rhs, kc_, n=W5):
                b = unit_bank()
                for c in range(kc_):
                    mm = pe.matmul(ps[:, b, 0:n], lhs3[:, c, i * P:(i + 1) * P], rhs[:, c, :],
                                   start=c == 0, stop=c == kc_ - 1)
                mm.then_inc(unit_done[b], 1)

            def f_logits():
                misc_bank()
                for i in range(TI):
                    for c in range(DC):
                        mm = pe.matmul(ps[:, 7, i * 8:(i + 1) * 8], hT3[:, c, i * P:(i + 1) * P],
                                       wf[:, c * 8:(c + 1) * 8], start=c == 0, stop=c == DC - 1)
                mm.then_inc(misc_done, 1)

            def mod2_out(q):
                misc_bank()
                pe.wait_ge(mod2_sum, q + 1)
                if q in (4, 5, 10, 11):
                    mm = pe.matmul(ps[:, 7, :], cc(C_ONE), mod2p[:], start=True, stop=True)
                else:
                    for m in range(4):
                        mm = pe.matmul(ps[:, 7, m:m + 1], mod2p[:, m * P:(m + 1) * P], cst[:, C_ONE:C_ONE + 1],
                                       start=True, stop=True)
                mm.then_inc(misc_done, 1)

            def stick_scores(h):
                b, m, lo = h % 2, h // 2, 64 * (h % 2)
                if h == 0:
                    pe.wait_ge(ld_cst, 16)
                    pe.wait_ge(unit_free[0], 2)
                    pe.wait_ge(unit_free[1], 2)
                if h >= 2:
                    pe.wait_ge(st_w, h - 1)
                k, q = kT3[0][lo:lo + 64, m, :], qT3[0][lo:lo + 64, m, :]
                pe.matmul(ps[:, 2 + b, 0:256], k[:, 0:P], q[:, :], start=True, stop=False, skip_group_check=True)
                pe.matmul(ps[:, 2 + b, 256:384], k[:, P:T], q[:, P:T], start=False, stop=False,
                          skip_group_check=True).then_inc(st_z, 1)

            def stick_after(h):
                b = h % 2
                L = zb(PT, b)
                pe.wait_ge(st_Lm, h + 1)
                pe.matmul(ps[:, 2 + b, 0:256], cc(C_GE), L[:, 0:256], start=False, stop=False, skip_group_check=True)
                pe.matmul(ps[:, 2 + b, P:256], cc(C_ONE), L[:, 256:384], start=False, stop=False, skip_group_check=True)
                pe.matmul(ps[:, 2 + b, 256:384], cc(C_GE), L[:, 256:384], start=False, stop=False, skip_group_check=True)
                for o in (0, 256):
                    mm = pe.matmul(ps[:, 2 + b, o:o + P], IDN, cc(C_NS), start=False, stop=True, skip_group_check=True)
                mm.then_inc(st_c, 1)

            def pv(w, v0, v1, h, blocks, start0):
                pe.matmul(ps[:, 5, h * HD:(h + 1) * HD], w[:, blocks[0]:blocks[0] + P], v0, start=start0,
                          stop=False, skip_group_check=True)
                pe.matmul(ps[:, 6, h * HD:(h + 1) * HD], w[:, blocks[1]:blocks[1] + P], v0, start=start0,
                          stop=False, skip_group_check=True)
                return pe.matmul(ps[:, 6, h * HD:(h + 1) * HD], w[:, blocks[2]:blocks[2] + P], v1, start=False,
                                 stop=False, skip_group_check=True)

            def stick_pv(h):
                if h == 0:
                    pe.wait_ge(unit_free[0], 3)
                    pe.wait_ge(unit_free[1], 3)
                pe.wait_ge(st_w, h + 1)
                pv(zb(Pb, h % 2), v3[0][:, 0, h * HD:(h + 1) * HD], v3[0][:, 1, h * HD:(h + 1) * HD], h,
                   (0, 128, 256), True).then_inc(st_pv, 1)

            def y_transposes(b, i):
                tr_bank()
                pe.wait_ge(ya_ok, 2 * b + i + 1)
                for c in range(4):
                    mm = pe.transpose(ps[:, 4, c * P:(c + 1) * P], sz3[b][:, i, c * P:(c + 1) * P], IDN)
                mm.then_inc(tr_done, 1)

            def fox_scores(h):
                b, m, lo = h % 2, h // 2, 64 * (h % 2)
                if h == 0:
                    pe.wait_ge(unit_free[0], 6)
                    pe.wait_ge(unit_free[1], 6)
                    pe.wait_ge(st_w, 8)
                if h >= 2:
                    pe.wait_ge(fx_m, h - 1)
                k, q = kT3[1][lo:lo + 64, m, :], qT3[1][lo:lo + 64, m, :]
                u = zb(U, b)
                pe.wait_ge(fx_u, h + 1)
                kw = dict(skip_group_check=True)
                pe.matmul(ps[:, 2 + b, 0:P], q[:, 0:P], k[:, 0:P], start=True, stop=False, **kw)
                pe.matmul(ps[:, 2 + b, P:384], q[:, P:T], k[:, 0:T], start=False, stop=False, **kw)
                pe.matmul(ps[:, 2 + b, 0:P], u[:, 0:P], cc(C_GT), start=False, stop=False, **kw)
                pe.matmul(ps[:, 2 + b, P:256], u[:, P:256], cc(C_GT), start=False, stop=False, **kw)
                pe.matmul(ps[:, 2 + b, P:384], u[:, 256:384], cst[:, C_ONE:C_ONE + 256], start=False,
                          stop=True, **kw).then_inc(fx_z, 1)

            def p_transposes(k, b, ready):
                tr_bank()
                pe.wait_ge(ready, k + 1)
                for c in range(3):
                    mm = pe.transpose(ps[:, 4, c * P:(c + 1) * P], zb(Pb, b)[:, c * P:(c + 1) * P], IDN)
                mm.then_inc(tr_done, 1)

            def fox_pv(h, tr_index):
                if h == 0:
                    pe.wait_ge(unit_free[0], 7)
                    pe.wait_ge(unit_free[1], 7)
                    pe.wait_ge(ya_ok, 2)
                pe.wait_ge(tr_free, tr_index + 1)
                pv(zb(PT, h % 2), v3[1][:, 0, h * HD:(h + 1) * HD], v3[1][:, 1, h * HD:(h + 1) * HD], h,
                   (0, 128, 256), True).then_inc(fx_pv, 1)

            pe.wait_ge(hta_done, 2)
            pe.wait_ge(htv_done, 2)
            fox_tr = {}
            for u in range(26):
                if u < 24:
                    q, half = u // 2, u % 2
                    n = proj(q)
                    if half == 0:
                        chunk_in(n)
                    if q in (0, 1, 4, 5):
                        stationary_unit(n, half)
                    else:
                        token_unit(hT3, half, cview(n), DC)
                if u == 0:
                    pe.wait_ge(ld_small, 16 * 8)
                    f_logits()
                if u % 2 == 1 and 3 <= u < 3 + 2 * MODQ:
                    if u == 3:
                        pe.wait_ge(ld_cst, 16)
                    mod2_out(u // 2 - 1)
                if 0 <= u - 4 < H:
                    stick_scores(u - 4)
                if 0 <= u - 5 < H:
                    stick_after(u - 5)
                if 0 <= u - 6 < H:
                    stick_pv(u - 6)
                if 0 <= u - 14 < H:
                    fox_scores(u - 14)
                if 0 <= u - 16 < H:
                    fox_pv(u - 16, fox_tr[u - 16])
                if u in (14, 15):
                    y_transposes(0, u - 14)
                if 0 <= u - 15 < H:
                    fox_tr[u - 15] = trs[0]
                    p_transposes(u - 15, (u - 15) % 2, fx_p)
            def gate_row(k):
                misc_bank()
                if k % 2 == 0:
                    mod_product(ADAG + k // 2, 7, misc_done)
                else:
                    pe.matmul(ps[:, 7, :], cc(C_INV), modt[:], start=True, stop=True).then_inc(misc_done, 1)

            def rel_bias(n0, n1):
                misc_bank()
                pe.matmul(ps[0:8, 7, 0:n1 - n0], rbx[0:33, :], hoT[0:33, n0:n1], start=True,
                          stop=True).then_inc(misc_done, 1)

            gate_row(0)
            pe.wait_ge(tr_free, 2)
            chunk_in(WO)
            for i in range(TI):
                for n in range(2):
                    token_unit(yT3[0], i, cview(WO)[:, :, n * W5:(n + 1) * W5], 4)
                    if 2 * i + n < 3:
                        gate_row(2 * i + n + 1)
                if i == 0:
                    y_transposes(1, 0)
            pe.wait_ge(ld_rows1, 32)
            pe.wait_ge(rb_ok, 1)
            rel_bias(0, W5)
            y_transposes(1, 1)
            chunk_in(WO + 1)
            for i in range(TI):
                pe.wait_ge(tr_free, trs[0] - 1 + i)
                for n in range(2):
                    token_unit(yT3[1], i, cview(WO + 1)[:, :, n * W5:(n + 1) * W5], 4)
                    if i == n == 0:
                        rel_bias(W5, BM)
                    if i == 1 and n == 0:
                        to_features(mg3, 0, 3)
            for i in range(TI):
                pe.wait_ge(hta_done, 3 + i)
                pe.wait_ge(htv_done, 3 + i)
                for n in range(2):
                    if i == 0:
                        chunk_in(WOUT + n)
                    if i == n == 1:
                        to_features(xn3, 0, 5)
                    token_unit(hT3, i, cview(WOUT + n), DC)
                    if i == n == 0:
                        to_features(mg3, 1, 4)
            for i in range(TI):
                pe.wait_ge(hta_done, 5 + i)
                pe.wait_ge(htv_done, 5 + i)
                for k in range(3):
                    if i == 0:
                        chunk_in(KV + k)
                    token_unit(hT3, i, cview(KV + k), DC, chunks[KV + k][1][1])
                    if i == k == 0:
                        to_features(xn3, 1, 6)

            def qk_transposes(i):
                pe.wait_ge(qk_ok, i + 1)
                for blocks in (range(4), range(4, 6)):
                    tr_bank()
                    for c in blocks:
                        mm = pe.transpose(ps[:, 4, (c % 4) * P:(c % 4 + 1) * P],
                                          QK4[:, i, 2 * c:2 * c + 2, :].rearrange("p h d -> p (h d)"), IDN)
                    mm.then_inc(tr_done, 1)

            def cmp_hidden(kv):
                chunk_in(CMP + kv)
                for j in range(16):
                    mm = pe.matmul(ps[0:32, 7, kv * 256:(kv + 1) * 256],
                                   X5[:, kv, j, :, :].rearrange("p g n -> p (g n)"),
                                   cview(CMP + kv)[:, j, :], start=j == 0, stop=j == 15)
                mm.then_inc(cp_h, 1)

            pe.wait_ge(cp_v, 2)
            for kv in range(2):
                for g in range(2):
                    for i in range(TI):
                        mm = pe.transpose(ps[:, 2 + kv, g * 256 + i * P:g * 256 + (i + 1) * P],
                                          kvd6[:, i, kv, g, :, :].rearrange("p a d -> p (a d)"), IDN)
            mm.then_inc(cp_T, 1)
            qk_transposes(0)
            pe.wait_ge(cp_X, 4)
            pe.wait_ge(misc_free, misc[0])
            cmp_hidden(0)
            qk_transposes(1)

            def attn_scores(t_, a):
                h = t_
                g, m, lo = h // 4, h % 4, 64 * (h // 4)
                v = 2 * t_ + a
                if v >= 2:
                    pe.wait_ge(fx_m, 8 + v - 1)
                q, k = qkT3[lo:lo + 64, m, :], qkT3[lo:lo + 64, 4 + a, :]
                pe.matmul(ps[:, 2 + a, 0:P], q[:, 0:P], k[:, 0:P], start=True, stop=False, skip_group_check=True)
                pe.matmul(ps[:, 2 + a, P:384], q[:, P:T], k[:, 0:T], start=False, stop=True,
                          skip_group_check=True).then_inc(fx_z, 1)

            attn_tr = {}

            def attn_pv(t_, a):
                g = t_ // 4
                pe.wait_ge(tr_free, attn_tr[2 * t_ + a] + 1)
                pv(zb(PT, a), vS4[:, a, 0, g * HD:(g + 1) * HD], vS4[:, a, 1, g * HD:(g + 1) * HD], t_,
                   (0, 128, 256), t_ == 0 and a == 0).then_inc(fx_pv, 1)

            def attn_transposes(t_, a):
                attn_tr[2 * t_ + a] = trs[0]
                p_transposes(2 * t_ + a, a, fx_sc)

            pe.wait_ge(tr_free, trs[0])
            pe.wait_ge(ya_ok, 4)
            for w in range(10):
                if w == 1:
                    cmp_hidden(1)
                if 2 <= w < 8:
                    k, i = (w - 2) // 2, w % 2
                    if i == 0:
                        chunk_in(CONV + 2 * k)
                    token_unit(hT3, i, cview(CONV + 2 * k), DC)
                if w in (5, 7):
                    if w == 7:
                        pe.wait_ge(cp_s, 1)
                    mod2_out(10 + w // 7)
                if w == 8:
                    pe.wait_ge(cv_w, 4)
                    for i in range(TI):
                        b = unit_bank()
                        terms = [(C_S1, 1, i), (C_S2, 0, i)] + ([(C_S1C, 1, 0), (C_S2C, 0, 0)] if i else [])
                        for k, (o, wi, i2) in enumerate(terms):
                            mm = pe.matmul(ps[:, b, :], cc(o), cwp[wi][:, i2, :], start=k == 0,
                                           stop=k == len(terms) - 1)
                        mm.then_inc(unit_done[b], 1)
                for a in range(2):
                    if 0 <= w - 2 < 8:
                        attn_pv(w - 2, a)
                    if 0 <= w - 1 < 8:
                        attn_transposes(w - 1, a)
                    if w < 8:
                        attn_scores(w, a)
                if w == 2:
                    pe.wait_ge(cp_H, 1)
                    tr_bank()
                    for c in range(4):
                        mm = pe.transpose(ps[:, 4, c * 32:(c + 1) * 32], Hh[0:32, c * P:(c + 1) * P],
                                          cst[0:32, C_ID:C_ID + 32])
                    mm.then_inc(tr_done, 1)
                    h_tr = trs[0]
                if w == 3:
                    pe.wait_ge(tr_free, h_tr)
                    for g in range(2):
                        for c in range(2):
                            pe.matmul(ps[0:16, 7, g * HD:(g + 1) * HD], HTk3[:, c, g * 16:(g + 1) * 16],
                                      w2c[:, c * HD:(c + 1) * HD], start=c == 0, stop=c == 1)
                    for g in range(2):
                        for c in range(2):
                            mm = pe.matmul(ps[:, 7, P + g * HD:P + (g + 1) * HD],
                                           HTv5[:, c, g, :, :].rearrange("p r n -> p (r n)"),
                                           w2c[:, (2 + c) * HD:(3 + c) * HD], start=c == 0, stop=c == 1)
                    mm.then_inc(cp_w2, 1)
                if w == 4:
                    pe.wait_ge(cp_k, 1)
                    tr_bank()
                    pe.transpose(ps[:, 4, 0:16], kc[0:16, :], cst[0:16, C_ID:C_ID + 16]).then_inc(tr_done, 1)
                    k_tr = trs[0]
                if w == 5:
                    pe.wait_ge(misc_free, misc[0])
                    pe.wait_ge(tr_free, k_tr)
                    for g in range(2):
                        lo = 64 * g
                        if g:
                            pe.wait_ge(cp_z, 1)
                        for i in range(TI):
                            for m in range(4):
                                o = (i * H + 4 * g + m) * 16
                                mm = pe.matmul(ps[:, 7, o:o + 16], qkT3[lo:lo + 64, m, i * P:(i + 1) * P],
                                               kcT[lo:lo + 64, :], start=True, stop=True)
                        mm.then_inc(cp_z, 1)
                if w == 7:
                    pe.wait_ge(cp_n, 1)
                    tr_bank()
                    for i in range(TI):
                        for g in range(2):
                            mm = pe.transpose(ps[:, 4, (2 * i + g) * P:(2 * i + g + 1) * P],
                                              Pc4[:, i, 4 * g:4 * g + 4, :].rearrange("p h n -> p (h n)"), IDN)
                    mm.then_inc(tr_done, 1)
                    c_tr = trs[0]
                if w == 9:
                    pe.wait_ge(tr_free, c_tr)
                    for i in range(TI):
                        for g in range(2):
                            mm = pe.matmul(ps[:, 5 + i, g * 256:(g + 1) * 256], PcT4[:, i, g, :], Vbd3[:, g, :],
                                           start=False, stop=False, skip_group_check=True)
                    mm.then_inc(cp_p, 1)
            for half, bank in ((1, 2), (0, 5)):
                for i in range(TI):
                    pe.wait_ge(xn_done, 7 + 2 * (1 - half) + i)
                    for c in range(4):
                        mm = pe.transpose(ps[:, bank + i, c * P:(c + 1) * P],
                                          xn3[:, i, (4 * half + c) * P:(4 * half + c + 1) * P], IDN)
                    mm.then_inc(xt_done, 1)
            for i in range(TI):
                pe.wait_ge(hta_done, 7 + i)
                pe.wait_ge(htv_done, 7 + i)
                for n in range(2):
                    if i == 0:
                        chunk_in(WO2 + n)
                    if i == n == 1:
                        to_features(xn3, 0, 11)
                    token_unit(hT3, i, cview(WO2 + n), DC)
            for i in range(TI):
                if i:
                    to_features(xn3, i, 11 + i)
                pe.wait_ge(hta_done, 9 + i)
                pe.wait_ge(htv_done, 9 + i)
                for c in range(DC):
                    mm = pe.matmul(ps[:, 7, i * 72:(i + 1) * 72], hT3[:, c, i * P:(i + 1) * P],
                                   wr[:, c * 72:(c + 1) * 72], start=c == 0, stop=c == DC - 1)
            mm.then_inc(r_lg, 1)
            pe.wait_ge(r_A, 1)
            A3 = rA.rearrange("p (i e) -> p i e", i=TI)
            pe.matmul(ps[:, 7, 0:64], cc(C_LT), A3[:, 0, :], start=True, stop=True)
            pe.matmul(ps[:, 7, 64:128], cc(C_ONE), A3[:, 0, :], start=True, stop=False)
            pe.matmul(ps[:, 7, 64:128], cc(C_LT), A3[:, 1, :], start=False, stop=True)
            pe.matmul(ps[0:64, 7, 128:129], A3[:, 0, :], cst[:, C_ONE:C_ONE + 1], start=True, stop=False)
            pe.matmul(ps[0:64, 7, 128:129], A3[:, 1, :], cst[:, C_ONE:C_ONE + 1], start=False,
                      stop=True).then_inc(r_rk, 1)
            pe.wait_ge(r_nb, 1)
            pe.matmul(ps[:, 4, 192:256], nb128[0:64, :], cst[0:64, C_LT:C_LT + 64], start=True, stop=True)
            pe.matmul(ps[:, 4, 256:257], nb128[0:64, :], cst[0:64, C_ONE:C_ONE + 1], start=True, stop=True)
            pe.matmul(ps[0:64, 4, 257:258], cst[0:64, C_LE:C_LE + 64], nb128[0:64, 0:1], start=True,
                      stop=True).then_inc(r_st, 1)
            pe.wait_ge(r_ci, 1)
            pe.matmul(ps[0:1, 5, 0:16], cst[0:64, C_ONE:C_ONE + 1], cmpi[0:64, 0:16], start=True,
                      stop=True).then_inc(r_it, 1)
            pe.wait_ge(ids_ok, 1)

            def round_(it):
                pe.wait_ge(m_sel, it + 1)
                for c in range(DC):
                    for i in range(TI):
                        mm = pe.matmul(ps[:, 4 + c // 4, (c % 4) * P:(c % 4 + 1) * P],
                                       xn3[:, i, c * P:(c + 1) * P], sel3[:, i, :], start=i == 0, stop=i == 1)
                mm.then_inc(m_d, 1)
                pe.wait_ge(m_wsel, it + 1)
                for i in range(TI):
                    mm = pe.transpose(ps[:, 6, i * P:(i + 1) * P], wsel3[:, i, :], IDN)
                mm.then_inc(m_wt, 1)
                pe.wait_ge(m_xe, it * 2 + 2)
                for s in range(8):
                    q, landed = place(it, s)
                    pe.wait_ge(mring_in[q], landed)
                    wv = mringv(q).rearrange("p (e r n) -> p e r n", e=4, r=2)
                    for r in range(2):
                        c = 2 * (s // 2) + r
                        for e in range(ITEMS):
                            mm = pe.matmul(ps[32 * e:32 * e + 32, s % 2, :], xe3[:, c, 32 * e:32 * e + 32],
                                           wv[:, e, r, :], start=c == 0, stop=c == DC - 1, skip_group_check=True)
                    mm.then_inc(mring_free, 1)
                pe.wait_ge(m_a, it + 1)
                pe.wait_ge(m_wc, it + 1)
                for j in range(4):
                    mm = pe.transpose(ps[:, 6, j * P:(j + 1) * P], hA[:, j * P:(j + 1) * P], IDN)
                mm.then_inc(m_at, 1)
                pe.wait_ge(m_atc, it + 1)
                for s in range(8, STAGES):
                    q, landed = place(it, s)
                    pe.wait_ge(mring_in[q], landed)
                    wv = mringv(q).rearrange("p (e n) -> p e n", e=4)
                    for n in range(2):
                        for e in range(ITEMS):
                            mm = pe.matmul(ps[32 * e:32 * e + 32, 2 + n, :], actT3[:, s - 8, 32 * e:32 * e + 32],
                                           wv[:, e, n * W5:(n + 1) * W5], start=s == 8, stop=s == STAGES - 1,
                                           skip_group_check=True)
                    mm.then_inc(mring_free, 1)
                pe.wait_ge(m_ye, it + 1)
                for k in range(4):
                    i, n = k // 2, k % 2
                    mm = pe.matmul(ps[:, (7, 6, 4, 5)[k], :], wc3[:, i, :], ye[:, n * W5:(n + 1) * W5],
                                   start=True, stop=True)
                    mm.then_inc(m_cb, 1)
                pe.wait_ge(m_cbf, it + 1)

            round_(0)
            with pe.Fori(1, MAIN) as it:
                round_(it)
            n_over = pe.value_load(ids[0:1, 16:17], min_val=0, max_val=16)
            with pe.If(n_over > 0):
                with pe.Fori(MAIN, ROUNDS) as it:
                    round_(it)

        @block.scalar
        def _(act):
            n_ch = [0]

            def link(ins):
                n_ch[0] += 1
                ins.then_inc(act_ch, 1)
                act.wait_ge(act_ch, n_ch[0])

            act.dma_start(rowsA[0:8, :], t["c"].rearrange("o (c p) -> (o c) p", p=P)).then_inc(ld_rowsA, 16)
            act.dma_start(rowsA[8:32, :], t["b_ada"].rearrange("o (c p) -> (o c) p", p=P)).then_inc(ld_rowsA, 16)
            act.dma_start(rowsA[32:40, :], t["norm_g"].rearrange("o (c p) -> (o c) p", p=P)).then_inc(ld_rowsA, 16)

            n_ms = [0]

            def squares(out_, src, width, acc_):
                act.activation(out_, src, ACT.Square, scale=width ** -0.5, accum_out=acc_).then_inc(ms_done, 1)
                n_ms[0] += 1

            def to_hT(a, i, k, bank=(2, 5)):
                act.wait_ge(xt_done, k)
                for c in range(4):
                    dst, src = hT3[:, c, i * P:(i + 1) * P], ps[:, bank[i], c * P:(c + 1) * P]
                    if a is None:
                        ins = act.copy(dst, src)
                    elif a[1] is None:
                        ins = act.activation(dst, src, ACT.Copy, scale=a[0][:, c:c + 1])
                    else:
                        ins = act.activation(dst, src, ACT.Identity, scale=a[0][:, c:c + 1], bias=a[1][:, c:c + 1])
                ins.then_inc(hta_done, 1)

            act.wait_ge(ld_x, 16)
            for i in range(TI):
                squares(xn3[:, i, :], x3[:, i, :], D, ssum[:, i:i + 1])
            act.wait_ge(ab_ok, 1)
            for i in range(TI):
                to_hT((ab[:, 0:8], ab[:, 8:16]), i, i + 1)
            act.wait_ge(colB_ok, 1)
            act.activation(colB[:, 120:128], colB[:, 0:8], ACT.Exp, scale=-1.0).then_inc(c2_e, 1)

            def unit_wait(u):
                act.wait_ge(unit_done[u % 2], u // 2 + 1)

            def unit_copy(u):
                q, half = u // 2, u % 2
                src = ps[:, u % 2, :]
                unit_wait(u)
                if q in (0, 4):
                    ins = act.copy(kT[q // 4][:, half * W5:(half + 1) * W5], src)
                elif q in (1, 5):
                    ins = act.mul(qT[q // 4][:, half * W5:(half + 1) * W5], src, QSCALE)
                else:
                    ins = act.copy(v3[q // 4][:, half, :], src)
                ins.then_inc(unit_free[u % 2], 1)

            def block_squares(i, n):
                act.wait_ge(x_ok, 2 * i + n + 1)
                if n_ms[0] > 2:
                    act.wait_ge(ms_done, n_ms[0])
                o = 4 + 4 * i + 2 * n
                squares(JA, x3[:, i, n * W5:(n + 1) * W5], D, ssum[:, o:o + 1])
                squares(JB, xn3[:, i, n * W5:(n + 1) * W5], D, ssum[:, o + 1:o + 2])

            def stick_soft(h):
                z = zb(zS, h % 2)
                act.wait_ge(st_zc, h + 1)
                link(act.activation(z, z, ACT.Exp))
                act.activation(z, z, ACT.Ln, bias=1.0).then_inc(st_ln, 1)

            def stick_weight(h):
                act.wait_ge(st_c, h + 1)
                if h >= 2:
                    act.wait_ge(st_pv, h - 1)
                act.activation(zb(Pb, h % 2), Z(h % 2), ACT.Exp).then_inc(st_w, 1)

            def soft_exp(k, b, pt_done):
                act.wait_ge(fx_m, k + 1)
                if pt_done is not None:
                    act.wait_ge(tr_done, pt_done)
                z, p = zb(zS, b), zb(Pb, b)
                act.activation(p[:, 0:P], z[:, 0:P], ACT.Exp, bias=MX[:, 16 + 2 * b:17 + 2 * b],
                               accum_out=SM[:, sm(k):sm(k) + 1])
                act.activation(p[:, P:384], z[:, P:384], ACT.Exp, bias=MX[:, 17 + 2 * b:18 + 2 * b],
                               accum_out=SM[:, sm(k) + 1:sm(k) + 2]).then_inc(fx_p, 1)

            def sm(k):
                return 2 * k if k < 8 else 16 + 2 * (k % 2)

            trs = [0]

            def p_copy(b, pv_need):
                act.wait_ge(tr_done, trs[0] + 1)
                if pv_need:
                    act.wait_ge(fx_pv, pv_need)
                act.copy(zb(PT, b), ps[:, 4, 0:384]).then_inc(tr_free, 1)
                trs[0] += 1

            fox_trd = {}
            for u in range(26):
                if u < 24:
                    q = u // 2
                    if q in (0, 1, 2, 4, 5, 6):
                        unit_copy(u)
                    elif q in (3, 7):
                        unit_wait(u)
                        act.activation(sz3[q // 4][:, u % 2, :], ps[:, u % 2, :], ACT.Exp, scale=-1.0).then_inc(e_sig, 1)
                    else:
                        act.wait_ge(unit_free[u % 2], u // 2 + 1)
                        gq = g3[:, u % 2, (q - 8) * W5:(q - 7) * W5]
                        act.activation(gq, gq, ACT.Exp, scale=-1.0).then_inc(e_sig, 1)
                if u == 0:
                    act.wait_ge(f_e, 1)
                    link(act.activation(fl[:, 32:48], fl[:, 32:48], ACT.Exp))
                    act.activation(fl[:, 32:48], fl[:, 32:48], ACT.Ln, bias=1.0).then_inc(f_l, 1)
                if 0 <= u - 4 < H:
                    stick_soft(u - 4)
                if 0 <= u - 5 < H:
                    stick_weight(u - 5)
                if u in (14, 15):
                    act.wait_ge(tr_done, trs[0] + 1)
                    act.copy(yT3[0][:, :, (u - 14) * P:(u - 13) * P],
                             ps[:, 4, :].rearrange("p (c t) -> p c t", c=4)).then_inc(tr_free, 1)
                    trs[0] += 1
                if 0 <= u - 14 < H:
                    k = u - 14
                    if k == 0:
                        act.wait_ge(st_pv, 8)
                    soft_exp(k, k % 2, fox_trd[k - 2] if k >= 2 else None)
                if 0 <= u - 15 < H:
                    k = u - 15
                    fox_trd[k] = trs[0] + 1
                    p_copy(k % 2, k - 1 if k >= 2 else 0)
            for i in range(TI):
                act.wait_ge(tr_done, trs[0] + 1)
                act.copy(yT3[1][:, :, i * P:(i + 1) * P],
                         ps[:, 4, :].rearrange("p (c t) -> p c t", c=4)).then_inc(tr_free, 1)
                trs[0] += 1
            for i in range(TI):
                to_hT(None, i, 3 + i)
            for n in range(2):
                block_squares(0, n)
            block_squares(1, 0)
            to_hT((ab[:, 16:24], ab[:, 24:32]), 0, 5)
            block_squares(1, 1)
            u0 = 36
            for i in range(TI):
                for k in range(3):
                    u = u0 + 3 * i + k
                    unit_wait(u)
                    src = ps[:, u % 2, :]
                    if k == 0:
                        s4 = src[:, 0:256].rearrange("p (kv g d) -> p kv g d", kv=2, g=2)
                        for a in range(2):
                            for kv in range(2):
                                act.copy(kvd6[:, i, kv, :, a, :], s4[:, kv, :, :])
                        act.copy(vS4[:, 0, i, :], src[:, 384:512]).then_inc(cp_v, 1)
                        act.copy(QK4[:, i, 8:10, :], src[:, 256:384].rearrange("p (h d) -> p h d", h=2)) \
                            .then_inc(unit_free[u % 2], 1)
                        if i == 0:
                            to_hT((ab[:, 16:24], ab[:, 24:32]), 1, 6)
                    elif k == 1:
                        act.copy(vS4[:, 1, i, :], src[:, 128:256])
                        act.copy(QK4[:, i, 10:12, :], src[:, 0:128].rearrange("p (h d) -> p h d", h=2))
                        act.activation(G3[:, i * 24:(i + 1) * 24], src[:, 256:280], ACT.Exp, scale=-1.0) \
                            .then_inc(unit_free[u % 2], 1)
                    else:
                        for g in range(2):
                            ins = act.copy(QK4[:, i, g:8:2, :],
                                           src[:, g * 256:(g + 1) * 256].rearrange("p (m d) -> p m d", m=4))
                        ins.then_inc(unit_free[u % 2], 1)
                        act.wait_ge(unit_free[u % 2], u // 2 + 1)
                        act.wait_ge(unit_free[(u - 1) % 2], (u - 1) // 2 + 1)
                        act.activation(xn3[:, i, 0:768], QK[:, i * 768:(i + 1) * 768], ACT.Square,
                                       scale=HD ** -0.5).then_inc(sq_ok, 1)

            def qk_copy(i):
                act.wait_ge(tr_done, trs[0] + 1)
                act.activation(qkT3[:, 0:4, i * P:(i + 1) * P], ps[:, 4, :].rearrange("p (c t) -> p c t", c=4),
                               ACT.Copy, scale=colB[:, 117:118]).then_inc(tr_free, 1)
                act.wait_ge(tr_done, trs[0] + 2)
                for c in range(2):
                    ins = act.activation(qkT3[:, 4 + c, i * P:(i + 1) * P], ps[:, 4, c * P:(c + 1) * P],
                                         ACT.Copy, scale=colB[:, 114 + c:115 + c])
                ins.then_inc(tr_free, 1)
                trs[0] += 2

            qk_copy(0)
            qk_copy(1)
            attn_trd = {}
            for w in range(10):
                if 2 <= w < 8:
                    k, i = (w - 2) // 2, w % 2
                    u = 42 + w - 2
                    if k != 1:
                        unit_wait(u)
                        act.copy((cu3, None, bgt3)[k][:, i, :], ps[:, u % 2, :]).then_inc(unit_free[u % 2], 1)
                if 0 <= w - 1 < 8:
                    for a in range(2):
                        v = 2 * (w - 1) + a
                        attn_trd[v] = trs[0] + 1
                        p_copy(a, 8 + v - 1)
                if w < 8:
                    for a in range(2):
                        soft_exp(8 + 2 * w + a, a, attn_trd.get(2 * (w - 1) + a))
                if w == 1:
                    act.wait_ge(cp_h, 2)
                    act.activation(HE[0:32, :], ps[0:32, 7, :], ACT.Exp, scale=-1.0).then_inc(cp_e, 1)
                if w == 2:
                    act.wait_ge(tr_done, trs[0] + 1)
                    act.wait_ge(pad_ok, 4)
                    for c in range(2):
                        act.copy(HTk3[:, c, :], ps[:, 4, c * 32:(c + 1) * 32])
                        for r in range(4):
                            ins = act.copy(HTv5[:, c, :, r, 0:16],
                                           ps[:, 4, (2 + c) * 32:(3 + c) * 32].rearrange("p (g n) -> p g n", g=2))
                    ins.then_inc(tr_free, 1)
                    trs[0] += 1
                if w == 4:
                    act.wait_ge(tr_done, trs[0] + 1)
                    act.activation(kcT, ps[:, 4, 0:16], ACT.Copy, scale=colB[:, 113:114]).then_inc(tr_free, 1)
                    trs[0] += 1
                if w == 5:
                    act.wait_ge(cp_s, 1)
                    act.activation(Pc4[:, :, :, 0:16], Sc4, ACT.Exp).then_inc(cp_x, 1)
                if w == 7:
                    act.wait_ge(tr_done, trs[0] + 1)
                    act.copy(PcT, ps[:, 4, :]).then_inc(tr_free, 1)
                    trs[0] += 1
            for i in range(TI):
                act.wait_ge(att_ok, i + 1)
                act.activation(hT[:, D + i * W5:D + (i + 1) * W5], xn3[:, i, W5:D], ACT.Square,
                               scale=HD ** -0.5).then_inc(sq_ok, 1)
            act.wait_ge(cp_p, 1)
            for i in range(TI):
                act.activation(hT[:, i * W5:(i + 1) * W5], ps[:, 5 + i, :], ACT.Square,
                               scale=HD ** -0.5).then_inc(sq_ok, 1)
            for i in range(TI):
                to_hT((colB[:, 72:80], None), i, 9 + i, (5, 6))
            for i in range(TI):
                for n in range(2):
                    act.wait_ge(x_ok, 4 + 2 * i + n + 1)
                    act.wait_ge(ms_done, n_ms[0])
                    squares(JA, x3[:, i, n * W5:(n + 1) * W5], D, ssum[:, 12 + 2 * i + n:13 + 2 * i + n])
                    if i == 1 and n == 0:
                        to_hT((ab[:, 32:40], ab[:, 40:48]), 0, 11)
            to_hT((ab[:, 32:40], ab[:, 40:48]), 1, 12)
            act.wait_ge(r_s, 1)
            act.activation(rG[:, 0:16], rG[:, 0:16], ACT.Exp).then_inc(r_e, 1)
            act.wait_ge(r_s, 2)
            act.activation(rt[:, 8:10], rt[:, 6:8], ACT.Exp).then_inc(r_e, 1)
            act.wait_ge(ids_ok, 1)

            def round_(it):
                act.wait_ge(m_d, it + 1)
                for c in range(4):
                    ins = act.activation(xe3[:, c, :], ps[:, 4, c * P:(c + 1) * P], ACT.Identity,
                                   scale=ab[:, 32 + c:33 + c], bias=ab[:, 40 + c:41 + c])
                ins.then_inc(m_xe, 1)
                act.wait_ge(mring_free, it * STAGES + 8)
                act.activation(hE, ps[:, 0, :], ACT.Exp, scale=-1.0).then_inc(m_e, 1)
                act.wait_ge(m_at, it + 1)
                act.copy(actT, ps[:, 6, :]).then_inc(m_atc, 1)

            with act.Fori(0, MAIN) as it:
                round_(it)
            n_over = act.value_load(ids[0:1, 16:17], min_val=0, max_val=16)
            with act.If(n_over > 0):
                with act.Fori(MAIN, ROUNDS) as it:
                    round_(it)

        @block.vector
        def _(dve):
            n_ch = [0]

            def link(ins):
                n_ch[0] += 1
                ins.then_inc(dve_ch, 1)
                dve.wait_ge(dve_ch, n_ch[0])

            def bc(ap, n):
                return bass.AP(tensor=ap.tensor, offset=ap.offset, ap=list(ap.ap) + [[0, n]])

            norm_k = [0]

            def root(mean, scale=1.0):
                (w, parts), o = NRM[norm_k[0]], NO[norm_k[0]]
                norm_k[0] += 1
                v, r, tm = (a[0:parts, o:o + w] for a in (VA, RS, TM))
                if mean is not None:
                    link(dve.tensor_scalar(v, mean, scale, EPS, ALU.mult, ALU.add))
                link(dve.tensor_scalar(tm.bitcast(I32), v.bitcast(I32), 1, None, ALU.logical_shift_right))
                link(dve.tensor_scalar(r.bitcast(I32), tm.bitcast(I32), -1.0, float(0x5f3759df), ALU.mult, ALU.add))
                for _ in range(3):
                    link(dve.scalar_tensor_tensor(tm, r, -0.5, r, ALU.mult, ALU.mult))
                    link(dve.tensor_tensor(tm, tm, v, ALU.mult))
                    link(dve.scalar_tensor_tensor(r, tm, 1.5, r, ALU.add, ALU.mult))
                return r

            def to_hT(a, i, k, bank=(3, 6)):
                dve.wait_ge(xt_done, k)
                for c in range(4, DC):
                    dst, src = hT3[:, c, i * P:(i + 1) * P], ps[:, bank[i], (c - 4) * P:(c - 3) * P]
                    if a is None:
                        ins = dve.tensor_copy(dst, src)
                    elif a[1] is None:
                        ins = dve.tensor_scalar(dst, src, a[0][:, c:c + 1], None, ALU.mult)
                    else:
                        ins = dve.tensor_scalar(dst, src, a[0][:, c:c + 1], a[1][:, c:c + 1], ALU.mult, ALU.add)
                ins.then_inc(htv_done, 1)

            dve.wait_ge(cols_tr, 1)
            link(dve.tensor_copy(colA[:], ps[:, 7, 0:40]))
            dve.tensor_copy(c32[:, 0:256].rearrange("p (c n) -> p c n", c=DC), bc(colA[:, 0:8], 32)).then_inc(c1_ok, 1)
            dve.wait_ge(ms_done, 2)
            r = root(ssum[:, 0:2])
            for i in range(TI):
                dve.tensor_scalar(xn3[:, i, :], x3[:, i, :], r[:, i:i + 1], None, ALU.mult).then_inc(xn_done, 1)
            for n in range(4):
                if n == 3:
                    dve.wait_ge(cols_tr, 2)
                    dve.tensor_copy(colB[:, 0:116], ps[:, 7, 0:116]).then_inc(colB_ok, 1)
                dve.wait_ge(mod_raw, n + 1)
                if n:
                    dve.wait_ge(ab_done, n)
                dve.tensor_copy(modt[:], ps[:, 4, :]).then_inc(mod_ok, 1)
            dve.wait_ge(ab_done, 4)
            dve.tensor_tensor(ab[:, 8:16], ps[:, 0, 0:8], colA[:, 8:16], ALU.add)
            link(dve.tensor_tensor(ab[:, 0:8], ps[:, 0, 8:16], colA[:, 16:24], ALU.add))
            dve.scalar_tensor_tensor(ab[:, 0:8], ab[:, 0:8], 1.0, colA[:, 32:40], ALU.add, ALU.mult).then_inc(ab_ok, 1)
            dve.wait_ge(ab_ok, 1)
            for i in range(TI):
                to_hT((ab[:, 0:8], ab[:, 8:16]), i, i + 1)
            dve.wait_ge(colB_ok, 1)
            dve.tensor_scalar(colB[:, 117:118], colB[:, 112:113], QSCALE, None, ALU.mult)
            dve.wait_ge(c2_e, 1)
            link(dve.tensor_scalar(colB[:, 120:128], colB[:, 120:128], 1.0, None, ALU.add))
            link(dve.reciprocal(colB[:, 120:128], colB[:, 120:128]))
            dve.tensor_tensor(colB[:, 120:128], colB[:, 120:128], colB[:, 0:8], ALU.mult).then_inc(c2_ok, 1)

            def unit_wait(u):
                dve.wait_ge(unit_done[u % 2], u // 2 + 1)

            def sigmoid_tail(e):
                link(dve.tensor_scalar(e, e, 1.0, None, ALU.add))
                link(dve.reciprocal(e, e))

            def stick_log(h):
                b = h % 2
                dve.wait_ge(st_z, h + 1)
                if h >= 1:
                    dve.wait_ge(st_L, h)
                dve.tensor_scalar(zb(zS, b), Z(b), 40.0, None, ALU.min).then_inc(st_zc, 1)
                link(dve.tensor_scalar(R[:], Z(b), 40.0, -40.0, ALU.max, ALU.add))
                dve.wait_ge(st_ln, h + 1)
                if h >= 2:
                    dve.wait_ge(st_c, h - 1)
                dve.scalar_tensor_tensor(zb(PT, b), zb(zS, b), -1.0, R[:], ALU.mult, ALU.subtract).then_inc(st_L, 1)

            def row_max(k, b, bias0, bias1):
                dve.wait_ge(fx_z, k + 1)
                if k >= 2:
                    dve.wait_ge(fx_p, k - 1)
                z = zb(zS, b)
                dve.tensor_tensor_reduce(z[:, 0:P], ps[:, 2 + b, 0:P], bias0, 1.0, -3e38, ALU.add, ALU.max,
                                         MX[:, 2 * b:2 * b + 1])
                link(dve.tensor_tensor_reduce(z[:, P:384], ps[:, 2 + b, P:384], bias1, 1.0, -3e38, ALU.add, ALU.max,
                                              MX[:, 2 * b + 1:2 * b + 2]))
                dve.tensor_scalar(MX[:, 16 + 2 * b:18 + 2 * b], MX[:, 2 * b:2 * b + 2], -1.0, None, ALU.mult) \
                    .then_inc(fx_m, 1)

            def gate_raw():
                dve.wait_ge(misc_done, misc[0] + 1)
                dve.tensor_copy(modt[:], ps[:, 7, :]).then_inc(misc_free, 1)
                misc[0] += 1

            def mod_row(o):
                dve.wait_ge(misc_done, misc[0] + 1)
                dve.tensor_tensor(grow[:, o:o + W5], grow[:, o:o + W5], ps[:, 7, :], ALU.add).then_inc(misc_free, 1)
                misc[0] += 1

            def mod2_part(q, half):
                n = mod2(q)
                if half == 0:
                    dve.wait_ge(ring_in[n % RING], 16 * (n // RING + 1))
                for c in range(4 * half, 4 * half + 4):
                    w, col = cview(n)[:, c, :], colB[:, 120 + c:121 + c]
                    if c == 0:
                        link(dve.tensor_scalar(mod2p[:], w, col, None, ALU.mult))
                    else:
                        ins = dve.scalar_tensor_tensor(mod2p[:], w, col, mod2p[:], ALU.mult, ALU.add)
                        if c < DC - 1:
                            link(ins)
                        else:
                            ins.then_inc(mod2_sum, 1)
                            dve.wait_ge(mod2_sum, q + 1)

            misc = [0]
            dve.wait_ge(c2_ok, 1)
            for u in range(26):
                q = u // 2
                if u == 0:
                    dve.wait_ge(misc_done, 1)
                    dve.wait_ge(ld_small, 16 * 8)
                    f2 = fl[:, 0:16].rearrange("p (i h) -> p i h", i=2)
                    b2 = bass.AP(tensor=bfr[:].tensor, offset=bfr[:].offset, ap=[bfr[:].ap[0], [0, 2], [1, 8]])
                    dve.tensor_tensor(f2, ps[:, 7, 0:16].rearrange("p (i h) -> p i h", i=2), b2,
                                      ALU.add).then_inc(misc_free, 1)
                    misc[0] += 1
                    dve.wait_ge(misc_free, 1)
                    link(dve.tensor_scalar(fl[:, 16:32], fl[:, 0:16], -1.0, None, ALU.mult))
                    dve.tensor_tensor(fl[:, 32:48], fl[:, 0:16], fl[:, 16:32], ALU.min).then_inc(f_e, 1)
                    dve.wait_ge(f_l, 1)
                    dve.scalar_tensor_tensor(fl[:, 48:64], fl[:, 0:16], 0.0, fl[:, 32:48], ALU.min,
                                             ALU.subtract).then_inc(f_lf, 1)
                if 16 <= u < 24:
                    unit_wait(u)
                    if u == 16:
                        dve.wait_ge(ld_bg, 32)
                    gq = g3[:, u % 2, (q - 8) * W5:(q - 7) * W5]
                    dve.tensor_tensor(gq, ps[:, u % 2, :], bg[:, (q - 8) * W5:(q - 7) * W5],
                                      ALU.add).then_inc(unit_free[u % 2], 1)
                if u % 2 == 1 and 3 <= u < 3 + 2 * MODQ:
                    k = u // 2 - 1
                    if k == 4:
                        dve.wait_ge(ld_grow, 48)
                    if k in (4, 5):
                        mod_row(D + (k - 4) * W5)
                    else:
                        dve.wait_ge(misc_done, misc[0] + 1)
                        dve.tensor_tensor(mod2c[:, 4 * k:4 * k + 4], ps[:, 7, 0:4], colB[:, 8 + 4 * k:12 + 4 * k],
                                          ALU.add).then_inc(misc_free, 1)
                        misc[0] += 1
                if 0 <= u - 4 < H:
                    stick_log(u - 4)
                if 0 <= u - 14 < H:
                    row_max(u - 14, u % 2, cst[:, C_NM + P:C_NM + 256], cst[:, C_NM:C_NM + 256])
                if u in (6, 7, 14, 15):
                    s = sz3[q // 4][:, u % 2, :]
                    dve.wait_ge(e_sig, (u - 5) if u < 8 else (u - 11))
                    sigmoid_tail(s)
                    dve.tensor_tensor(s, s, ps[:, u % 2, :], ALU.mult).then_inc(unit_free[u % 2], 1)
                if u == 13:
                    dve.wait_ge(st_pv, 8)
                    dve.wait_ge(unit_free[0], 4)
                    dve.wait_ge(unit_free[1], 4)
                    for i in range(TI):
                        dve.tensor_tensor(sz3[0][:, i, :], sz3[0][:, i, :], ps[:, 5 + i, :], ALU.mult).then_inc(ya_ok, 1)
                if u == 23:
                    dve.wait_ge(fx_pv, 8)
                    dve.wait_ge(unit_free[0], 8)
                    dve.wait_ge(unit_free[1], 8)
                    link(dve.reciprocal(CO[:, 0:16], SM[:, 0:16]))
                    for i in range(TI):
                        s = sz3[1][:, i, :]
                        link(dve.tensor_tensor(s, s, ps[:, 5 + i, :], ALU.mult))
                        s8 = s.rearrange("p (h d) -> p h d", h=H)
                        dve.tensor_tensor(s8, s8, bc(CO[:, i:16:2], HD), ALU.mult).then_inc(ya_ok, 1)
                if 16 <= u < 22:
                    dve.wait_ge(e_sig, u - 11)
                    sigmoid_tail(g3[:, u % 2, (q - 8) * W5:(q - 7) * W5])
                if 1 <= u <= 2 * MODQ:
                    mod2_part((u - 1) // 2, (u - 1) % 2)
            for o, sh, sc, g in ((16, 0, 8, 56), (32, 24, 32, 64)):
                dve.tensor_copy(ab[:, o + 8:o + 16], mod2c[:, sh:sh + 8])
                link(dve.scalar_tensor_tensor(ab[:, o:o + 8], mod2c[:, sc:sc + 8], 1.0, colB[:, g:g + 8],
                                              ALU.add, ALU.mult))
            tmp = zS[:, 0:W5]
            for b in range(2):
                for i in range(TI):
                    for n in range(2):
                        u = 24 + 4 * b + 2 * i + n
                        if b == 0:
                            if n == 0:
                                gate_raw()
                            else:
                                mod_row(i * W5)
                        unit_wait(u)
                        if u in (28, 29):
                            lo, n_ = (0, W5) if u == 28 else (W5, BM - W5)
                            dve.wait_ge(misc_done, misc[0] + 1)
                            dve.tensor_copy(bR[:, lo:lo + n_], ps[0:8, 7, 0:n_]).then_inc(misc_free, 1)
                            misc[0] += 1
                        g = g3[:, i, b * D + n * W5:b * D + (n + 1) * W5]
                        m = mg3[:, i, n * W5:(n + 1) * W5]
                        if b == 0:
                            dve.tensor_tensor(m, g, ps[:, u % 2, :], ALU.mult).then_inc(unit_free[u % 2], 1)
                            if i == 1:
                                dve.wait_ge(e_sig, 11 + n)
                                sigmoid_tail(g3[:, n, 3 * W5:4 * W5])
                        else:
                            dve.tensor_tensor(tmp, g, ps[:, u % 2, :], ALU.mult).then_inc(unit_free[u % 2], 1)
                            dve.wait_ge(unit_free[u % 2], u // 2 + 1)
                            ins = dve.tensor_tensor(m, m, tmp, ALU.add)
                            if n == 1:
                                ins.then_inc(xn_done, 1)
                                dve.wait_ge(xn_done, 3 + i)
                            else:
                                link(ins)
                            if i == 1 and n == 0:
                                to_hT(None, 0, 3)

            def residual(u, o, i, n, done):
                unit_wait(u)
                dve.tensor_tensor(tmp, grow[:, o + n * W5:o + (n + 1) * W5], ps[:, u % 2, :],
                                  ALU.mult).then_inc(unit_free[u % 2], 1)
                dve.wait_ge(unit_free[u % 2], u // 2 + 1)
                xs = x3[:, i, n * W5:(n + 1) * W5]
                ins = dve.tensor_tensor(xs, xs, tmp, ALU.add)
                if done:
                    ins.then_inc(x_ok, 1)
                else:
                    link(ins)

            for i in range(TI):
                for n in range(2):
                    residual(32 + 2 * i + n, 0, i, n, False)
                    xs = x3[:, i, n * W5:(n + 1) * W5]
                    dve.tensor_tensor(xn3[:, i, n * W5:(n + 1) * W5], xs, fg[:, n * W5:(n + 1) * W5],
                                      ALU.mult).then_inc(x_ok, 1)
                    if i == n == 0:
                        to_hT(None, 1, 4)
                    if i == 1 and n == 0:
                        to_hT((ab[:, 16:24], ab[:, 24:32]), 0, 5)
                k, o = norm_k[0], NO[norm_k[0]]
                dve.wait_ge(ms_done, 2 + 4 * i + 4)
                q = 4 + 4 * i
                link(dve.tensor_tensor(MS[:, o:o + 2], ssum[:, q:q + 2], ssum[:, q + 2:q + 4], ALU.add))
                link(dve.tensor_scalar(VA[:, o:o + 1], MS[:, o:o + 1], EPS, None, ALU.add))
                link(dve.reciprocal(TM[:, o:o + 1], VA[:, o:o + 1]))
                link(dve.tensor_tensor(TM[:, o + 1:o + 2], MS[:, o + 1:o + 2], TM[:, o:o + 1], ALU.mult))
                link(dve.tensor_scalar(VA[:, o + 1:o + 2], TM[:, o + 1:o + 2], EPS, None, ALU.add))
                r = root(None)
                link(dve.tensor_scalar(x3[:, i, :], xn3[:, i, :], r[:, 0:1], None, ALU.mult))
                dve.tensor_scalar(xn3[:, i, :], x3[:, i, :], r[:, 1:2], None, ALU.mult).then_inc(xn_done, 1)
            to_hT((ab[:, 16:24], ab[:, 24:32]), 1, 6)

            def qk_norm(i):
                dve.wait_ge(sq_ok, i + 1)
                o = NO[norm_k[0]]
                link(dve.tensor_reduce(MS[:, o:o + 12], xn3[:, i, 0:768].rearrange("p (h d) -> p h d", d=HD), AX, ALU.add))
                r = root(MS[:, o:o + 12])
                dve.tensor_tensor(QK4[:, i], QK4[:, i], bc(r, HD), ALU.mult).then_inc(qk_ok, 1)

            qk_norm(0)
            dve.wait_ge(pad_ok, 1)
            dve.wait_ge(cp_T, 1)
            for kv in range(2):
                for a in range(2):
                    lo = 64 * a
                    src = ps[lo:lo + 64, 2 + kv, :]
                    pstep = src.ap[0]
                    t_in = bass.AP(tensor=src.tensor, offset=src.offset + a, ap=[pstep, [2, 16], [256, 2], [16, NCMP]])
                    pos = colB[lo:lo + 64, 80 + 16 * kv:96 + 16 * kv]
                    p_in = bass.AP(tensor=pos.tensor, offset=pos.offset, ap=[pos.ap[0], [1, 16], [0, 2], [0, NCMP]])
                    dve.tensor_tensor(X5[lo:lo + 64, kv, :, :, 0:NCMP], t_in, p_in, ALU.add).then_inc(cp_X, 1)
            qk_norm(1)
            dve.wait_ge(unit_free[0], 21)
            sigmoid_tail(G3)
            dve.wait_ge(ld_bias, 16)
            for w in range(10):
                if w in (4, 5):
                    u, i = 40 + w, w % 2
                    unit_wait(u)
                    dve.wait_ge(unit_free[u % 2], u // 2)
                    dve.tensor_tensor(cu3[:, i, :], cu3[:, i, :], ps[:, u % 2, :], ALU.mult).then_inc(unit_free[u % 2], 1)
                if w < 8:
                    for a in range(2):
                        row_max(8 + 2 * w + a, a, B[:, w, P:256], B[:, w, 0:256])
                    for a in range(2):
                        k = 8 + 2 * w + a
                        dve.wait_ge(fx_p, k + 1)
                        c2 = CO[:, 2 * a:2 * a + 2]
                        link(dve.reciprocal(c2, SM[:, 16 + 2 * a:18 + 2 * a]))
                        link(dve.tensor_tensor(c2, c2, G34[:, :, w, 1 + a], ALU.mult))
                        p_ = zb(Pb, a)
                        dve.tensor_scalar(p_[:, 0:P], p_[:, 0:P], c2[:, 0:1], None, ALU.mult)
                        dve.tensor_scalar(p_[:, P:384], p_[:, P:384], c2[:, 1:2], None, ALU.mult).then_inc(fx_sc, 1)
                if w in (5, 7):
                    mod_row(2 * D + (w // 7) * W5)
                if w == 1:
                    dve.wait_ge(cp_e, 1)
                    he = HE[0:32, :]
                    sigmoid_tail(he)
                    dve.tensor_tensor(Hh[0:32, :], he, ps[0:32, 7, :], ALU.mult).then_inc(cp_H, 1)
                if w == 3:
                    dve.wait_ge(cp_w2, 1)
                    dve.wait_ge(pad_ok, 4)
                    for r in range(4):
                        dve.tensor_copy(Vbd3[32 * r:32 * r + 32, :, r * HD:(r + 1) * HD],
                                        ps[32 * r:32 * r + 32, 7, P:256].rearrange("p (g d) -> p g d", g=2))
                    link(dve.tensor_copy(kc[0:16, :], ps[0:16, 7, 0:P]))
                    link(dve.tensor_tensor(HE[0:16, 0:P], kc[0:16, :], kc[0:16, :], ALU.mult))
                    o = NO[norm_k[0]]
                    link(dve.tensor_reduce(MS[0:16, o:o + 2], HE[0:16, 0:P].rearrange("p (g d) -> p g d", g=2), AX, ALU.add))
                    r = root(MS[0:16, o:o + 2], 1.0 / HD)
                    k3 = kc[0:16, :].rearrange("p (g d) -> p g d", g=2)
                    dve.tensor_tensor(k3, k3, bc(r, HD), ALU.mult).then_inc(cp_k, 1)
                if w == 5:
                    dve.wait_ge(cp_z, 2)
                    for i in range(TI):
                        f0 = 31 + P * (1 - i)
                        ins = dve.tensor_tensor(Sc4[:, i, :, :],
                                                ps[:, 7, i * P:(i + 1) * P].rearrange("p (h n) -> p h n", h=H),
                                                B[:, :, f0:f0 + 241:16], ALU.add)
                    link(ins)
                    Sf = Sc.rearrange("p (h n) -> p h n", n=16)
                    link(dve.tensor_reduce(cm[:, 0:16], Sf, AX, ALU.max))
                    link(dve.tensor_scalar(cm[:, 0:16], cm[:, 0:16], -1e20, None, ALU.max))
                    dve.tensor_tensor(Sf, Sf, bc(cm[:, 0:16], 16), ALU.subtract).then_inc(cp_s, 1)
                if w in (3, 4, 5, 6):
                    mod2_part(10 + (w - 3) // 2, (w - 3) % 2)
                if w == 6:
                    dve.wait_ge(cp_x, 1)
                    c16 = cm[:, 16:32]
                    Pf = Pc.rearrange("p (h n) -> p h n", n=32)[:, :, 0:16]
                    link(dve.tensor_reduce(c16, Pf, AX, ALU.add))
                    link(dve.tensor_scalar(c16, c16, 1e-30, None, ALU.max))
                    link(dve.reciprocal(c16, c16))
                    link(dve.tensor_tensor(c16, c16, G3[:, 0:48:3], ALU.mult))
                    dve.tensor_tensor(Pf, Pf, bc(c16, 16), ALU.mult).then_inc(cp_n, 1)
            for i in range(TI):
                u = 48 + i
                unit_wait(u)
                dve.wait_ge(cv_w2, i + 1)
                yc = xn3[:, i, W5:D]
                dve.tensor_tensor(yc, ps[:, u % 2, :], cwp[2][:, i, :], ALU.add).then_inc(unit_free[u % 2], 1)
                dve.wait_ge(unit_free[u % 2], u // 2 + 1)
                dve.tensor_tensor(yc, yc, bgt3[:, i, :], ALU.mult).then_inc(att_ok, 1)
            for half in (1, 0):
                dve.wait_ge(sq_ok, 4 if half else 6)
                o = NO[norm_k[0]]
                link(dve.tensor_reduce(MS[:, o:o + 16], hT[:, half * D:(half + 1) * D].rearrange("p (h d) -> p h d", d=HD),
                                       AX, ALU.add))
                r = root(MS[:, o:o + 16])
                for i in range(TI):
                    dst = xn3[:, i, half * W5:(half + 1) * W5].rearrange("p (h d) -> p h d", d=HD)
                    src = dst if half else ps[:, 5 + i, :].rearrange("p (h d) -> p h d", d=HD)
                    dve.tensor_tensor(dst, src, bc(r[:, i * H:(i + 1) * H], HD), ALU.mult).then_inc(xn_done, 1)
            for i in range(TI):
                to_hT((colB[:, 72:80], None), i, 7 + i, (2, 3))
            for i in range(TI):
                for n in range(2):
                    residual(50 + 2 * i + n, D, i, n, True)
                    dve.wait_ge(x_ok, 4 + 2 * i + n + 1)
                    if i == 1 and n == 0:
                        to_hT((ab[:, 32:40], ab[:, 40:48]), 0, 11)
                dve.wait_ge(ms_done, 10 + 2 * i + 2)
                o = NO[norm_k[0]]
                q = 12 + 2 * i
                link(dve.tensor_tensor(MS[:, o:o + 1], ssum[:, q:q + 1], ssum[:, q + 1:q + 2], ALU.add))
                r = root(MS[:, o:o + 1])
                dve.tensor_scalar(xn3[:, i, :], x3[:, i, :], r, None, ALU.mult).then_inc(xn_done, 1)
            to_hT((ab[:, 32:40], ab[:, 40:48]), 1, 12)
            L3 = rL.rearrange("p (i n) -> p i n", i=2)
            E3 = rE.rearrange("p (i e) -> p i e", i=2)
            E4 = rE.rearrange("p (i g e) -> p i g e", i=2, g=8)
            O1 = rO1.rearrange("p (i e) -> p i e", i=2)
            O2 = rO2.rearrange("p (i e) -> p i e", i=2)
            P3 = rP.rearrange("p (i e) -> p i e", i=2)
            G2 = rG[:, 0:16].rearrange("p (i g) -> p i g", i=2)
            OG = rG[:, 16:32].rearrange("p (i g) -> p i g", i=2)
            PG = rG[:, 32:48].rearrange("p (i g) -> p i g", i=2)
            T3 = rT.rearrange("p (i e) -> p i e", i=2)

            def rb(ap, n):
                return bass.AP(tensor=ap.tensor, offset=ap.offset, ap=[ap.ap[0], [0, 2], [1, n]])

            def first_max(dst3, src3, desc, n, mx, scratch3):
                link(dve.tensor_reduce(mx, src3, AX, ALU.max))
                link(dve.tensor_tensor(scratch3, src3, bc(mx, n), ALU.is_equal))
                link(dve.tensor_tensor(scratch3, scratch3, rb(desc, n), ALU.mult))
                link(dve.tensor_reduce(rt[:, 30:32], scratch3, AX, ALU.max))
                link(dve.tensor_tensor(dst3, scratch3, bc(rt[:, 30:32], n), ALU.is_equal))

            dve.wait_ge(r_lg, 1)
            link(dve.tensor_tensor(L3, ps[:, 7, 0:144].rearrange("p (i n) -> p i n", i=2), rb(br[:, 0:72], 72), ALU.add))
            first_max(OG, L3[:, :, 0:8], cst[:, C_D8:C_D8 + 8], 8, rt[:, 0:2], PG)
            dve.tensor_tensor(G2, L3[:, :, 0:8], bc(rt[:, 0:2], 8), ALU.subtract).then_inc(r_s, 1)
            link(dve.tensor_scalar(PG, OG, -NEG, NEG, ALU.mult, ALU.add))
            for i in range(TI):
                e3 = L3[:, i, 8:72].rearrange("p (g e) -> p g e", g=8)
                link(dve.tensor_tensor(E4[:, i], e3, bc(OG[:, i, :], 8), ALU.mult))
                link(dve.tensor_tensor(E4[:, i], E4[:, i], bc(PG[:, i, :], 8), ALU.add))
            first_max(O1, E3, cst[:, C_D64:C_D64 + 64], 64, rt[:, 2:4], T3)
            link(dve.scalar_tensor_tensor(rE, rO1, -3e30, rE, ALU.mult, ALU.add))
            first_max(O2, E3, cst[:, C_D64:C_D64 + 64], 64, rt[:, 4:6], T3)
            dve.tensor_tensor(rA, rO1, rO2, ALU.add).then_inc(r_A, 1)
            dve.tensor_tensor(rt[:, 6:8], rt[:, 4:6], rt[:, 2:4], ALU.subtract).then_inc(r_s, 1)
            dve.wait_ge(r_e, 2)
            link(dve.tensor_reduce(rt[:, 10:12], G2, AX, ALU.add))
            link(dve.tensor_scalar(rt[:, 12:14], rt[:, 8:10], 1.0, None, ALU.add))
            link(dve.tensor_tensor(rt[:, 10:12], rt[:, 10:12], rt[:, 12:14], ALU.mult))
            link(dve.reciprocal(rt[:, 14:16], rt[:, 10:12]))
            link(dve.tensor_tensor(rt[:, 16:18], rt[:, 14:16], rt[:, 8:10], ALU.mult))
            dve.wait_ge(r_rk, 1)
            link(dve.tensor_copy(rt[0:64, 20:21], ps[0:64, 7, 128:129]))
            link(dve.tensor_scalar(rt[0:64, 22:30], cst[0:64, C_THR:C_THR + 8], rt[0:64, 20:21], None, ALU.is_lt))
            link(dve.tensor_reduce(rt[0:64, 21:22], rt[0:64, 22:30], AX, ALU.add))
            dve.tensor_scalar(nb128[0:64, :], cst[0:64, C_ONE:C_ONE + P], rt[0:64, 21:22], None, ALU.mult).then_inc(r_nb, 1)
            link(dve.tensor_copy(rP, ps[:, 7, 0:128]))
            dve.wait_ge(r_st, 1)
            e32 = T3[:, 0, :]
            link(dve.tensor_scalar(e32, cst[:, C_D64:C_D64 + 64], -float(SLOTS), float(SLOTS * NE), ALU.mult, ALU.add))
            link(dve.scalar_tensor_tensor(T3[:, 1, :], ps[:, 4, 192:256], float(SLOTS), e32, ALU.mult, ALU.subtract))
            link(dve.tensor_scalar(T3[:, 1, :], T3[:, 1, :], float(SLOTS * (NE - 1)), None, ALU.add))
            link(dve.tensor_copy(rt[0:64, 20:21], ps[0:64, 4, 257:258]))
            dve.tensor_scalar(cmpi[0:64, 0:16], cst[0:64, C_IOTA:C_IOTA + 16], rt[0:64, 20:21], None,
                              ALU.is_ge).then_inc(r_ci, 1)
            link(dve.tensor_scalar(rE, rP, float(SLOTS), None, ALU.is_ge))
            link(dve.tensor_tensor(E3, E3, rb(T3[:, 1, :], 64), ALU.mult))
            link(dve.tensor_tensor(rP, rP, rE, ALU.add))
            link(dve.tensor_tensor(P3, P3, rb(e32, 64), ALU.add))
            for o, dst in ((rO1, rQ[:, 0:2]), (rO2, rQ[:, 2:4])):
                link(dve.tensor_tensor(rE, o, rP, ALU.mult))
                link(dve.tensor_reduce(dst, E3, AX, ALU.add))
            dve.wait_ge(r_it, 1)
            link(dve.tensor_scalar(ids[0:1, 0:16], ps[0:1, 5, 0:16], float(NE - 1), None, ALU.min))
            dve.tensor_copy(ids[0:1, 16:17], ps[0:1, 4, 256:257]).then_inc(ids_ok, 1)

            LINKS = 11

            def round_(it):
                j = [0]

                def link_(ins):
                    j[0] += 1
                    ins.then_inc(m_ch, 1)
                    dve.wait_ge(m_ch, it * LINKS + j[0])

                iota = cc(C_IOTA)
                p1, p2 = ([rQ[:, 2 * k + i:2 * k + i + 1] for i in range(TI)] for k in range(2))
                for i in range(TI):
                    ins = dve.tensor_scalar(sel3[:, i, :], iota, p1[i], None, ALU.is_equal)
                link_(ins)
                for i in range(TI):
                    ins = dve.scalar_tensor_tensor(sel3[:, i, :], iota, p2[i], sel3[:, i, :], ALU.is_equal, ALU.add)
                ins.then_inc(m_sel, 1)
                for i in range(TI):
                    dve.tensor_scalar(wsel3[:, i, :], iota, p1[i], rt[:, 14 + i:15 + i], ALU.is_equal, ALU.mult)
                    link_(dve.tensor_scalar(rT, iota, p2[i], rt[:, 16 + i:17 + i], ALU.is_equal, ALU.mult))
                    ins = dve.tensor_tensor(wsel3[:, i, :], wsel3[:, i, :], rT, ALU.add)
                    if i == 0:
                        link_(ins)
                    else:
                        ins.then_inc(m_wsel, 1)
                dve.wait_ge(m_d, it + 1)
                for c in range(4, DC):
                    ins = dve.tensor_scalar(xe3[:, c, :], ps[:, 5, (c - 4) * P:(c - 3) * P], ab[:, 32 + c:33 + c],
                                            ab[:, 40 + c:41 + c], ALU.mult, ALU.add)
                ins.then_inc(m_xe, 1)
                dve.wait_ge(m_wt, it + 1)
                dve.tensor_copy(wc, ps[:, 6, 0:256]).then_inc(m_wc, 1)
                dve.wait_ge(m_e, it + 1)
                link_(dve.tensor_scalar(hE, hE, 1.0, None, ALU.add))
                link_(dve.reciprocal(hE, hE))
                link_(dve.tensor_tensor(hE, hE, ps[:, 0, :], ALU.mult))
                dve.tensor_tensor(hA, hE, ps[:, 1, :], ALU.mult).then_inc(m_a, 1)
                dve.wait_ge(mring_free, it * STAGES + STAGES)
                dve.tensor_tensor(ye, ps[:, 2:4, :].rearrange("p a b -> p (a b)"), grow[:, 2 * D:3 * D],
                                  ALU.mult).then_inc(m_ye, 1)
                for k in range(4):
                    dve.wait_ge(m_cb, it * 4 + (k + 1))
                    a_ = x3[:, k // 2, (k % 2) * W5:(k % 2 + 1) * W5]
                    ins = dve.tensor_tensor(a_, a_, ps[:, (7, 6, 4, 5)[k], :], ALU.add)
                    if k < 3:
                        link_(ins)
                    else:
                        ins.then_inc(m_cbf, 1)
                link_(dve.tensor_scalar(rQ[:, 0:4], rQ[:, 0:4], float(-P), None, ALU.add))
                dve.wait_ge(m_cbf, it + 1)
                assert j[0] == LINKS

            with dve.Fori(0, MAIN) as it:
                round_(it)
            n_over = dve.value_load(ids[0:1, 16:17], min_val=0, max_val=16)
            with dve.If(n_over > 0):
                with dve.Fori(MAIN, ROUNDS) as it:
                    round_(it)

        @block.gpsimd
        def _(pool):
            rw = [(0, t["c_2"]), (8, t["b_ada_2"]), (56, t["norm1_w_2"]), (64, t["norm2_w_2"]), (72, t["out_norm_w_2"])]
            for r, a in rw:
                n = a.shape[1] // P
                pool.dma_start(rowsB[r:r + n, :], a.rearrange("o (c p) -> (o c) p", p=P)).then_inc(ld_rowsB, 16)
            for r, a in ((80, t["cmp_pos_k_2"]), (96, t["cmp_pos_v_2"])):
                pool.dma_start(rowsB[r:r + 16, :], a[0].rearrange("(j a) d -> j (a d)", a=2)).then_inc(ld_rowsB, 16)
            for a in range(2):
                pool.dma_start(rowsB[112:113, a * HD:(a + 1) * HD], t["q_norm_w_2"]).then_inc(ld_rowsB, 16)
                pool.dma_start(rowsB[113:116, a * HD:(a + 1) * HD], t["k_norm_w_2"][0]).then_inc(ld_rowsB, 16)
            pool.dma_start(bfr[:], rows(t["b_forget"], 0, 8)).then_inc(ld_small, 16)
            pool.dma_start(wf[:].rearrange("p (c n) -> p c n", c=DC),
                           w_in[:, 4096:4104].rearrange("(c p) n -> p c n", p=P)).then_inc(ld_small, 16)
            wr3 = wr[:].rearrange("p (c n) -> p c n", c=DC)
            pool.dma_start(wr3[:, :, 0:8], t["w_group_2"][0].rearrange("(c p) n -> p c n", p=P)).then_inc(ld_small, 16)
            pool.dma_start(wr3[:, :, 8:72], t["w_expert_2"][0].rearrange("(c p) n -> p c n", p=P)).then_inc(ld_small, 16)
            pool.dma_start(br[:, 0:8], rows(t["b_group_2"], 0, 8)).then_inc(ld_small, 16)
            pool.dma_start(br[:, 8:72], rows(t["b_expert_2"], 0, 64)).then_inc(ld_small, 16)
            for k, a in enumerate((t["cmp_k_w2_2"], t["cmp_v_w2_2"])):
                pool.dma_start(w2c[:, k * P:(k + 1) * P].rearrange("p (c n) -> p c n", c=2),
                               a[0].rearrange("(c p) n -> p c n", p=P)).then_inc(ld_small, 16)
            pool.wait_ge(mod_raw, 4)
            pool.dma_start(cst[:, 2 * P:], t["constants"][:, 2 * P:]).then_inc(ld_cst, 16)
            pool.dma_start(bg, rows(t["b_gate"], 0, 2 * D)).then_inc(ld_bg, 16)
            pool.dma_start(fg, rows(t["final_g"], 0, D)).then_inc(ld_bg, 16)
            for k, (a, o) in enumerate(((t["b_ada"], 2 * D), (t["b_ada_2"], 2 * D), (t["b_ada_2"], 5 * D))):
                pool.dma_start(grow[:, k * D:(k + 1) * D], rows(a, o, D)).then_inc(ld_grow, 16)
            pool.memset(rbx[:], NEG).then_inc(rb_ok, 1)
            pool.wait_ge(rb_ok, 1)
            pool.dma_start(rbx[0:32, :], t["rel_bias_2"]).then_inc(ld_rows1, 16)
            pool.dma_start(hoT[:], t["buckets"]).then_inc(ld_rows1, 16)

            def below_diagonal(tile):
                return pool.affine_select(out=diag(tile), in_=diag(tile), compare_op=ALU.is_gt, fill=0.0, base=0,
                                          pattern=[[0, 2], [1, P]], channel_multiplier=-1)

            for h in range(H):
                pool.wait_ge(st_L, h + 1)
                below_diagonal(zb(PT, h % 2)).then_inc(st_Lm, 1)
            pool.wait_ge(f_lf, 1)
            pool.wait_ge(ld_cst, 16)
            for h in range(H):
                if h >= 2:
                    pool.wait_ge(fx_z, h - 1)
                u = zb(U, h % 2)
                pool.tensor_scalar(u[:, 0:P], cc(C_LE), fl[:, 48 + h:49 + h], None, ALU.mult)
                pool.tensor_scalar(u[:, P:256], cc(C_ONE), fl[:, 48 + h:49 + h], None, ALU.mult)
                pool.tensor_scalar(u[:, 256:384], cc(C_LE), fl[:, 56 + h:57 + h], None, ALU.mult).then_inc(fx_u, 1)
            pool.wait_ge(misc_free, 17)
            pool.dma_start(bias_dram.rearrange("q h m -> h q m"),
                           bass.AP(tensor=bR.tensor, offset=bR.offset, ap=[bR.ap[0], [0, P], [1, BM]])).then_inc(st_bias, 16)
            pool.wait_ge(st_bias, 16)
            pool.wait_ge(x_ok, 1)
            pool.dma_start(B, bass.AP(tensor=bias_dram.tensor, offset=P - 1, ap=[[H * BM - 1, P], [BM, H], [1, BW]])) \
                .then_inc(ld_bias, 16)
            for a in (X, HTv, Vbd, Pc):
                pool.memset(a, 0.0).then_inc(pad_ok, 1)
            for k in range(3):
                pool.dma_start(cw[:, k * W5:(k + 1) * W5], rows(t["conv_w_2"], k * W5, W5)).then_inc(ld_cw, 16)
            pool.wait_ge(ld_cw, 48)
            for i in range(TI):
                pool.wait_ge(unit_free[i], 23)
                for k in range(3):
                    pool.tensor_tensor(cwp[k][:, i, :], cu3[:, i, :], cw[:, k * W5:(k + 1) * W5],
                                       ALU.mult).then_inc((cv_w, cv_w, cv_w2)[k], 1)


_INS = ["x", "c", "w_ada", "b_ada", "norm_g", "w_in", "b_forget", "w_o_sb", "w_o_fox", "b_gate", "w_out", "final_g",
        "c_2", "w_ada_2", "b_ada_2", "norm1_w_2", "w_in_2", "q_norm_w_2", "k_norm_w_2", "cmp_pos_k_2", "cmp_pos_v_2",
        "cmp_k_w1_2", "cmp_k_w2_2", "cmp_v_w1_2", "cmp_v_w2_2", "conv_w_2", "out_norm_w_2", "w_out_2", "rel_bias_2",
        "norm2_w_2", "w_group_2", "b_group_2", "w_expert_2", "b_expert_2", "w1_2", "w3_2", "w2_2"]


def kernel(**inputs):
    import numpy as _np
    import concourse.bacc as _bacc
    from concourse.bass_utils import run_bass_kernel_spmd as _run

    nc = _bacc.Bacc("TRN2", target_bir_lowering=False, num_devices=1)
    arrays = {n: _np.ascontiguousarray(inputs[n]) for n in _INS}
    arrays["constants"] = constants()
    arrays["buckets"] = bucket_onehot()
    t = {n: nc.dram_tensor(f"in_{n}_dram", a.shape, F32, kind="ExternalInput").ap() for n, a in arrays.items()}
    out = nc.dram_tensor("out_0_dram", (1, T, D), F32, kind="ExternalOutput").ap()
    build(nc, t, out)
    r = _run(nc, [{f"in_{n}_dram": a for n, a in arrays.items()}], core_ids=[0])
    return r.results[0]["out_0_dram"]
```
